# Optimizing a Trainium2 kernel written in Bass

```python
import math
import jax, jax.numpy as jnp
from jax import lax
import numpy as np

D_MODEL = 1024
BATCH = 1
SEQ = 512
DEPTH = 1

CHUNK = 64
MIX_WIDTH = D_MODEL
HGRN_WIDTH = MIX_WIDTH // 2
HGRN_HEAD_DIM = 128
HGRN_HEADS = HGRN_WIDTH // HGRN_HEAD_DIM
S5_WIDTH = MIX_WIDTH - HGRN_WIDTH
S5_GROUP = 16
S5_GROUPS = S5_WIDTH // S5_GROUP
S5_STATE = 64
IN_SPLITS = (HGRN_WIDTH, 2 * HGRN_WIDTH, 3 * HGRN_WIDTH, 4 * HGRN_WIDTH)
IN_COLS = 4 * HGRN_WIDTH + S5_WIDTH
N_MEM = 256
XA_HEADS = 4
XA_HEAD_DIM = D_MODEL // XA_HEADS
XA_SCALE = XA_HEAD_DIM ** -0.5
N_EXPERTS = 32
TOP_K = 4
D_FF = D_MODEL
SWIGLU_LIMIT = 7.0
SWIGLU_ALPHA = 1.702
MOE_BLOCK = 128
DEEPNORM_ALPHA = (2 * DEPTH) ** 0.25
DEEPNORM_BETA = (8 * DEPTH) ** -0.25
LN_EPS = 1e-5
RMS_EPS = 1e-6
S5_DT_MIN = 1e-3
S5_DT_MAX = 1e-1

kernel_name = "hgrn2_s5_xattn_moe_deepnorm_block"

def layer_norm(x, g, b):
    xf = x.astype(jnp.float32)
    mu = jnp.mean(xf, axis=-1, keepdims=True)
    var = jnp.mean(jnp.square(xf - mu), axis=-1, keepdims=True)
    return ((xf - mu) * lax.rsqrt(var + LN_EPS) * g + b).astype(x.dtype)

def hgrn2_mixer(q, f_logit, i_in, g, lb, norm_g):
    B, S, _ = q.shape
    nc = S // CHUNK
    f = lb + (1.0 - lb) * jax.nn.sigmoid(f_logit.astype(jnp.float32))
    log_f = jnp.log(f)
    k = 1.0 - f

    def heads(t):
        return t.reshape(B, nc, CHUNK, HGRN_HEADS, HGRN_HEAD_DIM).transpose(1, 0, 3, 2, 4)

    qc, kc, vc, lc = heads(q.astype(jnp.float32)), heads(k), heads(i_in.astype(jnp.float32)), heads(log_f)
    causal = jnp.tril(jnp.ones((CHUNK, CHUNK), dtype=bool))[:, :, None]

    def step(state, inp):
        qb, kb, vb, lfb = inp
        cum = jnp.cumsum(lfb, axis=2)
        diff = cum[:, :, :, None, :] - cum[:, :, None, :, :]
        decay = jnp.exp(jnp.where(causal, diff, -jnp.inf))
        scores = jnp.einsum('bhtd,bhsd,bhtsd->bhts', qb, kb, decay)
        intra = jnp.einsum('bhts,bhse->bhte', scores, vb)
        inter = jnp.einsum('bhtd,bhde->bhte', qb * jnp.exp(cum), state)
        last = cum[:, :, -1:, :]
        k_dec = kb * jnp.exp(last - cum)
        state = jnp.exp(last[:, :, 0, :])[..., None] * state + jnp.einsum('bhsd,bhse->bhde', k_dec, vb)
        return state, intra + inter

    state0 = jnp.zeros((B, HGRN_HEADS, HGRN_HEAD_DIM, HGRN_HEAD_DIM), jnp.float32)
    _, o = lax.scan(step, state0, (qc, kc, vc, lc))
    o = o.transpose(1, 0, 3, 2, 4).reshape(B, S, HGRN_HEADS, HGRN_HEAD_DIM)
    o = o * lax.rsqrt(jnp.mean(jnp.square(o), axis=-1, keepdims=True) + RMS_EPS) * norm_g
    return o.reshape(B, S, HGRN_WIDTH) * jax.nn.silu(g.astype(jnp.float32))

def s5_mixer(u, lam_re, lam_im, log_dt, b_re, b_im, c_re, c_im, d_skip, w_glu, b_glu):
    B, S, _ = u.shape
    uf = u.astype(jnp.float32)
    lam = lax.complex(lam_re.astype(jnp.float32), lam_im.astype(jnp.float32))
    dt = jnp.exp(log_dt.astype(jnp.float32))
    lam_bar = jnp.exp(lam * dt)
    b_mat = lax.complex(b_re.astype(jnp.float32), b_im.astype(jnp.float32))
    b_bar = ((lam_bar - 1.0) / lam)[..., None] * b_mat
    bu = jnp.einsum('gpn,bsgn->bsgp', b_bar, uf.reshape(B, S, S5_GROUPS, S5_GROUP))
    a = jnp.broadcast_to(lam_bar, bu.shape)

    def combine(left, right):
        a_l, b_l = left
        a_r, b_r = right
        return a_r * a_l, a_r * b_l + b_r

    _, states = lax.associative_scan(combine, (a, bu), axis=1)
    c_mat = lax.complex(c_re.astype(jnp.float32), c_im.astype(jnp.float32))
    y = jnp.einsum('gnp,bsgp->bsgn', c_mat, states).real.reshape(B, S, S5_WIDTH) + d_skip * uf
    y = jax.nn.gelu(y)
    return y * jax.nn.sigmoid(y @ w_glu.astype(jnp.float32) + b_glu)

def cross_attention(h, mem, w_q, w_k, w_v, w_o):
    B, S, D = h.shape
    q = (h @ w_q).reshape(B, S, XA_HEADS, XA_HEAD_DIM)
    k = (mem @ w_k).reshape(B, -1, XA_HEADS, XA_HEAD_DIM)
    v = (mem @ w_v).reshape(B, -1, XA_HEADS, XA_HEAD_DIM)
    s = jnp.einsum('bqhd,bkhd->bhqk', q, k).astype(jnp.float32) * XA_SCALE
    p = jax.nn.softmax(s, axis=-1).astype(v.dtype)
    o = jnp.einsum('bhqk,bkhd->bqhd', p, v).reshape(B, S, D)
    return o @ w_o

def moe_ffn(h, w_router, b_router, w1, b1, w2, b2):
    B, S, D = h.shape
    t = h.reshape(-1, D)
    T = t.shape[0]
    A = T * TOP_K
    logits = (t @ w_router + b_router).astype(jnp.float32)
    top_vals, top_idx = lax.top_k(logits, TOP_K)
    gates = jax.nn.softmax(top_vals, axis=-1)
    flat_e = top_idx.reshape(-1)
    flat_tok = jnp.repeat(jnp.arange(T, dtype=jnp.int32), TOP_K)
    flat_gate = gates.reshape(-1)
    order = jnp.argsort(flat_e)
    sorted_e = flat_e[order]
    counts = jnp.bincount(flat_e, length=N_EXPERTS)
    padded = (counts + MOE_BLOCK - 1) // MOE_BLOCK * MOE_BLOCK
    pad_end = jnp.cumsum(padded)
    pad_start = pad_end - padded
    grp_start = jnp.cumsum(counts) - counts
    dest = pad_start[sorted_e] + jnp.arange(A, dtype=jnp.int32) - grp_start[sorted_e]
    n_blocks = A // MOE_BLOCK + N_EXPERTS
    R = n_blocks * MOE_BLOCK
    row_tok = jnp.zeros((R,), jnp.int32).at[dest].set(flat_tok[order])
    row_gate = jnp.zeros((R,), jnp.float32).at[dest].set(flat_gate[order])
    block_start = jnp.arange(n_blocks, dtype=jnp.int32) * MOE_BLOCK
    block_expert = jnp.minimum(jnp.searchsorted(pad_end, block_start, side='right'), N_EXPERTS - 1)
    xb = t[row_tok].reshape(n_blocks, MOE_BLOCK, D)

    def expert_block(args):
        xe, e = args
        hh = xe @ w1[e] + b1[e]
        x_glu = jnp.minimum(hh[:, :D_FF], SWIGLU_LIMIT)
        x_lin = jnp.clip(hh[:, D_FF:], -SWIGLU_LIMIT, SWIGLU_LIMIT)
        act = x_glu * jax.nn.sigmoid(SWIGLU_ALPHA * x_glu) * (x_lin + 1.0)
        return act @ w2[e] + b2[e]

    yb = lax.map(expert_block, (xb, block_expert))
    y = yb.reshape(R, D).astype(jnp.float32) * row_gate[:, None]
    out = jnp.zeros((T, D), jnp.float32).at[row_tok].add(y)
    return out.reshape(B, S, D).astype(h.dtype)

def setup_inputs(seed: int = 0) -> dict:
    key = jax.random.key(seed)
    ks = jax.random.split(key, 40)
    L = DEPTH
    f32 = jnp.float32

    def nrm(k, shape, std):
        return jax.random.normal(k, shape, f32) * std

    def gain(k, shape):
        return 1.0 + 0.02 * jax.random.normal(k, shape, f32)

    n_idx = jnp.arange(S5_STATE, dtype=f32)
    return {
        "x": nrm(ks[0], (BATCH, SEQ, D_MODEL), 1.0),
        "mem": nrm(ks[1], (BATCH, N_MEM, D_MODEL), 1.0),
        "ln_in_g": gain(ks[2], (D_MODEL,)),
        "ln_in_b": nrm(ks[3], (D_MODEL,), 0.02),
        "w_in": nrm(ks[4], (L, D_MODEL, IN_COLS), D_MODEL ** -0.5),
        "hgrn_lb_logits": nrm(ks[5], (L + 1, HGRN_WIDTH), 0.5),
        "hgrn_norm_g": gain(ks[6], (L, HGRN_HEAD_DIM)),
        "s5_lam_re": -0.5 + 0.01 * jax.random.normal(ks[7], (L, S5_GROUPS, S5_STATE), f32),
        "s5_lam_im": math.pi * n_idx + 0.01 * jax.random.normal(ks[8], (L, S5_GROUPS, S5_STATE), f32),
        "s5_log_dt": jax.random.uniform(ks[9], (L, S5_GROUPS, S5_STATE), f32,
                                        minval=math.log(S5_DT_MIN), maxval=math.log(S5_DT_MAX)),
        "s5_b_re": nrm(ks[10], (L, S5_GROUPS, S5_STATE, S5_GROUP), (2 * S5_GROUP) ** -0.5),
        "s5_b_im": nrm(ks[11], (L, S5_GROUPS, S5_STATE, S5_GROUP), (2 * S5_GROUP) ** -0.5),
        "s5_c_re": nrm(ks[12], (L, S5_GROUPS, S5_GROUP, S5_STATE), (2 * S5_STATE) ** -0.5),
        "s5_c_im": nrm(ks[13], (L, S5_GROUPS, S5_GROUP, S5_STATE), (2 * S5_STATE) ** -0.5),
        "s5_d": nrm(ks[14], (L, S5_WIDTH), 1.0),
        "s5_w_glu": nrm(ks[15], (L, S5_WIDTH, S5_WIDTH), S5_WIDTH ** -0.5),
        "s5_b_glu": nrm(ks[16], (L, S5_WIDTH), 0.02),
        "w_out": nrm(ks[17], (L, MIX_WIDTH, D_MODEL), DEEPNORM_BETA * MIX_WIDTH ** -0.5),
        "ln1_g": gain(ks[18], (L, D_MODEL)),
        "ln1_b": nrm(ks[19], (L, D_MODEL), 0.02),
        "xa_w_q": nrm(ks[20], (L, D_MODEL, D_MODEL), D_MODEL ** -0.5),
        "xa_w_k": nrm(ks[21], (L, D_MODEL, D_MODEL), D_MODEL ** -0.5),
        "xa_w_v": nrm(ks[22], (L, D_MODEL, D_MODEL), D_MODEL ** -0.5),
        "xa_w_o": nrm(ks[23], (L, D_MODEL, D_MODEL), DEEPNORM_BETA * D_MODEL ** -0.5),
        "ln2_g": gain(ks[24], (L, D_MODEL)),
        "ln2_b": nrm(ks[25], (L, D_MODEL), 0.02),
        "router_w": nrm(ks[26], (L, D_MODEL, N_EXPERTS), D_MODEL ** -0.5),
        "router_b": nrm(ks[27], (L, N_EXPERTS), 0.01),
        "exp_w1": nrm(ks[28], (L, N_EXPERTS, D_MODEL, 2 * D_FF), D_MODEL ** -0.5),
        "exp_b1": nrm(ks[29], (L, N_EXPERTS, 2 * D_FF), 0.02),
        "exp_w2": nrm(ks[30], (L, N_EXPERTS, D_FF, D_MODEL), DEEPNORM_BETA * D_FF ** -0.5),
        "exp_b2": nrm(ks[31], (L, N_EXPERTS, D_MODEL), 0.02),
        "ln3_g": gain(ks[32], (L, D_MODEL)),
        "ln3_b": nrm(ks[33], (L, D_MODEL), 0.02),
    }

def reference(x, mem, ln_in_g, ln_in_b, w_in, hgrn_lb_logits, hgrn_norm_g, s5_lam_re, s5_lam_im,
              s5_log_dt, s5_b_re, s5_b_im, s5_c_re, s5_c_im, s5_d, s5_w_glu, s5_b_glu, w_out,
              ln1_g, ln1_b, xa_w_q, xa_w_k, xa_w_v, xa_w_o, ln2_g, ln2_b, router_w, router_b,
              exp_w1, exp_b1, exp_w2, exp_b2, ln3_g, ln3_b):
    h = layer_norm(x, ln_in_g, ln_in_b)
    lb_all = jnp.cumsum(jax.nn.softmax(hgrn_lb_logits.astype(jnp.float32), axis=0), axis=0)
    for l in range(DEPTH):
        proj = h @ w_in[l]
        q, f_logit, i_in, g, u = jnp.split(proj, IN_SPLITS, axis=-1)
        o_a = hgrn2_mixer(q, f_logit, i_in, g, lb_all[l], hgrn_norm_g[l])
        o_b = s5_mixer(u, s5_lam_re[l], s5_lam_im[l], s5_log_dt[l], s5_b_re[l], s5_b_im[l],
                       s5_c_re[l], s5_c_im[l], s5_d[l], s5_w_glu[l], s5_b_glu[l])
        mix = jnp.concatenate([o_a, o_b], axis=-1).astype(h.dtype) @ w_out[l]
        h = layer_norm(DEEPNORM_ALPHA * h + mix, ln1_g[l], ln1_b[l])
        xa = cross_attention(h, mem, xa_w_q[l], xa_w_k[l], xa_w_v[l], xa_w_o[l])
        h = layer_norm(DEEPNORM_ALPHA * h + xa, ln2_g[l], ln2_b[l])
        ff = moe_ffn(h, router_w[l], router_b[l], exp_w1[l], exp_b1[l], exp_w2[l], exp_b2[l])
        h = layer_norm(DEEPNORM_ALPHA * h + ff, ln3_g[l], ln3_b[l])
    return h


_drawn_inputs = setup_inputs


def setup_inputs(seed=0):
    import zlib

    import numpy as np

    out = dict(_drawn_inputs(seed))
    spreads = {}
    factors = {'hgrn_norm_g': 4.945,
     's5_lam_re': 64.0,
     's5_lam_im': 30.152,
     's5_log_dt': 30.712,
     's5_b_re': 36.088,
     's5_b_im': 45.848,
     's5_c_re': 37.072,
     's5_c_im': 42.184,
     's5_b_glu': 28.679,
     'router_b': 3.505,
     'exp_b1': 8.0,
     'exp_b2': 6.453,
     'ln3_g': 7.527,
     'ln3_b': 7.793}
    for name, (base, spread) in spreads.items():
        noise = np.random.default_rng([zlib.crc32(name.encode()), seed]).standard_normal(out[name].shape)
        drawn = base * np.exp(spread * noise) if base else spread * noise
        out[name] = __import__('jax').numpy.asarray(drawn.astype(out[name].dtype))
    for name, factor in factors.items():
        out[name] = (out[name] * factor).astype(out[name].dtype)
    return out
```

```python
import numpy as np
import concourse.bass as bass
from concourse import mybir
from concourse.alu_op_type import AluOpType as ALU

ACT = mybir.ActivationFunctionType
AX = mybir.AxisListType
F32, I32, U32, U8 = mybir.dt.float32, mybir.dt.int32, mybir.dt.uint32, mybir.dt.uint8

P = 128
D = 1024
T = 512
NT = T // P
KD = D // P
HW = 512
NH = 4
G, PST, N = 32, 64, 16
GI = G // 2
L = 8
NC = T // L
M = 256
XD = 256
SCALE = XD ** -0.5
E, FF, TOPK = 32, 1024, 4
CAP = 96
QMAX = (T - 1) // CAP
NBX = E + (T * TOPK) // (CAP + 1) + 1 + 2
LIMIT, SW_ALPHA = 7.0, 1.702
ALPHA = 2.0 ** 0.25
LN_EPS, RMS_EPS = 1e-5, 1e-6
MAGIC = 12582912.0
TWO_PI = 6.283185307179586
TP1 = 6.28125
TP2 = float(np.float32(0.0019353071))
TP3 = float(TWO_PI - TP1 - TP2)
PI_BELOW = 3.1415925

RING, SLOT = 12, 2048
PRE = 8
STREAM = ([("u", i) for i in range(2)] + [("wk", i) for i in range(4)] + [("wv", i) for i in range(4)]
          + [("glu", 0)] + [("main", i) for i in range(8)] + [("wout", i) for i in range(4)]
          + [("wq", i) for i in range(4)] + [("wo", i) for i in range(4)])
SLOT_OF = {w: (n % PRE, n // PRE + 1) for n, w in enumerate(STREAM)}
USES = [sum(n % PRE == s for n in range(len(STREAM))) for s in range(PRE)]
LAST_JOB = {"u": "u3", "wk": "K3", "wv": "V1.1", "glu": "z3", "main": "g3", "wout": "w3.1", "wq": "aq7",
            "wo": "wo3.1"}

LEVELS = [64, 32, 16, 8, 4, 2, 1]


def job_order():
    j = ["par", "cT"]
    j += [f"hT0.{t}.{h}" for t in range(NT) for h in range(2)]
    j += [f"W{r}.{q}" for r in range(2) for q in range(4)]
    j += [f"KK{q}" for q in range(8)]
    j += [f"u{c}" for c in range(4)]
    for c in range(4):
        j += [f"U{c}.{h}" for h in range(2)]
        if c:
            j += [f"ug{c - 1}"]
    j += ["ug3"]
    j += [f"Z{r}.{h}" for r in range(2) for h in range(2)]
    j += [f"mT{m}.{h}" for m in range(2) for h in range(2)]
    j += [f"K{i}" for i in range(4)] + [f"V{m}.{h}" for m in range(2) for h in range(2)]
    for c in range(4):
        j += [f"Y{c}.{h}" for h in range(2)]
        if c:
            j += [f"yT{c - 1}"]
    j += ["yT3"] + [f"z{c}" for c in range(4)]
    j += [f"f{h}" for h in range(4)] + [f"q{h}" for h in range(4)]
    j += [f"i{t}" for t in range(NT)] + [f"g{t}" for t in range(NT)]
    j += [f"s{n}.{t}" for n in range(len(LEVELS) + 1) for t in range(NT)]
    j += [f"kd{t}" for t in range(NT)]
    for t in range(NT):
        j += [f"o{t}"] + ([f"st{t}"] if t < NT - 1 else [])
        if t:
            j += [f"oaT{t - 1}"]
    j += [f"oaT{NT - 1}"]
    for t in range(NT):
        j += [f"w{t}.{h}" for h in range(2)]
        if t:
            j += [f"hT1.{t - 1}.{h}" for h in range(2)]
    j += [f"hT1.{NT - 1}.{h}" for h in range(2)]
    j += [f"aq{c}" for c in range(8)]
    for t in range(NT):
        j += [f"sc{t}.{h}" for h in range(2)]
        if t:
            j += [f"PT{t - 1}.{h}" for h in range(2)]
    j += [f"PT{NT - 1}.{h}" for h in range(2)]
    j += [f"ao{c}" for c in range(8)]
    for t in range(NT):
        j += [f"wo{t}.{h}" for h in range(2)]
        if t:
            j += [f"hT2.{t - 1}.{h}" for h in range(2)]
    j += [f"hT2.{NT - 1}.{h}" for h in range(2)]
    j += ["b1T", "lg", "pos", "GT", "tab"] + [f"gb{t}.{h}" for t in range(NT) for h in range(2)]
    return j


JOBS = {name: (n % 8, n // 8 + 1) for n, name in enumerate(job_order())}


def trunk_layer(nc, A, out):
    x, mem = A["x"][0], A["mem"][0]
    w_in, w_out, w_glu = A["w_in"][0], A["w_out"][0], A["s5_w_glu"][0]
    w1, w2 = A["exp_w1"][0], A["exp_w2"][0]

    h0_rows = nc.dram_tensor("h0_rows", [T, D], F32, kind="Internal").ap()
    h2_rows = nc.dram_tensor("h2_rows", [T, D], F32, kind="Internal").ap()
    y_rows = nc.dram_tensor("y_rows", [T * TOPK, D], F32, kind="Internal").ap()

    def sb(name, shape, dt=F32):
        return nc.alloc_sbuf_tensor(name, shape, dt)

    ring = sb("ring", [P, RING, SLOT])
    hbuf = sb("hbuf", [P, NT, D])
    hT = sb("hT", [P, KD, T])
    lnw = sb("lnw", [P, 2, D])
    kv = sb("kv", [P, 4096])
    ident = sb("ident", [P, P])
    tri = sb("tri", [P, P])
    ones = sb("ones", [P, P])
    masks = sb("masks", [P, len(LEVELS) + 1, P], U8)
    b1T = sb("b1T", [P, E * 16])
    C = sb("arena_c", [P, 11392])
    small = sb("small", [P, 1280])

    def flat(t, a, n):
        return t[:, a:a + n]

    A_ = ring[:, PRE:RING, :].rearrange("p s n -> p (s n)")
    B_ = hbuf[:, :, :].rearrange("p t d -> p (t d)")

    Wst = A_[:, 0:4096].rearrange("p (r g m) -> p r g m", r=2, g=GI)
    Toe = A_[:, 4096:8192].rearrange("p (g m) -> p g m", g=G)
    Vc = flat(C, 0, 4096).rearrange("p (r g k n) -> p r g k n", r=2, g=GI, k=L)
    Qb = flat(C, 4096, 4096).rearrange("p (r g k n) -> p r g k n", r=2, g=GI, k=L)
    Ub = flat(C, 4096, 2048).rearrange("p (b g m) -> p b g m", b=2, g=8)
    Yb = flat(C, 4096, 2048).rearrange("p (b j g n) -> p b j g n", b=2, j=L, g=8)
    X = flat(C, 6144, 2 * GI * (NC + 1)).rearrange("p (r g c) -> p r g c", r=2, g=GI)
    memx = flat(C, 8256, 2048).rearrange("p (m d) -> p m d", m=2)
    s5T = flat(C, 8256, 2048).rearrange("p (c t) -> p c t", c=4)
    KKs = kv[0:N, :].rearrange("p (g m) -> p g m", g=G)
    ug = B_[:, 0:2048].rearrange("p (g c) -> p g c", g=G)
    memT = B_[:, 2048:4096].rearrange("p (k m) -> p k m", k=KD)
    ycm = B_[:, 2048:4096].rearrange("p (c t) -> p c t", c=4)
    ucm = flat(kv, 2048, 2048).rearrange("p (c t) -> p c t", c=4)
    kT = flat(kv, 0, 2048).rearrange("p (c m) -> p c m", c=KD)
    vm = flat(kv, 2048, 2048).rearrange("p (m d) -> p m d", m=2)
    qh, kh, cum, P0 = (A_[:, 2048 * i:2048 * i + 2048] for i in range(4))
    P1, Sc = B_[:, 0:2048], B_[:, 2048:4096].rearrange("p (t h s) -> p t h s", t=NT, h=NH)
    vh = flat(C, 0, 2048).rearrange("p (t e) -> p t e", t=NT)
    gs = flat(C, 2048, 2048).rearrange("p (t e) -> p t e", t=NT)
    qe = flat(C, 4096, 2048)
    oa = flat(C, 6144, 2048).rearrange("p (t e) -> p t e", t=NT)
    st = flat(C, 10368, 512).rearrange("p (h e) -> p h e", h=NH)
    sq = flat(C, 10880, 512)
    kdT = cum.rearrange("p (t h d) -> p t h d", t=NT, h=NH)
    h0b = A_[:, 0:4096].rearrange("p (t d) -> p t d", t=NT)
    qT = flat(C, 0, 4096).rearrange("p (c t) -> p c t", c=KD)
    Pb = flat(C, 4096, 2048).rearrange("p (b h m) -> p b h m", b=2, h=NH)
    PT = flat(C, 6144, 4096).rearrange("p (m h t) -> p m h t", m=2, h=NH)
    Aoh = flat(C, 0, 16 * CAP).rearrange("p (i s) -> p i s", i=16)
    Boh = flat(C, 1536, 16 * NBX).rearrange("p (i s) -> p i s", i=16)
    Xg = C[0:CAP, 0:D]
    xT = flat(C, 1024, KD * CAP).rearrange("p (k s) -> p k s", k=KD)
    glu = flat(C, 1792, 768)
    lin = flat(C, 2560, 768)
    sig = flat(C, 3328, 768)
    act_ = flat(C, 4096, 768).rearrange("p (k s) -> p k s", k=KD)
    ysb = C[0:CAP, 4864:4864 + D]
    rt = C[:, 6912:11392]
    b1raw = flat(kv, 0, 512).rearrange("p (q f) -> p q f", q=4)
    b2sb = kv[0:E, 512:512 + D]
    GTs = kv[0:E, 1792:2304]
    Msk = rt[:, 640:768].rearrange("p (t e) -> p t e", t=NT)
    Gt = rt[:, 768:896].rearrange("p (t e) -> p t e", t=NT)
    rw = flat(kv, 1536, KD * E).rearrange("p (k e) -> p k e", k=KD)

    at = [0]

    def sm(n, parts=P):
        a = at[0]
        at[0] += n
        assert at[0] <= 1280
        return small[0:parts, a:a + n]

    rows = b1T[0:16, 0:128]
    lam_in = b1T[0:GI, 128:512]
    dn = sm(128, G)
    rowsT = sm(96)
    ab = sm(16 * 24).rearrange("p (n g) -> p n g", g=GI)
    lb = sm(8)
    lbx = sm(12)
    rms = sm(32)
    amax, asum = sm(16), sm(16)
    mvs = sm(12)
    topv = sm(32)
    ntop, gsum = sm(4), sm(4)
    ngb = sm(128)
    stat = sm(16)
    mv = sm(8)
    el = sm(16)
    z1 = sm(32).rearrange("p (r g) -> p r g", r=2)
    z2 = sm(32).rearrange("p (r g) -> p r g", r=2)
    z3 = sm(32).rearrange("p (r g) -> p r g", r=2)
    gate = sm(16).rearrange("p (t k) -> p t k", t=NT)
    rbb = sm(32)
    idle = sm(1)
    gix, six = nc.alloc_sbuf_tensor("gix", [CAP, 1], I32), nc.alloc_sbuf_tensor("six", [CAP, 1], I32)
    stab = nc.alloc_sbuf_tensor("stab", [CAP, NBX], I32)
    gtab = nc.alloc_sbuf_tensor("gtab", [CAP, NBX], I32)
    etab = nc.alloc_sbuf_tensor("etab", [1, NBX], I32)
    nbt = nc.alloc_sbuf_tensor("nbt", [1, 2], I32)
    s5p = flat(C, 8256, 2048)
    braw = s5p[:, 0:512].rearrange("p (r g n) -> p r g n", r=2, g=GI)
    bbar = flat(C, 10368, 512).rearrange("p (r g n) -> p r g n", r=2, g=GI)
    craw = s5p[:, 512:1024].rearrange("p (r i a m) -> p r i a m", r=2, i=2, a=2)
    cpar = flat(C, 10880, 512).rearrange("p (r g n) -> p r g n", r=2, g=GI)
    tq = [s5p[:, 1024 + 256 * i:1280 + 256 * i].rearrange("p (g n) -> p g n", g=GI) for i in range(2)]
    tv = [s5p[:, 1536 + 256 * i:1792 + 256 * i].rearrange("p (g n) -> p g n", g=GI) for i in range(2)]

    skip = b1T[0:N, :].rearrange("p (g n) -> p g n", g=G)

    ps = nc.alloc_psum_tensor("ps", [P, 8, 512], F32)
    S = {}

    def sem(name):
        if name not in S:
            S[name] = nc.alloc_semaphore(name)
        return S[name]

    bank_full = [sem(f"bank_full{b}") for b in range(8)]
    bank_free = [sem(f"bank_free{b}") for b in range(8)]
    slot_full = [sem(f"slot_full{s}") for s in range(RING)]
    slot_free = [sem(f"slot_free{s}") for s in range(RING)]

    def bank(job):
        return ps[:, JOBS[job][0], :]

    def wait_full(eng, job):
        b, use = JOBS[job]
        eng.wait_ge(bank_full[b], use)

    def wait_read(eng, job):
        b, use = JOBS[job]
        eng.wait_ge(bank_free[b], use)

    def freed(job, ins):
        ins.then_inc(bank_free[JOBS[job][0]], 1)

    block = nc.Block()
    with block:
        @block.sync
        def _(sp):
            for t in range(NT):
                sp.dma_start(hbuf[:, t, :], x[t * P:(t + 1) * P, :]).then_inc(sem(f"x_in{t}"), 16)
            sp.dma_start(lnw[:, 0, :], A["ln_in_g"].partition_broadcast(P)).then_inc(sem("ln_in"), 16)
            sp.dma_start(lnw[:, 1, :], A["ln_in_b"].partition_broadcast(P)).then_inc(sem("ln_in"), 16)

            def norm_weights(n, g, b):
                sp.wait_ge(sem("normed"), NT * n)
                sp.dma_start(lnw[:, 0, :], A[g][0].partition_broadcast(P)).then_inc(sem("ln_in"), 16)
                sp.dma_start(lnw[:, 1, :], A[b][0].partition_broadcast(P)).then_inc(sem("ln_in"), 16)

            def two_chunks(w, i):
                return w[i * 256:(i + 1) * 256, :].rearrange("(k p) n -> p k n", p=P)

            for n, (w, i) in enumerate(STREAM):
                s, use = SLOT_OF[w, i]
                if use > 1:
                    wait_full(sp, LAST_JOB[STREAM[n - PRE][0]])
                if w == "u":
                    src = w_in[i * 512:(i + 1) * 512, 4 * HW:5 * HW].rearrange("(k p) n -> p k n", p=P)
                elif w == "glu":
                    src = w_glu.rearrange("(k p) n -> p k n", p=P)
                elif w == "main":
                    src = w_in[i * P:(i + 1) * P, 0:4 * HW]
                else:
                    src = two_chunks({"wk": A["xa_w_k"][0], "wv": A["xa_w_v"][0], "wout": w_out,
                                      "wq": A["xa_w_q"][0], "wo": A["xa_w_o"][0]}[w], i)
                dst = ring[:, s, :]
                if w != "main":
                    dst = dst.rearrange("p (k n) -> p k n", n=512 if w in ("u", "glu") else D)
                sp.dma_start(dst, src).then_inc(slot_full[s], 16)
                if (w, i) == ("main", 7):
                    norm_weights(1, "ln1_g", "ln1_b")
                    sp.wait_ge(sem("kdec_ready"), 1)
                    sp.wait_ge(sem("h0_out"), 16 * NT)
                    for t in range(NT):
                        sp.dma_start(h0b[:, t, :], h0_rows[t * P:(t + 1) * P, :]).then_inc(sem("h0_in"), 16)
                if (w, i) == ("wo", 3):
                    norm_weights(2, "ln2_g", "ln2_b")

            def load_w1(k, e_rows):
                sp.dma_start(ring[:, k, :], e_rows).then_inc(slot_full[k], 16)

            def load_w1_dyn(b, e):
                for k in range(8):
                    sp.wait_ge(slot_free[k], b)
                    load_w1(k, w1[bass.ds(e, 1), k * P:(k + 1) * P, :].rearrange("a p n -> p (a n)"))

            def load_w2_dyn(b, e):
                for q in range(4):
                    sp.wait_ge(slot_free[8 + q], b)
                    sp.dma_start(ring[:, 8 + q, :].rearrange("p (k n) -> p k n", k=2),
                                 w2[bass.ds(e, 1), q * 256:(q + 1) * 256, :]
                                 .rearrange("a (k p) n -> p (a k) n", p=P)).then_inc(slot_full[8 + q], 16)

            for k in range(8):
                n = max(n for n in range(len(STREAM)) if n % PRE == k)
                wait_full(sp, LAST_JOB[STREAM[n][0]])
                load_w1(k, w1[0, k * P:(k + 1) * P, :])
            sp.wait_ge(sem("normed"), 2 * NT)
            for q in range(4):
                sp.dma_start(ring[:, 8 + q, :].rearrange("p (k n) -> p k n", k=2),
                             two_chunks(w2[0], q)).then_inc(slot_full[8 + q], 16)
            wait_full(sp, "ao7")
            sp.dma_start(b1raw, A["exp_b1"][0].rearrange("e (f p) -> (e f) p", p=P)
                         .rearrange("(q r) p -> r q p", q=4)).then_inc(sem("late_in"), 16)
            sp.dma_start(b2sb, A["exp_b2"][0]).then_inc(sem("late_in"), 16)
            sp.dma_start(rw, A["router_w"][0].rearrange("(k p) e -> p k e", p=P)).then_inc(sem("late_in"), 16)
            for t in range(NT):
                sp.wait_ge(sem("normed"), 2 * NT + t + 1)
                sp.dma_start(h2_rows[t * P:(t + 1) * P, :], hbuf[:, t, :]).then_inc(sem("h2_out"), 16)
            norm_weights(3, "ln3_g", "ln3_b")
            sp.wait_ge(sem("tables_ready"), 1)
            nb = sp.value_load(nbt[0:1, 0:1], min_val=E, max_val=NBX - 1)
            last = sp.value_load(nbt[0:1, 1:2], min_val=E - 1, max_val=NBX - 2)
            for k in range(8):
                sp.wait_ge(slot_free[k], 1)
                load_w1(k, w1[1, k * P:(k + 1) * P, :])
            with sp.Fori(1, last) as b:
                e = sp.value_load(etab[0:1, bass.ds(b + 1, 1)], min_val=0, max_val=E - 1)
                before = sp.value_load(etab[0:1, bass.ds(b, 1)], min_val=0, max_val=E - 1)
                load_w1_dyn(b + 1, e)
                load_w2_dyn(b, before)
            load_w2_dyn(last, sp.value_load(etab[0:1, bass.ds(last, 1)], min_val=0, max_val=E - 1))
            sp.wait_ge(sem("y_scattered"), nb * 16)
            for t in range(NT):
                sp.dma_start(ring[:, 2 * t:2 * t + 2, :].rearrange("p (a s) n -> p a (s n)", a=1),
                             y_rows[t * 512:(t + 1) * 512, :].rearrange("(p a k) d -> p a (k d)", a=1, k=TOPK))\
                  .then_inc(sem(f"y_in{t}"), 16)
            for t in range(NT):
                sp.wait_ge(sem("normed"), 3 * NT + t + 1)
                sp.dma_start(out[0, t * P:(t + 1) * P, :], hbuf[:, t, :]).then_inc(sem("out_done"), 16)
            sp.wait_ge(sem("out_done"), 16 * NT)

        @block.gpsimd
        def _(pool):
            gp = nc.gpsimd
            step = [0]

            def link(ins):
                step[0] += 1
                ins.then_inc(sem("pool_step"), 1)
                pool.wait_ge(sem("pool_step"), step[0])

            gp.memset(ones[:, :], 1.0)
            gp.memset(tri[:, :], 1.0)
            link(gp.memset(ident[:, :], 1.0))
            gp.affine_select(out=tri[:, :], in_=tri[:, :], compare_op=ALU.is_gt, fill=0.0, base=0,
                             pattern=[[1, P]], channel_multiplier=-1)
            gp.affine_select(out=ident[:, :], in_=ident[:, :], compare_op=ALU.is_equal, fill=0.0, base=0,
                             pattern=[[-1, P]], channel_multiplier=1).then_inc(sem("consts"), 1)
            wait_read(pool, "cT")
            pool.wait_ge(sem("s5_abar"), 1)
            ar = ab[:, 0, :].unsqueeze(2).to_broadcast([P, GI, N])
            ai = ab[:, 1, :].unsqueeze(2).to_broadcast([P, GI, N])

            def times_conj(o0, o1, v0, v1):
                gp.tensor_tensor(tv[0], v0, ar, ALU.mult)
                link(gp.tensor_tensor(tv[1], v1, ai, ALU.mult))
                link(gp.tensor_tensor(o0, tv[0], tv[1], ALU.add))
                gp.tensor_tensor(tv[0], v1, ar, ALU.mult)
                link(gp.tensor_tensor(tv[1], v0, ai, ALU.mult))
                link(gp.tensor_tensor(o1, tv[0], tv[1], ALU.subtract))

            times_conj(Vc[:, 0, :, 0, :], Vc[:, 1, :, 0, :], cpar[:, 0], cpar[:, 1])
            for k in range(1, L):
                times_conj(Vc[:, 0, :, k, :], Vc[:, 1, :, k, :], Vc[:, 0, :, k - 1, :], Vc[:, 1, :, k - 1, :])
            gp.memset(Toe, 0.0).then_inc(sem("s5_v"), 1)
            pool.wait_ge(sem("s5_v"), 1)
            for q in range(8):
                wait_read(pool, f"KK{q}")
            link(gp.tensor_tensor(skip, ident[0:N, 0:N].unsqueeze(1).to_broadcast([N, G, N]),
                                  rowsT[0:N, 64:96].unsqueeze(2).to_broadcast([N, G, N]), ALU.mult))
            link(gp.tensor_tensor(KKs[:, :, 0:N], KKs[:, :, 0:N], skip, ALU.add))
            for i in range(L):
                gp.dma_start(Toe[i * N:(i + 1) * N, :, i * N:P], KKs[:, :, 0:P - i * N])\
                  .then_inc(sem("toe_shifted"), 16)
            pool.wait_ge(sem("toe_shifted"), 16 * L)
            gp.memset(X[:, :, :, 0], 0.0).then_inc(sem("toe_ready"), 1)
            pool.wait_ge(sem("glu_done"), 4)
            gp.memset(Sc, 0.0).then_inc(sem("scores_zero"), 1)
            pool.wait_ge(sem("tables_ready"), 1)
            pool.wait_ge(sem("h2_out"), 16 * NT)
            last = pool.value_load(nbt[0:1, 1:2], min_val=E - 1, max_val=NBX - 2)

            last_token, last_choice = pool.to_reg(T - 1), pool.to_reg(T * TOPK - 1)

            def gather():
                gp.indirect_dma_start(Xg, None, h2_rows, bass.IndirectOffsetOnAxis(ap=gix[:, 0:1].bitcast(U32), axis=0),
                                      bounds_check=last_token, oob_is_err=False).then_inc(sem("x_gathered"), 16)

            def indices(dst, table, b, n):
                gp.tensor_copy(dst[:, :], table[:, bass.ds(b, 1)]).then_inc(sem("pool_step"), 1)
                pool.wait_ge(sem("pool_step"), n)
                gp.tensor_tensor(idle, ones[:, 0:1], ones[:, 0:1], ALU.add)

            def scatter():
                gp.indirect_dma_start(y_rows, bass.IndirectOffsetOnAxis(ap=six[:, 0:1].bitcast(U32), axis=0), ysb, None,
                                      bounds_check=last_choice, oob_is_err=False).then_inc(sem("y_scattered"), 16)

            link(gp.memset(Xg, 0.0))
            link(gp.tensor_copy(gix[:, :], gtab[:, 0:1]))
            gather()
            pool.wait_ge(sem("x_gathered"), 16)
            pool.wait_ge(sem("xt_full"), 1)
            link(gp.tensor_copy(gix[:, :], gtab[:, 1:2]))
            gather()
            base = step[0]
            with pool.Fori(0, last) as b:
                pool.wait_ge(sem("x_gathered"), 16 * b + 32)
                pool.wait_ge(sem("xt_full"), b + 2)
                indices(gix, gtab, b + 2, 2 * b + (base + 1))
                gather()
                pool.wait_ge(sem("y_copied"), b + 1)
                pool.wait_ge(sem("y_scattered"), 16 * b)
                indices(six, stab, b, 2 * b + (base + 2))
                scatter()
            pool.wait_ge(sem("y_copied"), last + 1)
            pool.wait_ge(sem("y_scattered"), 16 * last)
            indices(six, stab, last, 2 * last + (base + 1))
            scatter()

        @block.scalar
        def _(act):
            sc = nc.scalar
            step = [0]

            def link(ins):
                step[0] += 1
                ins.then_inc(sem("act_step"), 1)
                act.wait_ge(sem("act_step"), step[0])

            def ld(o, i, name="params"):
                act.dma_start(o, i).then_inc(sem(name), 16)

            ld(rows[0:8, :], A["hgrn_lb_logits"].rearrange("r (h d) -> (r h) d", d=P))
            ld(rows[8:12, :], A["s5_b_glu"].rearrange("a (c d) -> (a c) d", d=P))
            ld(rows[12:16, :], A["s5_b_glu"].rearrange("a (c d) -> (a c) d", d=P))
            for i, nm in enumerate(("s5_lam_re", "s5_lam_im", "s5_log_dt")):
                ld(lam_in[:, i * P:(i + 1) * P].rearrange("g (a p) -> g a p", a=2),
                   A[nm][0].rearrange("(a g) p -> g a p", a=2))
            ld(dn.rearrange("g (i n) -> g i n", n=N),
               A["s5_d"][0].rearrange("(g n) -> g n", n=N).unsqueeze(1).to_broadcast([G, L, N]))
            for r, nm in enumerate(("s5_b_re", "s5_b_im")):
                for a in range(2):
                    ld(braw[a * PST:(a + 1) * PST, r], A[nm][0, a * GI:(a + 1) * GI].rearrange("g p n -> p g n"))
            for r, nm in enumerate(("s5_c_re", "s5_c_im")):
                for i in range(2):
                    ld(craw[:, r, i], A[nm][0].rearrange("(a i g) n p -> i (g n) a p", a=2, i=2)[i])
            ld(ngb, A["hgrn_norm_g"][0].partition_broadcast(P))
            ld(rbb, A["router_b"][0].partition_broadcast(P))
            def copy(dst, src):
                return sc.activation(dst, src, ACT.Copy)

            def norm_roots(n):
                for t in range(NT):
                    act.wait_ge(sem("var_ready"), NT * n + t + 1)
                    sc.activation(stat[:, t:t + 1], stat[:, t:t + 1], ACT.Sqrt).then_inc(sem("std_ready"), 1)

            act.wait_ge(sem("var_ready"), 1)
            sc.activation(stat[:, 0:1], stat[:, 0:1], ACT.Sqrt).then_inc(sem("std_ready"), 1)
            for t in range(NT):
                if t < NT - 1:
                    act.wait_ge(sem("var_ready"), t + 2)
                    sc.activation(stat[:, t + 1:t + 2], stat[:, t + 1:t + 2], ACT.Sqrt).then_inc(sem("std_ready"), 1)
                for h in range(2):
                    j = f"hT0.{t}.{h}"
                    wait_full(act, j)
                    freed(j, copy(hT[:, 4 * h:4 * h + 4, t * P:(t + 1) * P],
                                  bank(j).rearrange("p (k n) -> p k n", k=4)))
            wait_read(act, "par")
            sc.activation(ab[:, 2, :], rowsT[:, 48:64], ACT.Exp).then_inc(sem("dt"), 1)
            act.wait_ge(sem("angles"), 1)
            sc.activation(ab[:, 3, :], ab[:, 3, :], ACT.Exp)
            sc.activation(ab[:, 5, :], ab[:, 5, :], ACT.Sin)
            sc.activation(ab[:, 6, :], ab[:, 6, :], ACT.Sin).then_inc(sem("sines"), 1)
            act.wait_ge(sem("lb_logits"), 1)
            sc.activation(lbx[:, 0:8], lbx[:, 0:8], ACT.Exp).then_inc(sem("lb_exp"), 1)

            for t in range(NT):
                act.wait_ge(sem("normed"), t + 1)
                act.dma_start(h0_rows[t * P:(t + 1) * P, :], hbuf[:, t, :]).then_inc(sem("h0_out"), 16)
            for r in range(2):
                for q in range(4):
                    j = f"W{r}.{q}"
                    wait_full(act, j)
                    freed(j, copy(Wst[:, r, 4 * q:4 * q + 4, :], bank(j).rearrange("p (g m) -> p g m", g=4)))
            for q in range(8):
                j = f"KK{q}"
                wait_full(act, j)
                freed(j, copy(KKs[:, 4 * q:4 * q + 4, :], bank(j)[0:N, :].rearrange("p (g m) -> p g m", g=4)))
            act.wait_ge(sem("s5_v"), 1)
            act.wait_ge(sem("q_ready"), 1)
            act.dma_start(memx, mem.rearrange("(m p) d -> p m d", p=P)).then_inc(sem("mem_in"), 16)
            act.wait_ge(sem("toe_shifted"), 16 * L)
            for c in range(4):
                j = f"u{c}"
                wait_full(act, j)
                freed(j, copy(ucm[:, c, :], bank(j)))
            act.wait_ge(sem("h0_out"), 16 * NT)
            for c in range(5):
                if c < 4:
                    for h in range(2):
                        j = f"U{c}.{h}"
                        wait_full(act, j)
                        dst = Ub[0:NC, c % 2].rearrange("p g (j n) -> p j g n", j=L)[:, 4 * h:4 * h + 4]
                        freed(j, copy(dst, bank(j)[0:NC, :].rearrange("p (j g n) -> p j g n", j=4, g=8)))
                if c:
                    j = f"ug{c - 1}"
                    wait_full(act, j)
                    freed(j, copy(ug[:, 8 * (c - 1):8 * c, :], bank(j).rearrange("p (g c) -> p g c", g=8)))
            act.wait_ge(sem("toe_ready"), 1)
            for r in range(2):
                for h in range(2):
                    j = f"Z{r}.{h}"
                    wait_full(act, j)
                    ins = copy(X[:, r, 8 * h:8 * h + 8, 1:NC + 1], bank(j).rearrange("p (g c) -> p g c", g=8))
                    freed(j, ins)
            for m in range(2):
                for h in range(2):
                    j = f"mT{m}.{h}"
                    wait_full(act, j)
                    freed(j, copy(memT[:, 4 * h:4 * h + 4, m * P:(m + 1) * P],
                                  bank(j).rearrange("p (k n) -> p k n", k=4)))
            for i in range(4):
                j = f"K{i}"
                wait_full(act, j)
                freed(j, copy(kT[:, 2 * i:2 * i + 2, :], bank(j).rearrange("p (k n) -> p k n", k=2)))
            for m in range(2):
                for h in range(2):
                    j = f"V{m}.{h}"
                    wait_full(act, j)
                    freed(j, copy(vm[:, m, 512 * h:512 * h + 512], bank(j)))
            for c in range(5):
                if c < 4:
                    for h in range(2):
                        j = f"Y{c}.{h}"
                        wait_full(act, j)
                        freed(j, copy(Yb[0:NC, c % 2, :, 4 * h:4 * h + 4, :].rearrange("p j g n -> p g j n"),
                                      bank(j)[0:NC, :].rearrange("p (g j n) -> p g j n", g=4, j=L)))
                if c:
                    j = f"yT{c - 1}"
                    wait_full(act, j)
                    freed(j, sc.activation(ycm[:, c - 1, :].rearrange("p (c j) -> p j c", j=L),
                                           bank(j).rearrange("p (j c) -> p j c", j=L), ACT.Gelu_apprx_tanh))
            for c in range(4):
                j = f"z{c}"
                wait_full(act, j)
                ins = sc.activation(s5T[:, c, :], bank(j), ACT.Sigmoid, bias=rowsT[:, 8 + c:9 + c])
                freed(j, ins)
            for h in range(4):
                j = f"f{h}"
                wait_full(act, j)
                freed(j, sc.activation(kh[:, h * T:(h + 1) * T], bank(j), ACT.Sigmoid))
            for h in range(4):
                j = f"q{h}"
                wait_full(act, j)
                freed(j, copy(qh[:, h * T:(h + 1) * T], bank(j)))
            act.wait_ge(sem("f_ready"), 4)
            sc.activation(P1, cum, ACT.Ln).then_inc(sem("logf_ready"), 1)
            for t in range(NT):
                j = f"i{t}"
                wait_full(act, j)
                freed(j, copy(vh[:, t, :], bank(j)))
            for t in range(NT):
                j = f"g{t}"
                wait_full(act, j)
                sc.activation(gs[:, t, :], bank(j), ACT.Sigmoid).then_inc(sem("sig_g"), 1)
            for n in range(len(LEVELS)):
                act.wait_ge(sem("diff_ready"), n + 1)
                buf = P0 if n % 2 == 0 else P1
                sc.activation(buf, buf, ACT.Exp).then_inc(sem("decay_ready"), 1)
            act.wait_ge(sem("cum_ready"), 1)
            sc.activation(qe, cum, ACT.Exp).then_inc(sem("qe_exp"), 1)
            sc.activation(el, cum.rearrange("p (b s) -> p b s", s=P)[:, :, P - 1], ACT.Exp).then_inc(sem("el_ready"), 1)
            act.wait_ge(sem("diff_ready"), len(LEVELS) + 1)
            sc.activation(P1, P1, ACT.Exp).then_inc(sem("decay_ready"), 1)
            for t in range(NT):
                j = f"kd{t}"
                wait_full(act, j)
                freed(j, copy(kdT[:, t], bank(j).rearrange("p (h d) -> p h d", h=NH)))
            for t in range(NT):
                j = f"o{t}"
                wait_full(act, j)
                for h in range(NH):
                    ins = sc.activation(sq[:, h * P:(h + 1) * P], bank(j)[:, h * P:(h + 1) * P], ACT.Square,
                                        accum_out=rms[:, 4 * t + h:4 * t + h + 1])
                ins.then_inc(sem("ms_ready"), 1)
                act.wait_ge(sem("ms_eps"), t + 1)
                sc.activation(rms[:, 16 + 4 * t:20 + 4 * t], rms[:, 16 + 4 * t:20 + 4 * t], ACT.Sqrt)\
                  .then_inc(sem("rms_ready"), 1)
                if t:
                    j = f"oaT{t - 1}"
                    wait_full(act, j)
                    freed(j, copy(hT[:, 0:4, (t - 1) * P:t * P], bank(j).rearrange("p (k n) -> p k n", k=4)))
            j = f"oaT{NT - 1}"
            wait_full(act, j)
            freed(j, copy(hT[:, 0:4, (NT - 1) * P:], bank(j).rearrange("p (k n) -> p k n", k=4)))

            def roots_and_transposes(n):
                for t in range(NT + 1):
                    if t < NT:
                        act.wait_ge(sem("var_ready"), NT * n + t + 1)
                        sc.activation(stat[:, t:t + 1], stat[:, t:t + 1], ACT.Sqrt).then_inc(sem("std_ready"), 1)
                    if t:
                        for h in range(2):
                            j = f"hT{n}.{t - 1}.{h}"
                            wait_full(act, j)
                            freed(j, copy(hT[:, 4 * h:4 * h + 4, (t - 1) * P:t * P],
                                          bank(j).rearrange("p (k n) -> p k n", k=4)))

            roots_and_transposes(1)
            for c in range(8):
                j = f"aq{c}"
                wait_full(act, j)
                freed(j, copy(qT[:, c, :], bank(j)))
            for t in range(NT + 1):
                if t < NT:
                    for h in range(2):
                        j = f"sc{t}.{h}"
                        act.wait_ge(sem("max_ready"), 2 * t + h + 1)
                        if t >= 2 and h == 0:
                            wait_full(act, f"PT{t - 2}.1")
                        for i in range(2):
                            hh = 2 * h + i
                            ins = sc.activation(Pb[:, t % 2, hh, :], bank(j)[:, M * i:M * i + M], ACT.Exp, scale=SCALE,
                                                bias=amax[:, 4 * t + hh:4 * t + hh + 1],
                                                accum_out=asum[:, 4 * t + hh:4 * t + hh + 1])
                        ins.then_inc(sem("exp_ready"), 1)
                if t:
                    for m in range(2):
                        j = f"PT{t - 1}.{m}"
                        wait_full(act, j)
                        freed(j, copy(PT[:, m, :, (t - 1) * P:t * P], bank(j).rearrange("p (h n) -> p h n", h=NH)))
            for c in range(8):
                j = f"ao{c}"
                wait_full(act, j)
                freed(j, copy(hT[:, c, :], bank(j)))
            roots_and_transposes(2)
            wait_full(act, "b1T")
            freed("b1T", copy(b1T[:, :], bank("b1T")))
            act.wait_ge(sem("top_ready"), 1)
            ins = None
            for t in range(NT):
                ins = sc.activation(gate[:, t, :], topv[:, 8 * t:8 * t + 4], ACT.Exp,
                                    bias=ntop[:, t:t + 1], accum_out=gsum[:, t:t + 1])
            ins.then_inc(sem("gate_exp"), 1)
            act.wait_ge(sem("tables_ready"), 1)
            last = act.value_load(nbt[0:1, 1:2], min_val=E - 1, max_val=NBX - 2)

            def transposed_rows():
                sc.activation(xT[:, 0:4, :], ps[:, 6, 0:4 * CAP].rearrange("p (k s) -> p k s", k=4), ACT.Copy)
                sc.activation(xT[:, 4:8, :], ps[:, 7, 0:4 * CAP].rearrange("p (k s) -> p k s", k=4), ACT.Copy)\
                  .then_inc(sem("xt_copied"), 1)

            def sigmoids():
                sc.activation(sig, glu, ACT.Sigmoid, scale=SW_ALPHA).then_inc(sem("sig_ready"), 1)

            def result_rows():
                sc.activation(ysb.rearrange("p (h n) -> p h n", h=2), ps[0:CAP, 4:6, :], ACT.Copy)\
                  .then_inc(sem("y_copied"), 1)

            act.wait_ge(sem("xt_full"), 1)
            transposed_rows()
            act.wait_ge(sem("xt_full"), 2)
            transposed_rows()
            act.wait_ge(sem("glu_ready"), 1)
            sigmoids()
            with act.Fori(0, last) as b:
                act.wait_ge(sem("xt_full"), b + 3)
                transposed_rows()
                act.wait_ge(sem("glu_ready"), b + 2)
                act.wait_ge(sem("act_ready"), b + 1)
                sigmoids()
                act.wait_ge(slot_free[11], b + 1)
                act.wait_ge(sem("y_scattered"), 16 * b)
                result_rows()
            act.wait_ge(slot_free[11], last + 1)
            act.wait_ge(sem("y_scattered"), 16 * last)
            result_rows()
            norm_roots(3)

        @block.vector
        def _(v):
            ve = nc.vector
            step, steps = [0], ["dve_step"]

            def link(ins):
                step[0] += 1
                ins.then_inc(sem(steps[0]), 1)
                v.wait_ge(sem(steps[0]), step[0])

            v.wait_ge(sem("consts"), 1)
            col = rt[:, 0:P]
            row = rt[:, P:2 * P]
            t0, t1, t2 = rt[:, 256:384], rt[:, 384:512], rt[:, 512:640]
            link(ve.tensor_tensor_scan(col, ones[:, :], ones[:, :], -1.0, ALU.mult, ALU.add))
            link(ve.tensor_tensor(t0, col, ident[:, :], ALU.mult))
            link(ve.tensor_reduce(row[:, 0:1], t0, AX.X, ALU.add))
            link(ve.tensor_copy(masks[:, 0, :], ident[:, :]))
            coli, rowi = rt[:, 640:768].bitcast(I32), rt[:, 768:769].bitcast(I32)
            rowb = rt[:, 896:1024].bitcast(I32)
            xr = rt[:, 1024:1152].bitcast(I32)
            link(ve.tensor_copy(coli, col))
            link(ve.tensor_copy(rowb, row[:, 0:1].to_broadcast([P, P])))
            link(ve.tensor_tensor(xr, coli, rowb, ALU.bitwise_xor))
            link(ve.tensor_copy(t0, xr))
            for n, hs in enumerate(LEVELS):
                link(ve.tensor_scalar(t1, t0, float(hs), None, ALU.is_ge))
                link(ve.tensor_scalar(t2, t0, float(2 * hs), None, ALU.is_lt))
                link(ve.tensor_tensor(t1, t1, t2, ALU.mult))
                link(ve.tensor_tensor(masks[:, n + 1, :], t1, tri[:, :], ALU.mult))

            def stats(n, t):
                link(ve.bn_stats(mvs[:, 0:6], hbuf[:, t, 0:512]))
                link(ve.bn_stats(mvs[:, 6:12], hbuf[:, t, 512:1024]))
                link(ve.bn_aggr(mv[:, 0:2], mvs))
                ve.tensor_scalar(stat[:, t:t + 1], mv[:, 1:2], LN_EPS, None, ALU.add).then_inc(sem("var_ready"), 1)
                v.wait_ge(sem("var_ready"), NT * n + t + 1)

            def normalise(n, t):
                v.wait_ge(sem("std_ready"), NT * n + t + 1)
                link(ve.reciprocal(mv[:, 2:3], stat[:, t:t + 1]))
                link(ve.scalar_tensor_tensor(out=hbuf[:, t, :], in0=hbuf[:, t, :], scalar=mv[:, 0:1],
                                             in1=lnw[:, 0, :], op0=ALU.subtract, op1=ALU.mult))
                ve.scalar_tensor_tensor(out=hbuf[:, t, :], in0=hbuf[:, t, :], scalar=mv[:, 2:3],
                                        in1=lnw[:, 1, :], op0=ALU.mult, op1=ALU.add).then_inc(sem("normed"), 1)
                v.wait_ge(sem("normed"), NT * n + t + 1)

            wait_full(v, "par")
            freed("par", ve.tensor_copy(rowsT, bank("par")[:, 0:96]))
            wait_read(v, "par")
            wait_full(v, "cT")
            ct = bank("cT").rearrange("p (r i m) -> p r i m", r=2, i=2)
            ve.tensor_copy(cpar[:, 0].rearrange("p (i g) n -> p i (g n)", i=2), ct[:, 0])
            freed("cT", ve.tensor_scalar(cpar[:, 1].rearrange("p (i g) n -> p i (g n)", i=2), ct[:, 1], -1.0, None,
                                         ALU.mult))
            v.wait_ge(sem("ln_in"), 32)
            for t in range(NT):
                v.wait_ge(sem(f"x_in{t}"), 16)
                stats(0, t)
                normalise(0, t)

            lamr, lami = rowsT[:, 16:32], rowsT[:, 32:48]
            v.wait_ge(sem("dt"), 1)
            link(ve.tensor_tensor(ab[:, 3, :], lamr, ab[:, 2, :], ALU.mult))
            link(ve.tensor_tensor(ab[:, 4, :], lami, ab[:, 2, :], ALU.mult))
            link(ve.tensor_scalar(ab[:, 7, :], ab[:, 4, :], 1.0 / TWO_PI, None, ALU.mult))
            link(ve.tensor_scalar(ab[:, 7, :], ab[:, 7, :], MAGIC, None, ALU.add))
            link(ve.tensor_scalar(ab[:, 7, :], ab[:, 7, :], MAGIC, None, ALU.subtract))
            for part in (TP1, TP2, TP3):
                link(ve.scalar_tensor_tensor(out=ab[:, 4, :], in0=ab[:, 7, :], scalar=-part, in1=ab[:, 4, :],
                                             op0=ALU.mult, op1=ALU.add))
            link(ve.tensor_scalar(ab[:, 5, :], ab[:, 4, :], -PI_BELOW, PI_BELOW, ALU.max, ALU.min))
            ve.tensor_scalar(ab[:, 6, :], ab[:, 5, :], 0.5, None, ALU.mult).then_inc(sem("angles"), 1)
            v.wait_ge(sem("sines"), 1)
            link(ve.tensor_tensor(ab[:, 6, :], ab[:, 6, :], ab[:, 6, :], ALU.mult))
            link(ve.tensor_scalar(ab[:, 6, :], ab[:, 6, :], -2.0, 1.0, ALU.mult, ALU.add))
            link(ve.tensor_tensor(ab[:, 0, :], ab[:, 3, :], ab[:, 6, :], ALU.mult))
            ve.tensor_tensor(ab[:, 1, :], ab[:, 3, :], ab[:, 5, :], ALU.mult).then_inc(sem("s5_abar"), 1)
            v.wait_ge(sem("s5_abar"), 1)
            nr, cr, ci, den, w = (ab[:, 8 + i, :] for i in range(5))
            link(ve.tensor_scalar(nr, ab[:, 0, :], -1.0, None, ALU.add))
            link(ve.tensor_tensor(den, lamr, lamr, ALU.mult))
            link(ve.tensor_tensor(w, lami, lami, ALU.mult))
            link(ve.tensor_tensor(den, den, w, ALU.add))
            link(ve.reciprocal(den, den))
            link(ve.tensor_tensor(cr, nr, lamr, ALU.mult))
            link(ve.tensor_tensor(w, ab[:, 1, :], lami, ALU.mult))
            link(ve.tensor_tensor(cr, cr, w, ALU.add))
            link(ve.tensor_tensor(cr, cr, den, ALU.mult))
            link(ve.tensor_tensor(ci, ab[:, 1, :], lamr, ALU.mult))
            link(ve.tensor_tensor(w, nr, lami, ALU.mult))
            link(ve.tensor_tensor(ci, ci, w, ALU.subtract))
            link(ve.tensor_tensor(ci, ci, den, ALU.mult))

            def times(o0, o1, a0, a1, b0, b1, t, done=None):
                ve.tensor_tensor(t[0], b0, a0, ALU.mult)
                link(ve.tensor_tensor(t[1], b1, a1, ALU.mult))
                link(ve.tensor_tensor(o0, t[0], t[1], ALU.subtract))
                ve.tensor_tensor(t[0], b1, a0, ALU.mult)
                link(ve.tensor_tensor(t[1], b0, a1, ALU.mult))
                ins = ve.tensor_tensor(o1, t[0], t[1], ALU.add)
                if done:
                    ins.then_inc(sem(done), 1)
                    v.wait_ge(sem(done), 1)
                else:
                    link(ins)

            def wide(a):
                return a.unsqueeze(2).to_broadcast([P, GI, N])

            times(bbar[:, 0], bbar[:, 1], wide(cr), wide(ci), braw[:, 0], braw[:, 1], tq)
            ve.tensor_copy(Qb[:, 0, :, L - 1, :], bbar[:, 0])
            link(ve.tensor_copy(Qb[:, 1, :, L - 1, :], bbar[:, 1]))
            for j in range(L - 2, -1, -1):
                times(Qb[:, 0, :, j, :], Qb[:, 1, :, j, :], wide(ab[:, 0, :]), wide(ab[:, 1, :]),
                      Qb[:, 0, :, j + 1, :], Qb[:, 1, :, j + 1, :], tq, None if j else "q_ready")
            pw = [ab[:, 13 + i, :] for i in range(6)]
            tt_ = [ab[:, 19 + i, :] for i in range(2)]
            times(pw[0], pw[1], ab[:, 0, :], ab[:, 1, :], ab[:, 0, :], ab[:, 1, :], tt_)
            times(pw[2], pw[3], pw[0], pw[1], pw[0], pw[1], tt_)
            times(pw[4], pw[5], pw[2], pw[3], pw[2], pw[3], tt_)
            a8r, a8i, a8n = pw[4], pw[5], ab[:, 21, :]
            link(ve.tensor_scalar(a8n, a8i, -1.0, None, ALU.mult))
            lg = rowsT[:, 0:8]
            link(ve.tensor_tensor(lbx[:, 8:12], lg[:, 0:4], lg[:, 4:8], ALU.max))
            ve.tensor_tensor(lbx[:, 0:8].rearrange("p (r h) -> p r h", r=2), lg.rearrange("p (r h) -> p r h", r=2),
                             lbx[:, 8:12].unsqueeze(1).to_broadcast([P, 2, NH]), ALU.subtract)\
              .then_inc(sem("lb_logits"), 1)
            v.wait_ge(sem("lb_exp"), 1)
            link(ve.tensor_tensor(lbx[:, 8:12], lbx[:, 0:4], lbx[:, 4:8], ALU.add))
            link(ve.reciprocal(lbx[:, 8:12], lbx[:, 8:12]))
            link(ve.tensor_tensor(lb[:, 0:4], lbx[:, 0:4], lbx[:, 8:12], ALU.mult))
            link(ve.tensor_scalar(lb[:, 4:8], lb[:, 0:4], -1.0, 1.0, ALU.mult, ALU.add))

            for r in range(2):
                for h in range(2):
                    wait_read(v, f"Z{r}.{h}")
            a8w = a8r.unsqueeze(1).to_broadcast([P, 2, GI])
            base = step[0]
            with v.Fori(0, NC) as c:
                old, new = X[:, :, :, bass.ds(c, 1)], X[:, :, :, bass.ds(c + 1, 1)]
                ve.tensor_tensor(z1, old.rearrange("p r g o -> p r (g o)"), a8w, ALU.mult)
                ve.tensor_tensor(z2[:, 0, :], old[:, 1].rearrange("p g o -> p (g o)"), a8n, ALU.mult)
                ve.tensor_tensor(z2[:, 1, :], old[:, 0].rearrange("p g o -> p (g o)"), a8i, ALU.mult)\
                  .then_inc(sem("dve_step"), 1)
                v.wait_ge(sem("dve_step"), 3 * c + (base + 1))
                ve.tensor_tensor(z3, z1, new.rearrange("p r g o -> p r (g o)"), ALU.add).then_inc(sem("dve_step"), 1)
                v.wait_ge(sem("dve_step"), 3 * c + (base + 2))
                ve.tensor_tensor(new.rearrange("p r g o -> p r (g o)"), z3, z2, ALU.add).then_inc(sem("dve_step"), 1)
                v.wait_ge(sem("dve_step"), 3 * c + (base + 3))
            step[0] = base + 3 * NC
            ve.memset(z1, 0.0).then_inc(sem("x_ready"), 1)
            for c in range(4):
                wait_read(v, f"z{c}")
                ve.tensor_tensor(s5T[:, c, :], s5T[:, c, :], ycm[:, c, :], ALU.mult).then_inc(sem("glu_done"), 1)

            for h in range(4):
                wait_read(v, f"f{h}")
                s = slice(h * T, (h + 1) * T)
                link(ve.tensor_scalar(cum[:, s], kh[:, s], lb[:, 4 + h:5 + h], lb[:, h:h + 1], ALU.mult, ALU.add))
                ve.tensor_scalar(kh[:, s], cum[:, s], -1.0, 1.0, ALU.mult, ALU.add).then_inc(sem("f_ready"), 1)
            v.wait_ge(sem("logf_ready"), 1)
            for i in range(16):
                s = slice(i * P, (i + 1) * P)
                ins = ve.tensor_tensor_scan(cum[:, s], ones[:, :], P1[:, s], 0.0, ALU.mult, ALU.add)
            ins.then_inc(sem("cum_ready"), 1)
            v.wait_ge(sem("cum_ready"), 1)
            def gates(t):
                v.wait_ge(sem("sig_g"), t + 1)
                j = f"g{t}"
                wait_full(v, j)
                link(ve.tensor_tensor(gs[:, t, :], gs[:, t, :], bank(j), ALU.mult))
                freed(j, ve.tensor_tensor(gs[:, t, :].rearrange("p (h e) -> p h e", h=NH),
                                          gs[:, t, :].rearrange("p (h e) -> p h e", h=NH),
                                          ngb.unsqueeze(1).to_broadcast([P, NH, P]), ALU.mult))

            def halves(a, hs):
                return a.rearrange("p (b w s) -> p b w s", w=2, s=hs)

            def diff(n):
                hs = LEVELS[n]
                buf = P0 if n % 2 == 0 else P1
                if n >= 2:
                    for t in range(NT):
                        wait_full(v, f"s{n - 1}.{t}")
                c4, d4 = halves(cum, hs), halves(buf, hs)
                ref = c4[:, :, 0, hs - 1:hs].to_broadcast([P, 2048 // (2 * hs), hs])
                ve.tensor_tensor(d4[:, :, 1, :], c4[:, :, 1, :], ref, ALU.subtract)
                ve.tensor_tensor(d4[:, :, 0, :], ref, c4[:, :, 0, :], ALU.subtract).then_inc(sem("diff_ready"), 1)

            def weigh(n):
                hs = LEVELS[n]
                buf = P0 if n % 2 == 0 else P1
                v.wait_ge(sem("decay_ready"), n + 1)
                d4, q4, k4 = halves(buf, hs), halves(qh, hs), halves(kh, hs)
                ve.tensor_tensor(d4[:, :, 1, :], d4[:, :, 1, :], q4[:, :, 1, :], ALU.mult)
                ve.tensor_tensor(d4[:, :, 0, :], d4[:, :, 0, :], k4[:, :, 0, :], ALU.mult).then_inc(sem("pair_ready"), 1)

            def place(n):
                for t in range(NT):
                    j = f"s{n}.{t}"
                    wait_full(v, j)
                    if n:
                        wait_read(v, f"s{n - 1}.{t}")
                    freed(j, ve.copy_predicated(Sc[:, t], masks[:, n, :].unsqueeze(1).to_broadcast([P, NH, P]),
                                                bank(j).rearrange("p (h s) -> p h s", h=NH)))

            for j in ("q0", "q1", "q2", "q3"):
                wait_read(v, j)
            diff(0)
            diff(1)
            for t in range(NT):
                gates(t)
            v.wait_ge(sem("scores_zero"), 1)
            weigh(0)
            place(0)
            for n in range(1, len(LEVELS)):
                weigh(n)
                place(n)
                if n + 1 < len(LEVELS):
                    diff(n + 1)
            v.wait_ge(sem("qe_exp"), 1)
            ve.tensor_tensor(qe, qe, qh, ALU.mult).then_inc(sem("qe_ready"), 1)
            for t in range(NT):
                wait_full(v, f"s{len(LEVELS) - 1}.{t}")
            c3 = cum.rearrange("p (b s) -> p b s", s=P)
            ve.tensor_tensor(P1.rearrange("p (b s) -> p b s", s=P), c3[:, :, P - 1:P].to_broadcast([P, 16, P]), c3,
                             ALU.subtract).then_inc(sem("diff_ready"), 1)
            v.wait_ge(sem("decay_ready"), len(LEVELS) + 1)
            ve.tensor_tensor(P1, P1, kh, ALU.mult).then_inc(sem("kdec_ready"), 1)
            place(len(LEVELS))
            v.wait_ge(sem("el_ready"), 1)
            for t in range(NT):
                if t < NT - 1:
                    j = f"st{t}"
                    wait_full(v, j)
                    for h in range(NH):
                        if t == 0:
                            ins = ve.tensor_copy(st[:, h, :], bank(j)[:, h * P:(h + 1) * P])
                        else:
                            ins = ve.scalar_tensor_tensor(out=st[:, h, :], in0=st[:, h, :],
                                                          scalar=el[:, 4 * h + t:4 * h + t + 1],
                                                          in1=bank(j)[:, h * P:(h + 1) * P], op0=ALU.mult, op1=ALU.add)
                    freed(j, ins)
                v.wait_ge(sem("ms_ready"), t + 1)
                a, b_ = rms[:, 4 * t:4 * t + 4], rms[:, 16 + 4 * t:20 + 4 * t]
                ve.tensor_scalar(b_, a, 1.0 / P, RMS_EPS, ALU.mult, ALU.add).then_inc(sem("ms_eps"), 1)
                v.wait_ge(sem("rms_ready"), t + 1)
                link(ve.reciprocal(a, b_))
                j = f"o{t}"
                for h in range(NH):
                    s = slice(h * P, (h + 1) * P)
                    ins = ve.scalar_tensor_tensor(out=oa[:, t, s], in0=bank(j)[:, s], scalar=rms[:, 4 * t + h:4 * t + h + 1],
                                                  in1=gs[:, t, s], op0=ALU.mult, op1=ALU.mult)
                freed(j, ins)

            def residual(n, name, src):
                for t in range(NT):
                    for h in range(2):
                        j = f"{name}{t}.{h}"
                        wait_full(v, j)
                        s = slice(512 * h, 512 * h + 512)
                        ins = ve.scalar_tensor_tensor(out=hbuf[:, t, s], in0=src[:, t, s], scalar=ALPHA, in1=bank(j),
                                                      op0=ALU.mult, op1=ALU.add)
                        freed(j, ins)
                        wait_read(v, j)
                    stats(n, t)
                    normalise(n, t)

            v.wait_ge(sem("h0_in"), 16 * NT)
            v.wait_ge(sem("ln_in"), 64)
            residual(1, "w", h0b)
            for t in range(NT):
                for h in range(2):
                    j = f"sc{t}.{h}"
                    wait_full(v, j)
                    m2 = amax[:, 4 * t + 2 * h:4 * t + 2 * h + 2]
                    link(ve.tensor_reduce(m2, bank(j).rearrange("p (i m) -> p i m", i=2), AX.X, ALU.max))
                    ve.tensor_scalar(m2, m2, -SCALE, None, ALU.mult).then_inc(sem("max_ready"), 1)
                for h in range(2):
                    j = f"sc{t}.{h}"
                    v.wait_ge(sem("exp_ready"), 2 * t + h + 1)
                    s2 = asum[:, 4 * t + 2 * h:4 * t + 2 * h + 2]
                    freed(j, ve.reciprocal(s2, s2))
                    wait_read(v, j)
                    for i in range(2):
                        hh = 2 * h + i
                        ins = ve.tensor_scalar(Pb[:, t % 2, hh, :], Pb[:, t % 2, hh, :],
                                               asum[:, 4 * t + hh:4 * t + hh + 1], None, ALU.mult)
                    ins.then_inc(sem("probs_ready"), 1)
            v.wait_ge(sem("ln_in"), 96)
            residual(2, "wo", hbuf)

            lgs = rt[:, 0:128].rearrange("p (t e) -> p t e", t=NT)
            OH = rt[:, 128:640].rearrange("p (i e) -> p i e", i=16)
            tmp = rt[:, 896:1408].rearrange("p (i e) -> p i e", i=16)
            pos = rt[:, 1408:1536].rearrange("p (t e) -> p t e", t=NT)
            cnt, nov, ovi, ovs = (rt[:, 1536 + 32 * i:1568 + 32 * i] for i in range(4))
            ix = rt[:, 1664:1696].bitcast(U32).rearrange("p (t k) -> p t k", t=NT)
            ixf = rt[:, 1696:1712]
            qq = rt[:, 1712:1840].rearrange("p (t e) -> p t e", t=NT)
            bl = rt[:, 1840:1968].rearrange("p (t e) -> p t e", t=NT)
            slk, blk = rt[:, 1968:1984], rt[:, 1984:2000]
            iof = rt[:, 2000:2000 + P]
            av = rt[:, 2128:2144]
            NX = NBX - E
            cmp_ = rt[0:1, 2144:2144 + NX * E].rearrange("p (b e) -> p b e", e=E)
            tabf = rt[0:CAP, 3000:3000 + NBX]
            etf = rt[0:1, 3100:3100 + NBX]
            prow = rt[:, 3200:3201]
            diag = tmp[:, 0:4, :].rearrange("p i e -> p (i e)")
            link(ve.tensor_tensor_scan(iof, ones[:, :], ones[:, :], -1.0, ALU.mult, ALU.add))
            link(ve.tensor_tensor(diag, iof, ident[:, :], ALU.mult))
            link(ve.tensor_reduce(prow, diag, AX.X, ALU.add))
            for t in range(NT):
                link(ve.tensor_scalar(av[:, 4 * t:4 * t + 4], iof[:, 0:4], float(512 * t + 1), None, ALU.add))
            link(ve.scalar_tensor_tensor(out=av, in0=prow.to_broadcast([P, 16]), scalar=4.0, in1=av,
                                         op0=ALU.mult, op1=ALU.add))
            wait_full(v, "lg")
            freed("lg", ve.tensor_tensor(lgs, bank("lg")[:, 0:128].rearrange("p (t e) -> p t e", t=NT),
                                         rbb.unsqueeze(1).to_broadcast([P, NT, E]), ALU.add))
            wait_read(v, "lg")
            for t in range(NT):
                link(ve.max(topv[:, 8 * t:8 * t + 8], lgs[:, t, :]))
                link(ve.max_index(rt[:, 3264 + 8 * t:3272 + 8 * t].bitcast(U32), topv[:, 8 * t:8 * t + 8], lgs[:, t, :]))
            tv3 = topv.rearrange("p (t k) -> p t k", t=NT)
            ve.tensor_scalar(ntop, tv3[:, :, 0], -1.0, None, ALU.mult).then_inc(sem("top_ready"), 1)
            link(ve.tensor_copy(ixf.rearrange("p (t k) -> p t k", t=NT),
                                rt[:, 3264:3296].bitcast(U32).rearrange("p (t k) -> p t k", t=NT)[:, :, 0:TOPK]))
            link(ve.tensor_tensor(OH, iof[:, 0:E].unsqueeze(1).to_broadcast([P, 16, E]),
                                  ixf.unsqueeze(2).to_broadcast([P, 16, E]), ALU.is_equal))

            def over_choices(o, a):
                return ve.tensor_reduce(o, a.rearrange("p (t k) e -> p t e k", t=NT), AX.X, ALU.add)

            over_choices(Msk, OH).then_inc(sem("chosen"), 1)
            v.wait_ge(sem("gate_exp"), 1)
            link(ve.reciprocal(gsum, gsum))
            link(ve.tensor_tensor(gate, gate, gsum.unsqueeze(2).to_broadcast([P, NT, TOPK]), ALU.mult))
            link(ve.tensor_tensor(tmp, OH, gate.rearrange("p t k -> p (t k)").unsqueeze(2).to_broadcast([P, 16, E]),
                                  ALU.mult))
            over_choices(Gt, tmp).then_inc(sem("gates_ready"), 1)
            wait_full(v, "pos")
            link(ve.tensor_copy(pos, bank("pos")[:, 0:128].rearrange("p (t e) -> p t e", t=NT)))
            freed("pos", ve.tensor_copy(cnt, bank("pos")[:, 128:160]))
            wait_read(v, "pos")
            wait_full(v, "GT")
            freed("GT", ve.tensor_copy(GTs, bank("GT")[0:E, :]))
            link(ve.tensor_scalar(nov, cnt, float(CAP), None, ALU.is_gt))
            for m in range(2, QMAX + 1):
                link(ve.scalar_tensor_tensor(out=nov, in0=cnt, scalar=float(m * CAP), in1=nov, op0=ALU.is_gt, op1=ALU.add))
            link(ve.tensor_tensor_scan(ovi, ones[:, 0:E], nov, 0.0, ALU.mult, ALU.add))
            link(ve.tensor_tensor(ovs, ovi, nov, ALU.subtract))
            link(ve.tensor_scalar(nbt[:, 0:1], ovi[0:1, E - 1:E], float(E), None, ALU.add))
            link(ve.tensor_scalar(nbt[:, 1:2], ovi[0:1, E - 1:E], float(E - 1), None, ALU.add))
            link(ve.tensor_scalar(qq, pos, float(CAP), None, ALU.is_ge))
            z = tmp[:, 0:4, :]
            link(ve.tensor_copy(z, qq))
            for m in range(2, QMAX + 1):
                link(ve.scalar_tensor_tensor(out=qq, in0=pos, scalar=float(m * CAP), in1=qq, op0=ALU.is_ge, op1=ALU.add))
            link(ve.scalar_tensor_tensor(out=pos, in0=qq, scalar=-float(CAP), in1=pos, op0=ALU.mult, op1=ALU.add))
            e4 = iof[:, 0:E].unsqueeze(1).to_broadcast([P, NT, E])
            link(ve.tensor_tensor(bl, qq, ovs.unsqueeze(1).to_broadcast([P, NT, E]), ALU.add))
            link(ve.tensor_tensor(bl, bl, e4, ALU.subtract))
            link(ve.scalar_tensor_tensor(out=bl, in0=bl, scalar=float(E - 1), in1=z, op0=ALU.add, op1=ALU.mult))
            link(ve.tensor_tensor(bl, bl, e4, ALU.add))

            def at_choice(o, a):
                o4 = OH.rearrange("p (t k) e -> p t k e", t=NT)
                t4 = tmp.rearrange("p (t k) e -> p t k e", t=NT)
                for t in range(NT):
                    ins = ve.tensor_tensor(t4[:, t], o4[:, t], a[:, t:t + 1, :].to_broadcast([P, TOPK, E]), ALU.mult)
                link(ins)
                link(ve.tensor_reduce(o, tmp, AX.X, ALU.add))

            at_choice(slk, pos)
            at_choice(blk, bl)
            link(ve.tensor_tensor(Aoh, iof[:, 0:CAP].unsqueeze(1).to_broadcast([P, 16, CAP]),
                                  slk.unsqueeze(2).to_broadcast([P, 16, CAP]), ALU.is_equal))
            ve.tensor_tensor(Boh, iof[:, 0:NBX].unsqueeze(1).to_broadcast([P, 16, NBX]),
                             blk.unsqueeze(2).to_broadcast([P, 16, NBX]), ALU.is_equal)
            ve.tensor_tensor(Aoh, Aoh, av.unsqueeze(2).to_broadcast([P, 16, CAP]), ALU.mult).then_inc(sem("onehots"), 1)
            link(ve.tensor_tensor(cmp_, ovi[0:1, :].unsqueeze(1).to_broadcast([1, NX, E]),
                                  iof[0:1, 0:NX].unsqueeze(2).to_broadcast([1, NX, E]), ALU.is_le))
            link(ve.tensor_reduce(etf[:, E:NBX], cmp_, AX.X, ALU.add))
            link(ve.tensor_copy(etf[:, 0:E], iof[0:1, 0:E]))
            link(ve.tensor_scalar(etab[:, :], etf, float(E - 1), None, ALU.min))
            wait_full(v, "tab")
            freed("tab", ve.tensor_scalar(tabf, bank("tab")[0:CAP, 0:NBX], -1.0, None, ALU.add))
            wait_read(v, "tab")
            link(ve.tensor_copy(stab[:, :], tabf))
            ve.tensor_scalar(gtab[:, :], stab[:, :], 2, None, ALU.arith_shift_right).then_inc(sem("tables_ready"), 1)
            v.wait_ge(sem("tables_ready"), 1)
            v.wait_ge(sem("h2_out"), 16 * NT)
            for t in range(NT):
                for h in range(2):
                    j = f"gb{t}.{h}"
                    wait_full(v, j)
                    s = slice(512 * h, 512 * h + 512)
                    freed(j, ve.scalar_tensor_tensor(out=hbuf[:, t, s], in0=hbuf[:, t, s], scalar=ALPHA, in1=bank(j),
                                                     op0=ALU.mult, op1=ALU.add))
                    wait_read(v, j)

            hh4 = ps[:, 0:4, 0:4 * CAP]
            g4 = glu.rearrange("p (b f s) -> p b f s", b=2, f=4)
            l4 = lin.rearrange("p (b f s) -> p b f s", b=2, f=4)
            wait_read(v, "b1T")
            last = v.value_load(nbt[0:1, 1:2], min_val=E - 1, max_val=NBX - 2)
            base = step[0]

            def swiglu(b, e, steps):
                n = [0]

                def link(ins):
                    n[0] += 1
                    ins.then_inc(sem("dve_step"), 1)
                    v.wait_ge(sem("dve_step"), steps + n[0])

                def bias(o):
                    return b1T[:, bass.ds(e * 16 + o, 8)].rearrange("p (b f) -> p b f", b=2).unsqueeze(3)

                v.wait_ge(slot_free[7], b + 1)
                for i in range(2):
                    ins = ve.tensor_tensor(g4[:, i], ps[:, i, 0:4 * CAP].rearrange("p (f s) -> p f s", f=4),
                                           bias(0)[:, i].to_broadcast([P, 4, CAP]), ALU.add)
                link(ins)
                ve.tensor_scalar(glu, glu, LIMIT, None, ALU.min).then_inc(sem("glu_ready"), 1)
                for i in range(2):
                    ins = ve.tensor_tensor(l4[:, i], ps[:, 2 + i, 0:4 * CAP].rearrange("p (f s) -> p f s", f=4),
                                           bias(8)[:, i].to_broadcast([P, 4, CAP]), ALU.add)
                ins.then_inc(sem("h_read"), 1)
                v.wait_ge(sem("h_read"), b + 1)
                link(ve.tensor_scalar(lin, lin, LIMIT, -LIMIT, ALU.min, ALU.max))
                link(ve.scalar_tensor_tensor(out=lin, in0=lin, scalar=1.0, in1=glu, op0=ALU.add, op1=ALU.mult))
                v.wait_ge(sem("sig_ready"), b + 1)
                v.wait_ge(slot_free[11], b)
                ve.tensor_tensor(act_.rearrange("p k s -> p (k s)"), lin, sig, ALU.mult).then_inc(sem("act_ready"), 1)
                return n[0]

            per = swiglu(0, 0, base)
            with v.Fori(0, last) as b:
                e = v.value_load(etab[0:1, bass.ds(b + 1, 1)], min_val=0, max_val=E - 1)
                swiglu(b + 1, e, (base + per) + per * b)
            step[0], steps[0] = 0, "sum_step"
            v.wait_ge(sem("ln_in"), 128)
            for t in range(NT):
                v.wait_ge(sem(f"y_in{t}"), 16)
                yt = ring[:, 2 * t:2 * t + 2, :].rearrange("p s n -> p (s n)").rearrange("p (k d) -> p k d", k=TOPK)
                for k in range(TOPK):
                    ve.scalar_tensor_tensor(out=hbuf[:, t, :], in0=yt[:, k, :], scalar=gate[:, t, k:k + 1],
                                            in1=hbuf[:, t, :], op0=ALU.mult, op1=ALU.add).then_inc(sem("summed"), 1)
                    v.wait_ge(sem("summed"), TOPK * t + k + 1)
                stats(3, t)
                normalise(3, t)

        @block.tensor
        def _(pe):
            te = nc.tensor

            def job(name):
                b, use = JOBS[name]
                if use > 1:
                    pe.wait_ge(bank_free[b], use - 1)
                return bank(name)

            def full(name, ins):
                ins.then_inc(bank_full[JOBS[name][0]], 1)

            def mm(o, l, r, start, stop):
                return te.matmul(o, l, r, start=start, stop=stop)

            def tr(o, i, k=P):
                return te.transpose(o, i, ident[0:k, 0:k])

            def weights(w, i):
                s, use = SLOT_OF[w, i]
                pe.wait_ge(slot_full[s], 16 * use)
                n = {"u": 512, "glu": 512, "main": SLOT}.get(w, D)
                return ring[:, s, :].rearrange("p (k n) -> p k n", n=n)

            pe.wait_ge(sem("consts"), 1)
            pe.wait_ge(sem("params"), 16 * 17)
            o = job("par")
            tr(o[:, 0:16], rows, 16)
            for i in range(3):
                tr(o[:, 16 + 16 * i:32 + 16 * i], lam_in[:, i * P:(i + 1) * P], 16)
            full("par", tr(o[:, 64:96], dn, 32))
            o = job("cT")
            for r in range(2):
                for i in range(2):
                    ins = tr(o[:, (2 * r + i) * P:(2 * r + i + 1) * P], craw[:, r, i].rearrange("p a m -> p (a m)"))
            full("cT", ins)

            def transpose_h(n, t):
                pe.wait_ge(sem("normed"), NT * n + t + 1)
                for h in range(2):
                    nm = f"hT{n}.{t}.{h}"
                    o = job(nm)
                    for k in range(4):
                        ins = tr(o[:, k * P:(k + 1) * P], hbuf[:, t, (4 * h + k) * P:(4 * h + k + 1) * P])
                    full(nm, ins)

            for t in range(NT):
                transpose_h(0, t)
            pe.wait_ge(sem("q_ready"), 1)
            for r in range(2):
                for q in range(4):
                    nm = f"W{r}.{q}"
                    o = job(nm)
                    for i in range(4):
                        ins = tr(o[:, i * P:(i + 1) * P], Qb[:, r, 4 * q + i].rearrange("p j n -> p (j n)"))
                    full(nm, ins)
            pe.wait_ge(sem("s5_v"), 1)
            for q in range(8):
                nm = f"KK{q}"
                o = job(nm)
                for i in range(4):
                    g = 4 * q + i
                    b0, gi = PST * (g // GI), g % GI
                    rws = slice(b0, b0 + PST)
                    for c0, c1, w in ((0, N, None), (N, P, 1)):
                        for r in range(2):
                            rhs = cpar[rws, r, gi, :] if w is None else \
                                Vc[rws, r, gi, 0:L - 1, :].rearrange("p k n -> p (k n)")
                            ins = mm(o[0:N, i * P + c0:i * P + c1], bbar[rws, r, gi, :], rhs, r == 0, r == 1)
                full(nm, ins)
            for t in range(NT):
                for h in range(2):
                    wait_read(pe, f"hT0.{t}.{h}")
            for c in range(4):
                nm = f"u{c}"
                o = job(nm)
                for k in range(KD):
                    w = weights("u", k // 4)
                    ins = mm(o, w[:, k % 4, c * P:(c + 1) * P], hT[:, k, :], k == 0, k == KD - 1)
                full(nm, ins)
            for c in range(5):
                if c < 4:
                    wait_read(pe, f"u{c}")
                    uj = ucm[:, c, :].rearrange("p (c j) -> p j c", j=L)
                    for h in range(2):
                        nm = f"U{c}.{h}"
                        o = job(nm)
                        for j in range(4):
                            ins = mm(o[0:NC, j * P:(j + 1) * P], uj[:, 4 * h + j, :], ident[:, :], True, True)
                        full(nm, ins)
                if c:
                    nm = f"ug{c - 1}"
                    wait_read(pe, f"U{c - 1}.1")
                    wait_read(pe, f"U{c - 1}.0")
                    o = job(nm)
                    for g in range(8):
                        ins = tr(o[:, g * NC:(g + 1) * NC], Ub[0:NC, (c - 1) % 2, g, :], NC)
                    full(nm, ins)
            for c in range(4):
                wait_read(pe, f"ug{c}")
            for r in range(2):
                for h in range(2):
                    nm = f"Z{r}.{h}"
                    o = job(nm)
                    for i in range(8):
                        for a in range(2):
                            gi = 8 * h + i
                            ins = mm(o[PST * a:PST * (a + 1), i * NC:(i + 1) * NC], Wst[:, r, gi, PST * a:PST * (a + 1)],
                                     ug[:, GI * a + gi, :], True, True)
                    full(nm, ins)
            pe.wait_ge(sem("mem_in"), 16)
            for m in range(2):
                for h in range(2):
                    nm = f"mT{m}.{h}"
                    o = job(nm)
                    for k in range(4):
                        ins = tr(o[:, k * P:(k + 1) * P], memx[:, m, (4 * h + k) * P:(4 * h + k + 1) * P])
                    full(nm, ins)
            for m in range(2):
                for h in range(2):
                    wait_read(pe, f"mT{m}.{h}")
            for i in range(4):
                nm = f"K{i}"
                o = job(nm)
                for c in range(2):
                    for k in range(KD):
                        w = weights("wk", k // 2)
                        ins = mm(o[:, c * M:(c + 1) * M], w[:, k % 2, (2 * i + c) * P:(2 * i + c + 1) * P], memT[:, k, :],
                                 k == 0, k == KD - 1)
                full(nm, ins)
            for m in range(2):
                for h in range(2):
                    nm = f"V{m}.{h}"
                    o = job(nm)
                    for k in range(KD):
                        w = weights("wv", k // 2)
                        ins = mm(o, memT[:, k, m * P:(m + 1) * P], w[:, k % 2, 512 * h:512 * h + 512], k == 0, k == KD - 1)
                    full(nm, ins)
            pe.wait_ge(sem("toe_ready"), 1)
            pe.wait_ge(sem("x_ready"), 1)
            for c in range(5):
                if c < 4:
                    for h in range(2):
                        nm = f"Y{c}.{h}"
                        o = job(nm)
                        for i in range(4):
                            g = 8 * c + 4 * h + i
                            b0, gi = PST * (g // GI), g % GI
                            oo = o[0:NC, i * P:(i + 1) * P]
                            mm(oo, ug[:, g, :], Toe[:, g, :], True, False)
                            for r in range(2):
                                ins = mm(oo, X[b0:b0 + PST, r, gi, 0:NC],
                                         Vc[b0:b0 + PST, r, gi].rearrange("p k n -> p (k n)"), False, r == 1)
                        full(nm, ins)
                if c:
                    nm = f"yT{c - 1}"
                    wait_read(pe, f"Y{c - 1}.0")
                    wait_read(pe, f"Y{c - 1}.1")
                    o = job(nm)
                    for j in range(L):
                        ins = tr(o[:, j * NC:(j + 1) * NC], Yb[0:NC, (c - 1) % 2, j].rearrange("p g n -> p (g n)"), NC)
                    full(nm, ins)
            for c in range(4):
                wait_read(pe, f"yT{c}")
            for c in range(4):
                nm = f"z{c}"
                o = job(nm)
                w = weights("glu", 0)
                for k in range(4):
                    ins = mm(o, w[:, k, c * P:(c + 1) * P], ycm[:, k, :], k == 0, k == 3)
                full(nm, ins)
            for nm0, off in (("f", HW), ("q", 0)):
                for h in range(4):
                    nm = f"{nm0}{h}"
                    o = job(nm)
                    for k in range(KD):
                        w = weights("main", k)
                        ins = mm(o, w[:, 0, off + h * P:off + (h + 1) * P], hT[:, k, :], k == 0, k == KD - 1)
                    full(nm, ins)
            for nm0, off in (("i", 2 * HW), ("g", 3 * HW)):
                for t in range(NT):
                    nm = f"{nm0}{t}"
                    o = job(nm)
                    for k in range(KD):
                        w = weights("main", k)
                        ins = mm(o, hT[:, k, t * P:(t + 1) * P], w[:, 0, off:off + HW], k == 0, k == KD - 1)
                    full(nm, ins)
            for n in range(len(LEVELS) + 1):
                if n == 0:
                    pe.wait_ge(sem("f_ready"), 4)
                    for h in range(4):
                        wait_read(pe, f"q{h}")
                    lt, rh = kh, qh
                else:
                    pe.wait_ge(sem("pair_ready"), n)
                    lt = rh = P0 if (n - 1) % 2 == 0 else P1
                for t in range(NT):
                    nm = f"s{n}.{t}"
                    o = job(nm)
                    for h in range(NH):
                        s = slice(h * T + t * P, h * T + (t + 1) * P)
                        ins = mm(o[:, h * P:(h + 1) * P], lt[:, s], rh[:, s], True, True)
                    full(nm, ins)
            pe.wait_ge(sem("kdec_ready"), 1)
            for t in range(NT):
                nm = f"kd{t}"
                o = job(nm)
                for h in range(NH):
                    s = slice(h * T + t * P, h * T + (t + 1) * P)
                    ins = tr(o[:, h * P:(h + 1) * P], P1[:, s])
                full(nm, ins)
            pe.wait_ge(sem("qe_ready"), 1)

            def transpose_oa(t):
                nm = f"oaT{t}"
                wait_read(pe, f"o{t}")
                o = job(nm)
                for c in range(4):
                    ins = tr(o[:, c * P:(c + 1) * P], oa[:, t, c * P:(c + 1) * P])
                full(nm, ins)

            for t in range(NT):
                wait_read(pe, f"s{len(LEVELS)}.{t}")
                wait_read(pe, f"kd{t}")
                if t:
                    wait_read(pe, f"st{t - 1}")
                nm = f"o{t}"
                o = job(nm)
                for h in range(NH):
                    oo = o[:, h * P:(h + 1) * P]
                    ins = mm(oo, Sc[:, t, h, :], vh[:, t, h * P:(h + 1) * P], True, t == 0)
                    if t:
                        ins = mm(oo, qe[:, h * T + t * P:h * T + (t + 1) * P], st[:, h, :], False, True)
                full(nm, ins)
                if t < NT - 1:
                    nm = f"st{t}"
                    o = job(nm)
                    for h in range(NH):
                        ins = mm(o[:, h * P:(h + 1) * P], kdT[:, t, h, :], vh[:, t, h * P:(h + 1) * P], True, True)
                    full(nm, ins)
                if t:
                    transpose_oa(t - 1)
            transpose_oa(NT - 1)

            def project(nm0, w0, n, left):
                for t in range(NT):
                    for h in range(2):
                        nm = f"{nm0}{t}.{h}"
                        o = job(nm)
                        for k in range(KD):
                            w = weights(w0, k // 2)
                            ins = mm(o, left(k, t), w[:, k % 2, 512 * h:512 * h + 512], k == 0, k == KD - 1)
                        full(nm, ins)
                    if t:
                        transpose_h(n, t - 1)
                transpose_h(n, NT - 1)

            for t in range(NT):
                wait_read(pe, f"oaT{t}")
            pe.wait_ge(sem("glu_done"), 4)
            project("w", "wout", 1, lambda k, t: hT[:, k, t * P:(t + 1) * P] if k < 4 else
                    s5T[:, k - 4, t * P:(t + 1) * P])
            for t in range(NT):
                for h in range(2):
                    wait_read(pe, f"hT1.{t}.{h}")
            for c in range(8):
                nm = f"aq{c}"
                o = job(nm)
                for k in range(KD):
                    w = weights("wq", k // 2)
                    ins = mm(o, w[:, k % 2, c * P:(c + 1) * P], hT[:, k, :], k == 0, k == KD - 1)
                full(nm, ins)
            for c in range(8):
                wait_read(pe, f"aq{c}")

            for t in range(NT + 1):
                if t < NT:
                    for h in range(2):
                        nm = f"sc{t}.{h}"
                        o = job(nm)
                        for i in range(2):
                            for kk in range(2):
                                c = 2 * (2 * h + i) + kk
                                ins = mm(o[:, i * M:(i + 1) * M], qT[:, c, t * P:(t + 1) * P], kT[:, c, :],
                                         kk == 0, kk == 1)
                        full(nm, ins)
                if t:
                    pe.wait_ge(sem("probs_ready"), 2 * t)
                    for m in range(2):
                        nm = f"PT{t - 1}.{m}"
                        o = job(nm)
                        for hh in range(NH):
                            ins = tr(o[:, hh * P:(hh + 1) * P], Pb[:, (t - 1) % 2, hh, m * P:(m + 1) * P])
                        full(nm, ins)
            for t in range(NT):
                for m in range(2):
                    wait_read(pe, f"PT{t}.{m}")
            for c in range(8):
                nm = f"ao{c}"
                o = job(nm)
                for m in range(2):
                    ins = mm(o, vm[:, m, c * P:(c + 1) * P], PT[:, m, c // 2, :], m == 0, m == 1)
                full(nm, ins)
            for c in range(8):
                wait_read(pe, f"ao{c}")
            project("wo", "wo", 2, lambda k, t: hT[:, k, t * P:(t + 1) * P])
            pe.wait_ge(sem("late_in"), 48)
            o = job("b1T")
            for q in range(4):
                ins = tr(o[:, q * P:(q + 1) * P], b1raw[:, q, :])
            full("b1T", ins)
            for t in range(NT):
                for h in range(2):
                    wait_read(pe, f"hT2.{t}.{h}")
            o = job("lg")
            for t in range(NT):
                for k in range(KD):
                    ins = mm(o[:, t * E:(t + 1) * E], hT[:, k, t * P:(t + 1) * P], rw[:, k, :], k == 0, k == KD - 1)
            full("lg", ins)
            pe.wait_ge(sem("chosen"), 1)
            o = job("pos")
            for t in range(NT):
                for i in range(t + 1):
                    mm(o[:, t * E:(t + 1) * E], (tri if i == t else ones)[:, :], Msk[:, i, :], i == 0, i == t)
            for i in range(NT):
                ins = mm(o[:, NT * E:NT * E + E], ones[:, :], Msk[:, i, :], i == 0, i == NT - 1)
            full("pos", ins)
            pe.wait_ge(sem("gates_ready"), 1)
            o = job("GT")
            for t in range(NT):
                ins = mm(o[0:E, t * P:(t + 1) * P], Gt[:, t, :], ident[:, :], True, True)
            full("GT", ins)
            pe.wait_ge(sem("onehots"), 1)
            o = job("tab")
            for i in range(16):
                ins = mm(o[0:CAP, 0:NBX], Aoh[:, i, :], Boh[:, i, :], i == 0, i == 15)
            full("tab", ins)
            wait_read(pe, "GT")
            for t in range(NT):
                for h in range(2):
                    nm = f"gb{t}.{h}"
                    o = job(nm)
                    full(nm, mm(o, GTs[:, t * P:(t + 1) * P], b2sb[:, 512 * h:512 * h + 512], True, True))
            pe.wait_ge(sem("tables_ready"), 1)
            last = pe.value_load(nbt[0:1, 1:2], min_val=E - 1, max_val=NBX - 2)
            for b_ in range(8):
                pe.wait_ge(bank_free[b_], sum(bb == b_ for bb, _ in JOBS.values()))

            def rows_in(b):
                pe.wait_ge(sem("x_gathered"), 16 * b + 16)
                for k in range(KD):
                    ins = tr(ps[:, 6 + k // 4, (k % 4) * CAP:(k % 4 + 1) * CAP], Xg[:, k * P:(k + 1) * P], CAP)
                ins.then_inc(sem("xt_full"), 1)

            def first(b):
                pe.wait_ge(sem("xt_copied"), b + 1)
                pe.wait_ge(sem("h_read"), b)
                for k in range(KD):
                    pe.wait_ge(slot_full[k], 16 * b + 16 * (USES[k] + 1))
                    for f in range(16):
                        ins = te.matmul(ps[:, f // 4, (f % 4) * CAP:(f % 4 + 1) * CAP],
                                        ring[:, k, f * P:(f + 1) * P], xT[:, k, :],
                                        start=(k == 0 and f % 4 == 0), stop=(k == KD - 1), skip_group_check=True)
                    ins.then_inc(slot_free[k], 1)

            def second(b):
                pe.wait_ge(sem("act_ready"), b + 1)
                pe.wait_ge(sem("y_copied"), b)
                for k in range(KD):
                    s = 8 + k // 2
                    if k % 2 == 0:
                        pe.wait_ge(slot_full[s], 16 * b + 16)
                    for h in range(2):
                        c0 = (k % 2) * D + 512 * h
                        ins = te.matmul(ps[0:CAP, 4 + h, :], act_[:, k, :], ring[:, s, c0:c0 + 512],
                                        start=(k == 0), stop=(k == KD - 1))
                    if k % 2 == 1:
                        ins.then_inc(slot_free[s], 1)

            rows_in(0)
            first(0)
            rows_in(1)
            with pe.Fori(0, last) as b:
                first(b + 1)
                rows_in(b + 2)
                second(b)
            second(last)


def kernel(**inputs):
    import concourse.bacc as _bacc
    from concourse.bass_utils import run_bass_kernel_spmd as _run

    nc = _bacc.Bacc("TRN2", target_bir_lowering=False, num_devices=1)
    arrays, aps = {}, {}
    for name, value in inputs.items():
        a = np.ascontiguousarray(value)
        arrays[f"in_{name}"] = a
        aps[name] = nc.dram_tensor(f"in_{name}", a.shape, mybir.dt.from_np(a.dtype), kind="ExternalInput").ap()
    out = nc.dram_tensor("out_rows", (1, T, D), F32, kind="ExternalOutput").ap()
    trunk_layer(nc, aps, out)
    r = _run(nc, [arrays], core_ids=[0])
    return r.results[0]["out_rows"]
```

```python
import numpy as np
import concourse.bass as bass
from concourse import mybir
from concourse.alu_op_type import AluOpType as ALU

ACT = mybir.ActivationFunctionType
AX = mybir.AxisListType
F32, I32, U32, U8 = mybir.dt.float32, mybir.dt.int32, mybir.dt.uint32, mybir.dt.uint8
F32R = mybir.dt.float32r

P = 128
D = 1024
T = 512
NT = T // P
KD = D // P
HW = 512
NH = 4
G, PST, N = 32, 64, 16
GI = G // 2
L = 8
NC = T // L
M = 256
XD = 256
SCALE = XD ** -0.5
E, FF, TOPK = 32, 1024, 4
CAP = 96
QMAX = (T - 1) // CAP
NBX = E + (T * TOPK) // (CAP + 1) + 1 + 2
LIMIT, SW_ALPHA = 7.0, 1.702
ALPHA = 2.0 ** 0.25
LN_EPS, RMS_EPS = 1e-5, 1e-6
MAGIC = 12582912.0
TWO_PI = 6.283185307179586
TP1 = 6.28125
TP2 = float(np.float32(0.0019353071))
TP3 = float(TWO_PI - TP1 - TP2)
PI_BELOW = 3.1415925

RING, SLOT = 12, 2048
PRE = 5
COLS = {"q": 0, "f": HW, "i": 2 * HW, "g": 3 * HW, "u": 4 * HW}
STREAM = ([("wk", i) for i in range(4)] + [("wv", i) for i in range(4)]
          + [(w, i) for w in ("u", "f", "q", "i") for i in range(2)] + [("glu", 0)]
          + [("g", i) for i in range(2)] + [("wout", i) for i in range(4)]
          + [("wq", i) for i in range(4)] + [("wo", i) for i in range(4)])
SLOT_OF = {w: (n % PRE, n // PRE + 1) for n, w in enumerate(STREAM)}
USES = [sum(n % PRE == s for n in range(len(STREAM))) for s in range(8)]
LAST_JOB = {"u": "u3", "wk": "K3", "wv": "V1.1", "glu": "z3", "f": "f3", "q": "q3", "i": "i3", "g": "g3",
            "wout": "w3.1", "wq": "aq7", "wo": "wo3.1"}

PARAMS = 17
LEVELS = [64, 32, 16, 8, 4, 2, 1]
BETWEEN = [["i0"], ["i1"], ["i2"], ["z0", "z1"], ["z2", "z3"], ["i3"], ["g0"], ["g1", "g2", "g3"]]


def job_order():
    j = [f"mT{m}.{h}" for m in range(2) for h in range(2)] + ["K0", "K1", "par", "cT", "K2", "K3"]
    for t in range(NT):
        j += [f"hT0.{t}.{h}" for h in range(2)] + [f"V{t // 2}.{t % 2}"]
    j += [f"u{c}" for c in range(4)]
    j += [f"W{r}.{q}" for r in range(2) for q in range(4)]
    j += [f"KK{q}" for q in range(8)]
    j += [f"f{h}" for h in range(4)] + [f"Z{r}.{h}" for r in range(2) for h in range(2)] + [f"q{h}" for h in range(4)]
    j += [f"Y{c}" for c in range(4)]
    for n in range(len(LEVELS) + 1):
        j += [f"s{n}.{t}" for t in range(NT)] + BETWEEN[n]
    j += [f"kd{t}" for t in range(NT)]
    for t in range(NT):
        j += [f"o{t}"] + ([f"st{t}"] if t < NT - 1 else [])
        if t:
            j += [f"oaT{t - 1}"]
    j += [f"oaT{NT - 1}"]
    for t in range(NT):
        j += [f"w{t}.{h}" for h in range(2)]
        if t:
            j += [f"hT1.{t - 1}.{h}" for h in range(2)]
    j += [f"hT1.{NT - 1}.{h}" for h in range(2)]
    j += [f"aq{c}" for c in range(8)]
    for t in range(NT):
        j += [f"sc{t}.{h}" for h in range(2)]
        if t:
            j += [f"PT{t - 1}.{h}" for h in range(2)]
    j += [f"PT{NT - 1}.{h}" for h in range(2)]
    j += [f"ao{c}" for c in range(8)] + ["b1T"]
    for t in range(NT):
        j += [f"wo{t}.{h}" for h in range(2)]
        if t:
            j += [f"hT2.{t - 1}.{h}" for h in range(2)]
    j += [f"hT2.{NT - 1}.{h}" for h in range(2)]
    gb = [f"gb{t}.{h}" for t in range(NT) for h in range(2)]
    return j + ["lg", "pos", "GT"] + gb[:4] + ["tab"] + gb[4:] + ["wtab"]


JOBS = {name: (n % 8, n // 8 + 1) for n, name in enumerate(job_order())}


def trunk_layer(nc, A, out):
    x, mem = A["x"][0], A["mem"][0]
    w_in, w_out, w_glu = A["w_in"][0], A["w_out"][0], A["s5_w_glu"][0]
    w1, w2 = A["exp_w1"][0], A["exp_w2"][0]

    def rows_in_dram(name, n, width):
        return nc.dram_tensor(name, [n, width], F32, kind="Internal").ap()

    h0_rows = rows_in_dram("h0_rows", T, D)
    h2_rows = rows_in_dram("h2_rows", T, D)
    sum_rows = rows_in_dram("sum_rows", T + CAP, D)
    u_rows = rows_in_dram("u_rows", HW, T)
    s5_rows = rows_in_dram("s5_rows", HW, T)

    place = {}

    def sb(name, shape, dt=F32):
        place[name] = (nc.sbuf_base + 31) // 32 * 32
        return nc.alloc_sbuf_tensor(name, shape, dt)

    def float32r_view(name, of, at, n):
        return nc.alloc_sbuf_tensor_at(name, [P, n], F32R, offset=place[of] + 4 * at)

    ring = sb("ring", [P, RING, SLOT])
    hbuf = sb("hbuf", [P, NT, D])
    hT = sb("hT", [P, KD, T])
    lnw = sb("lnw", [P, 2, D])
    kv = sb("kv", [P, 4096])
    ident = sb("ident", [P, P])
    tri = sb("tri", [P, P])
    ones = sb("ones", [P, P])
    masks = sb("masks", [P, len(LEVELS) + 1, P], U8)
    b1T = sb("b1T", [P, E * 16])
    C = sb("arena_c", [P, 11392])
    small = sb("small", [P, 1280])

    def flat(t, a, n):
        return t[:, a:a + n]

    B_ = hbuf[:, :, :].rearrange("p t d -> p (t d)")

    W_ = [ring[:, PRE + i, :] for i in range(RING - PRE)]
    W34, W56 = (ring[:, PRE + i:PRE + i + 2, :].rearrange("p s n -> p (s n)") for i in (3, 5))
    W12 = ring[:, PRE + 1:PRE + 3, :].rearrange("p s n -> p (s n)")
    memx = W_[3].rearrange("p (m d) -> p m d", m=2)
    memT = W_[4].rearrange("p (k m) -> p k m", k=KD)
    Wst = W34.rearrange("p (r g m) -> p r g m", r=2, g=GI)
    ucm = W_[5].rearrange("p (c t) -> p c t", c=4)
    Toe = W56.rearrange("p (g m) -> p g m", g=G)
    Vc = flat(C, 0, 4096).rearrange("p (r g k n) -> p r g k n", r=2, g=GI, k=L)
    Qb = flat(C, 4096, 4096).rearrange("p (r g k n) -> p r g k n", r=2, g=GI, k=L)
    X = flat(C, 6144, 2 * GI * (NC + 1)).rearrange("p (r g c) -> p r g c", r=2, g=GI)
    turn = W_[0].rearrange("p (r g c) -> p r g c", r=2, g=GI)
    t3 = [flat(C, 4096 + 1024 * i, 1024) for i in range(2)] + [flat(C, 10368, 1024)]
    KKs = W12[0:N, :].rearrange("p (g m) -> p g m", g=G)
    ug = B_[:, 0:2048].rearrange("p (g c) -> p g c", g=G)
    Ys = flat(C, 4096, 2048).rearrange("p (g c) -> p g c", g=G)
    ycm = W_[5].rearrange("p (c t) -> p c t", c=4)
    s5g = flat(C, 4096, 2048).rearrange("p (c t) -> p c t", c=4)
    s5T = W_[6].rearrange("p (c t) -> p c t", c=4)
    kT = flat(kv, 0, 2048).rearrange("p (c m) -> p c m", c=KD)
    vm = flat(kv, 2048, 2048).rearrange("p (m d) -> p m d", m=2)
    cum, qh, P0, P1 = W_[1], W_[2], W_[3], B_[:, 2048:4096]
    kh = flat(C, 8256, 2048)
    Sc = W_[4].rearrange("p (t h s) -> p t h s", t=NT, h=NH)
    vh = flat(C, 0, 2048).rearrange("p (t e) -> p t e", t=NT)
    gs = flat(C, 2048, 2048).rearrange("p (t e) -> p t e", t=NT)
    qe = flat(C, 6144, 2048)
    oa = flat(C, 4096, 2048).rearrange("p (t e) -> p t e", t=NT)
    st = flat(C, 10368, 512).rearrange("p (h e) -> p h e", h=NH)
    sq = flat(C, 10880, 512)
    kdT = cum.rearrange("p (t h d) -> p t h d", t=NT, h=NH)
    qT = flat(C, 0, 4096).rearrange("p (c t) -> p c t", c=KD)
    Pb = flat(C, 4096, 2048).rearrange("p (b h m) -> p b h m", b=2, h=NH)
    PT = flat(C, 6144, 4096).rearrange("p (m h t) -> p m h t", m=2, h=NH)
    Aoh = flat(kv, 2304, 16 * CAP).rearrange("p (i s) -> p i s", i=16)
    Atok = flat(C, 1792, 16 * CAP).rearrange("p (i s) -> p i s", i=16)
    Boh = flat(C, 5888, 16 * NBX).rearrange("p (i s) -> p i s", i=16)
    Xg = C[0:CAP, 0:D]
    xT = flat(C, 1024, KD * CAP).rearrange("p (k s) -> p k s", k=KD)
    glu = flat(C, 1792, KD * CAP)
    lin = flat(C, 2560, KD * CAP)
    sig = flat(C, 3328, KD * CAP)
    act_ = flat(C, 4096, KD * CAP)
    act_hi = float32r_view("act_high", "arena_c", 5888, KD * CAP)
    act_lo = float32r_view("act_rest", "arena_c", 6720, KD * CAP)
    w2_hi = [float32r_view(f"w2_high{i}", "hT" if i < 2 else "kv", SLOT * (i % 2), SLOT) for i in range(4)]
    w2_lo = [float32r_view(f"w2_rest{i}", "ring", SLOT * (8 + i), SLOT) for i in range(4)]
    ysb = C[0:CAP, 4864:4864 + D]
    rt = C[:, 6912:11392]
    b1raw = flat(C, 10368, 512).rearrange("p (q f) -> p q f", q=4)
    b2sb = kv[0:E, 512:512 + D]
    GTs = kv[0:E, 1792:2304]
    Msk = rt[:, 640:768].rearrange("p (t e) -> p t e", t=NT)
    Gt = rt[:, 768:896].rearrange("p (t e) -> p t e", t=NT)
    rw = flat(C, 10880, KD * E).rearrange("p (k e) -> p k e", k=KD)

    at = [0]

    def sm(n, parts=P):
        a = at[0]
        at[0] += n
        assert at[0] <= 1280
        return small[0:parts, a:a + n]

    rows = b1T[0:16, 0:128]
    lam_in = b1T[0:GI, 128:512]
    dn = sm(128, G)
    rowsT = sm(96)
    ab = sm(16 * 24).rearrange("p (n g) -> p n g", g=GI)
    lb = sm(8)
    lbx = sm(12)
    rms = sm(32)
    amax, asum = sm(16), sm(16)
    mvs = sm(12)
    topv = sm(32)
    ntop, gsum = sm(4), sm(4)
    ngb = sm(128)
    stat = sm(16)
    mv = sm(8)
    el = sm(16)
    z1 = sm(32).rearrange("p (r g) -> p r g", r=2)
    z2 = sm(32).rearrange("p (r g) -> p r g", r=2)
    z3 = sm(32).rearrange("p (r g) -> p r g", r=2)
    gate = sm(16).rearrange("p (t k) -> p t k", t=NT)
    rbb = sm(32)
    idle = sm(1)
    gix, six = nc.alloc_sbuf_tensor("gix", [CAP, 1], I32), nc.alloc_sbuf_tensor("six", [CAP, 1], I32)
    gtab = nc.alloc_sbuf_tensor("gtab", [CAP, NBX], I32)
    stab = nc.alloc_sbuf_tensor("stab", [CAP, NBX], I32)
    wtab = nc.alloc_sbuf_tensor("wtab", [CAP, NBX], F32)
    etab = nc.alloc_sbuf_tensor("etab", [1, NBX], I32)
    nbt = nc.alloc_sbuf_tensor("nbt", [1, 2], I32)
    s5p = flat(C, 8256, 2048)
    braw = s5p[:, 0:512].rearrange("p (r g n) -> p r g n", r=2, g=GI)
    bbar = flat(C, 10368, 512).rearrange("p (r g n) -> p r g n", r=2, g=GI)
    craw = s5p[:, 512:1024].rearrange("p (r i a m) -> p r i a m", r=2, i=2, a=2)
    cpar = flat(C, 10880, 512).rearrange("p (r g n) -> p r g n", r=2, g=GI)
    tq = [s5p[:, 1024 + 256 * i:1280 + 256 * i].rearrange("p (g n) -> p g n", g=GI) for i in range(2)]
    masktmp = W_[0]
    tv = [s5p[:, 1536 + 256 * i:1792 + 256 * i].rearrange("p (g n) -> p g n", g=GI) for i in range(2)]

    skip = b1T[0:N, :].rearrange("p (g n) -> p g n", g=G)

    ps = nc.alloc_psum_tensor("ps", [P, 8, 512], F32)
    S = {}

    def sem(name):
        if name not in S:
            S[name] = nc.alloc_semaphore(name)
        return S[name]

    bank_full = [sem(f"bank_full{b}") for b in range(8)]
    bank_free = [sem(f"bank_free{b}") for b in range(8)]
    slot_full = [sem(f"slot_full{s}") for s in range(RING)]
    slot_free = [sem(f"slot_free{s}") for s in range(RING)]

    def bank(job):
        return ps[:, JOBS[job][0], :]

    def wait_full(eng, job):
        b, use = JOBS[job]
        eng.wait_ge(bank_full[b], use)

    def wait_read(eng, job):
        b, use = JOBS[job]
        eng.wait_ge(bank_free[b], use)

    def freed(job, ins):
        ins.then_inc(bank_free[JOBS[job][0]], 1)

    block = nc.Block()
    with block:
        @block.sync
        def _(sp):
            for t in range(NT):
                sp.dma_start(hbuf[:, t, :], x[t * P:(t + 1) * P, :]).then_inc(sem(f"x_in{t}"), 16)
            sp.dma_start(lnw[:, 0, :], A["ln_in_g"].partition_broadcast(P)).then_inc(sem("ln_in"), 16)
            sp.dma_start(lnw[:, 1, :], A["ln_in_b"].partition_broadcast(P)).then_inc(sem("ln_in"), 16)
            for i, nm in enumerate(("s5_lam_re", "s5_lam_im", "s5_log_dt")):
                sp.dma_start(lam_in[:, i * P:(i + 1) * P].rearrange("g (a p) -> g a p", a=2),
                             A[nm][0].rearrange("(a g) p -> g a p", a=2)).then_inc(sem("params"), 16)
            for r, nm in enumerate(("s5_b_re", "s5_b_im")):
                for a in range(2):
                    sp.dma_start(braw[a * PST:(a + 1) * PST, r],
                                 A[nm][0, a * GI:(a + 1) * GI].rearrange("g p n -> p g n")).then_inc(sem("params"), 16)

            def two_chunks(w, i):
                return w[i * 256:(i + 1) * 256, :].rearrange("(k p) n -> p k n", p=P)

            for n, (w, i) in enumerate(STREAM):
                s, use = SLOT_OF[w, i]
                if use > 1:
                    wait_full(sp, LAST_JOB[STREAM[n - PRE][0]])
                if w in COLS:
                    src = w_in[i * 512:(i + 1) * 512, COLS[w]:COLS[w] + HW].rearrange("(k p) n -> p k n", p=P)
                elif w == "glu":
                    src = w_glu.rearrange("(k p) n -> p k n", p=P)
                else:
                    src = two_chunks({"wk": A["xa_w_k"][0], "wv": A["xa_w_v"][0], "wout": w_out,
                                      "wq": A["xa_w_q"][0], "wo": A["xa_w_o"][0]}[w], i)
                dst = ring[:, s, :].rearrange("p (k n) -> p k n", n=D if w[0] == "w" else HW)
                sp.dma_start(dst, src).then_inc(slot_full[s], 16)

            def load_w1(k, e_rows):
                sp.dma_start(ring[:, k, :], e_rows).then_inc(slot_full[k], 16)

            def load_w1_dyn(b, e):
                for k in range(8):
                    sp.wait_ge(slot_free[k], b)
                    load_w1(k, w1[bass.ds(e, 1), k * P:(k + 1) * P, :].rearrange("a p n -> p (a n)"))

            def load_w2_dyn(b, e):
                for q in range(4):
                    sp.wait_ge(slot_free[8 + q], b)
                    sp.dma_start(ring[:, 8 + q, :].rearrange("p (k n) -> p k n", k=2),
                                 w2[bass.ds(e, 1), q * 256:(q + 1) * 256, :]
                                 .rearrange("a (k p) n -> p (a k) n", p=P)).then_inc(slot_full[8 + q], 16)

            sp.wait_ge(sem("normed"), 2 * NT)
            for k in range(PRE, 8):
                load_w1(k, w1[0, k * P:(k + 1) * P, :])
            for q in range(4):
                sp.dma_start(ring[:, 8 + q, :].rearrange("p (k n) -> p k n", k=2),
                             two_chunks(w2[0], q)).then_inc(slot_full[8 + q], 16)
            for k in range(PRE):
                n = max(n for n in range(len(STREAM)) if n % PRE == k)
                wait_full(sp, LAST_JOB[STREAM[n][0]])
                load_w1(k, w1[0, k * P:(k + 1) * P, :])
            for t in range(NT):
                sp.wait_ge(sem("normed"), 2 * NT + t + 1)
                sp.dma_start(h2_rows[t * P:(t + 1) * P, :], hbuf[:, t, :]).then_inc(sem("h2_out"), 16)
            for t in range(NT):
                wait_read(sp, f"gb{t}.0")
                wait_read(sp, f"gb{t}.1")
                sp.dma_start(sum_rows[t * P:(t + 1) * P, :], hbuf[:, t, :]).then_inc(sem("sum_out"), 16)
            sp.dma_start(sum_rows[T:T + CAP, :], hbuf[0:CAP, 0, :]).then_inc(sem("sum_out"), 16)
            sp.wait_ge(sem("tables_ready"), 1)
            nb = sp.value_load(nbt[0:1, 0:1], min_val=E, max_val=NBX - 1)
            last = sp.value_load(nbt[0:1, 1:2], min_val=E - 1, max_val=NBX - 2)
            for k in range(8):
                sp.wait_ge(slot_free[k], 1)
                load_w1(k, w1[1, k * P:(k + 1) * P, :])
            with sp.Fori(1, last) as b:
                e = sp.value_load(etab[0:1, bass.ds(b + 1, 1)], min_val=0, max_val=E - 1)
                before = sp.value_load(etab[0:1, bass.ds(b, 1)], min_val=0, max_val=E - 1)
                load_w1_dyn(b + 1, e)
                load_w2_dyn(b, before)
            load_w2_dyn(last, sp.value_load(etab[0:1, bass.ds(last, 1)], min_val=0, max_val=E - 1))
            sp.wait_ge(sem("y_added"), nb * 16)
            for t in range(NT):
                sp.dma_start(hbuf[:, t, :], sum_rows[t * P:(t + 1) * P, :]).then_inc(sem(f"sum_in{t}"), 16)
            for t in range(NT):
                sp.wait_ge(sem("normed"), 3 * NT + t + 1)
                sp.dma_start(out[0, t * P:(t + 1) * P, :], hbuf[:, t, :]).then_inc(sem("out_done"), 16)
            sp.wait_ge(sem("out_done"), 16 * NT)

        @block.gpsimd
        def _(pool):
            gp = nc.gpsimd
            step = [0]

            def link(ins):
                step[0] += 1
                ins.then_inc(sem("pool_step"), 1)
                pool.wait_ge(sem("pool_step"), step[0])

            gp.memset(ones[:, :], 1.0)
            gp.memset(tri[:, :], 1.0)
            link(gp.memset(ident[:, :], 1.0))
            gp.affine_select(out=tri[:, :], in_=tri[:, :], compare_op=ALU.is_gt, fill=0.0, base=0,
                             pattern=[[1, P]], channel_multiplier=-1)
            gp.affine_select(out=ident[:, :], in_=ident[:, :], compare_op=ALU.is_equal, fill=0.0, base=0,
                             pattern=[[-1, P]], channel_multiplier=1).then_inc(sem("consts"), 1)
            wait_read(pool, "cT")
            pool.wait_ge(sem("s5_abar"), 1)
            ar = ab[:, 0, :].unsqueeze(2).to_broadcast([P, GI, N])
            ai = ab[:, 1, :].unsqueeze(2).to_broadcast([P, GI, N])

            def times_conj(o0, o1, v0, v1):
                gp.tensor_tensor(tv[0], v0, ar, ALU.mult)
                link(gp.tensor_tensor(tv[1], v1, ai, ALU.mult))
                link(gp.tensor_tensor(o0, tv[0], tv[1], ALU.add))
                gp.tensor_tensor(tv[0], v1, ar, ALU.mult)
                link(gp.tensor_tensor(tv[1], v0, ai, ALU.mult))
                link(gp.tensor_tensor(o1, tv[0], tv[1], ALU.subtract))

            times_conj(Vc[:, 0, :, 0, :], Vc[:, 1, :, 0, :], cpar[:, 0], cpar[:, 1])
            for k in range(1, L):
                times_conj(Vc[:, 0, :, k, :], Vc[:, 1, :, k, :], Vc[:, 0, :, k - 1, :], Vc[:, 1, :, k - 1, :])
            gp.memset(idle, 0.0).then_inc(sem("s5_v"), 1)
            pool.wait_ge(sem("u_out"), 16)
            link(gp.memset(Toe, 0.0))
            for q in range(8):
                wait_read(pool, f"KK{q}")
            link(gp.tensor_tensor(skip, ident[0:N, 0:N].unsqueeze(1).to_broadcast([N, G, N]),
                                  rowsT[0:N, 64:96].unsqueeze(2).to_broadcast([N, G, N]), ALU.mult))
            link(gp.tensor_tensor(KKs[:, :, 0:N], KKs[:, :, 0:N], skip, ALU.add))
            for i in range(L):
                gp.dma_start(Toe[i * N:(i + 1) * N, :, i * N:P], KKs[:, :, 0:P - i * N])\
                  .then_inc(sem("toe_shifted"), 16)
            pool.wait_ge(sem("toe_shifted"), 16 * L)
            gp.memset(X[:, :, :, 0], 0.0).then_inc(sem("toe_ready"), 1)
            wait_full(pool, "Z1.1")
            gp.memset(Sc, 0.0).then_inc(sem("scores_zero"), 1)
            wait_full(pool, "lg")
            link(gp.memset(Xg, 0.0))
            pool.wait_ge(sem("tables_ready"), 1)
            pool.wait_ge(sem("h2_out"), 16 * NT)
            last = pool.value_load(nbt[0:1, 1:2], min_val=E - 1, max_val=NBX - 2)

            last_token = pool.to_reg(T - 1)

            def gather():
                gp.indirect_dma_start(Xg, None, h2_rows, bass.IndirectOffsetOnAxis(ap=gix[:, 0:1].bitcast(U32), axis=0),
                                      bounds_check=last_token, oob_is_err=False).then_inc(sem("x_gathered"), 16)

            def indices(dst, table, b, n):
                gp.tensor_copy(dst[:, :], table[:, bass.ds(b, 1)]).then_inc(sem("pool_step"), 1)
                pool.wait_ge(sem("pool_step"), n)
                gp.tensor_tensor(idle, ones[:, 0:1], ones[:, 0:1], ALU.add)

            def scatter():
                gp.indirect_dma_start(sum_rows, bass.IndirectOffsetOnAxis(ap=six[:, 0:1].bitcast(U32), axis=0), ysb, None,
                                      compute_op=ALU.add).then_inc(sem("y_added"), 16)

            link(gp.tensor_copy(gix[:, :], gtab[:, 0:1]))
            gather()
            pool.wait_ge(sem("x_gathered"), 16)
            pool.wait_ge(sem("xt_full"), 1)
            link(gp.tensor_copy(gix[:, :], gtab[:, 1:2]))
            gather()
            pool.wait_ge(sem("x_gathered"), 32)
            pool.wait_ge(sem("xt_full"), 2)
            link(gp.tensor_copy(gix[:, :], gtab[:, 2:3]))
            gather()
            pool.wait_ge(sem("sum_out"), 16 * (NT + 1))
            pool.wait_ge(sem("y_copied"), 1)
            link(gp.tensor_copy(six[:, :], stab[:, 0:1]))
            scatter()
            base = step[0]
            with pool.Fori(1, last) as b:
                pool.wait_ge(sem("x_gathered"), 16 * b + 32)
                pool.wait_ge(sem("xt_full"), b + 2)
                indices(gix, gtab, b + 2, 2 * b + (base - 1))
                gather()
                pool.wait_ge(sem("y_copied"), b + 1)
                pool.wait_ge(sem("y_added"), 16 * b)
                indices(six, stab, b, 2 * b + base)
                scatter()
            pool.wait_ge(sem("y_copied"), last + 1)
            pool.wait_ge(sem("y_added"), 16 * last)
            indices(six, stab, last, 2 * last + (base - 1))
            scatter()

        @block.scalar
        def _(act):
            sc = nc.scalar
            step = [0]

            def link(ins):
                step[0] += 1
                ins.then_inc(sem("act_step"), 1)
                act.wait_ge(sem("act_step"), step[0])

            def ld(o, i, name="params"):
                act.dma_start(o, i).then_inc(sem(name), 16)

            ld(memx, mem.rearrange("(m p) d -> p m d", p=P), "mem_in")
            ld(rows[0:8, :], A["hgrn_lb_logits"].rearrange("r (h d) -> (r h) d", d=P))
            ld(rows[8:12, :], A["s5_b_glu"].rearrange("a (c d) -> (a c) d", d=P))
            ld(rows[12:16, :], A["s5_b_glu"].rearrange("a (c d) -> (a c) d", d=P))
            ld(dn.rearrange("g (i n) -> g i n", n=N),
               A["s5_d"][0].rearrange("(g n) -> g n", n=N).unsqueeze(1).to_broadcast([G, L, N]))
            for r, nm in enumerate(("s5_c_re", "s5_c_im")):
                for i in range(2):
                    ld(craw[:, r, i], A[nm][0].rearrange("(a i g) n p -> i (g n) a p", a=2, i=2)[i])
            ld(ngb, A["hgrn_norm_g"][0].partition_broadcast(P))
            ld(rbb, A["router_b"][0].partition_broadcast(P))

            def copy(dst, src):
                return sc.activation(dst, src, ACT.Copy)

            def evac(j, dst, src):
                wait_full(act, j)
                freed(j, copy(dst, src))

            def transposed_h(n, t):
                for h in range(2):
                    j = f"hT{n}.{t}.{h}"
                    evac(j, hT[:, 4 * h:4 * h + 4, t * P:(t + 1) * P], bank(j).rearrange("p (k n) -> p k n", k=4))

            def norm_weights(n, g, b):
                act.wait_ge(sem("normed"), NT * n)
                ld(lnw[:, 0, :], A[g][0].partition_broadcast(P), "ln_in")
                ld(lnw[:, 1, :], A[b][0].partition_broadcast(P), "ln_in")

            act.wait_ge(sem("var_ready"), NT)
            sc.activation(stat[:, 0:NT], stat[:, 0:NT], ACT.Sqrt).then_inc(sem("std_ready"), NT)
            for m in range(2):
                for h in range(2):
                    j = f"mT{m}.{h}"
                    evac(j, memT[:, 4 * h:4 * h + 4, m * P:(m + 1) * P], bank(j).rearrange("p (k n) -> p k n", k=4))
            for i in range(4):
                if i == 2:
                    wait_read(act, "par")
                    sc.activation(ab[:, 2, :], rowsT[:, 48:64], ACT.Exp).then_inc(sem("dt"), 1)
                j = f"K{i}"
                evac(j, kT[:, 2 * i:2 * i + 2, :], bank(j).rearrange("p (k n) -> p k n", k=2))
            for t in range(NT):
                if t == 1:
                    act.wait_ge(sem("angles"), 1)
                    sc.activation(ab[:, 3, :], ab[:, 3, :], ACT.Exp)
                    sc.activation(ab[:, 5, :], ab[:, 5, :], ACT.Sin)
                    sc.activation(ab[:, 6, :], ab[:, 6, :], ACT.Sin).then_inc(sem("sines"), 1)
                transposed_h(0, t)
                evac(f"V{t // 2}.{t % 2}", vm[:, t // 2, 512 * (t % 2):512 * (t % 2) + 512], bank(f"V{t // 2}.{t % 2}"))
            for t in range(NT):
                act.wait_ge(sem("normed"), t + 1)
                act.dma_start(h0_rows[t * P:(t + 1) * P, :], hbuf[:, t, :]).then_inc(sem("h0_out"), 16)
            norm_weights(1, "ln1_g", "ln1_b")
            for c in range(4):
                j = f"u{c}"
                evac(j, ucm[:, c, :].rearrange("p (j c) -> p c j", j=L), bank(j).rearrange("p (c j) -> p c j", j=L))
            wait_read(act, "u3")
            act.dma_start(u_rows.rearrange("(c p) t -> p c t", p=P), ucm).then_inc(sem("u_out"), 16)
            for r in range(2):
                for q in range(4):
                    j = f"W{r}.{q}"
                    evac(j, Wst[:, r, 4 * q:4 * q + 4, :], bank(j).rearrange("p (g m) -> p g m", g=4))
            act.wait_ge(sem("u_out"), 16)
            act.wait_ge(sem("h0_out"), 16 * NT)
            for j in range(L):
                act.dma_start(ug[j * N:(j + 1) * N], u_rows.rearrange("(g n) (j c) -> j n g c", n=N, j=L)[j])\
                   .then_inc(sem("u_in"), 16)
            for q in range(8):
                j = f"KK{q}"
                evac(j, KKs[:, 4 * q:4 * q + 4, :], bank(j)[0:N, :].rearrange("p (g m) -> p g m", g=4))
            act.wait_ge(sem("lb_logits"), 1)
            sc.activation(lbx[:, 0:8], lbx[:, 0:8], ACT.Exp).then_inc(sem("lb_exp"), 1)
            act.wait_ge(sem("s5_v"), 1)
            for h in range(4):
                j = f"f{h}"
                wait_full(act, j)
                freed(j, sc.activation(kh[:, h * T:(h + 1) * T], bank(j), ACT.Sigmoid))
            act.wait_ge(sem("f_ready"), 4)
            sc.activation(P1, cum, ACT.Ln).then_inc(sem("logf_ready"), 1)
            for r in range(2):
                for h in range(2):
                    j = f"Z{r}.{h}"
                    evac(j, X[:, r, 8 * h:8 * h + 8, 1:NC + 1], bank(j).rearrange("p (g c) -> p g c", g=8))
            for h in range(4):
                j = f"q{h}"
                evac(j, qh[:, h * T:(h + 1) * T], bank(j))
            for c in range(4):
                j = f"Y{c}"
                wait_full(act, j)
                freed(j, sc.activation(Ys[:, 8 * c:8 * c + 8, :], bank(j).rearrange("p (g c) -> p g c", g=8),
                                       ACT.Gelu_apprx_tanh))
            wait_read(act, "Y3")
            for j in range(L):
                act.dma_start(s5_rows.rearrange("(g n) (j c) -> j n g c", n=N, j=L)[j], Ys[j * N:(j + 1) * N])\
                   .then_inc(sem("s5_out"), 16)

            def decay(n):
                act.wait_ge(sem("diff_ready"), n + 1)
                buf = P0 if n % 2 == 0 else P1
                sc.activation(buf, buf, ACT.Exp).then_inc(sem("decay_ready"), 1)

            def between(j):
                c = int(j[1])
                if j[0] == "i":
                    evac(j, vh[:, c, :], bank(j))
                elif j[0] == "g":
                    wait_full(act, j)
                    sc.activation(gs[:, c, :], bank(j), ACT.Sigmoid).then_inc(sem("sig_g"), 1)
                else:
                    wait_full(act, j)
                    freed(j, sc.activation(s5g[:, c, :], bank(j), ACT.Sigmoid, bias=rowsT[:, 8 + c:9 + c]))

            decay(0)
            decay(1)
            act.wait_ge(sem("s5_out"), 16 * L)
            act.dma_start(ycm, s5_rows.rearrange("(c p) t -> p c t", p=P)).then_inc(sem("s5_in"), 16)
            for n in range(len(LEVELS)):
                for j in BETWEEN[n]:
                    between(j)
                if n + 2 < len(LEVELS):
                    decay(n + 2)
            sc.activation(qe, cum, ACT.Exp).then_inc(sem("qe_exp"), 1)
            sc.activation(el, cum.rearrange("p (b s) -> p b s", s=P)[:, :, P - 1], ACT.Exp).then_inc(sem("el_ready"), 1)
            act.wait_ge(sem("diff_ready"), len(LEVELS) + 1)
            sc.activation(P1, P1, ACT.Exp).then_inc(sem("decay_ready"), 1)
            for j in BETWEEN[-1]:
                between(j)
            for t in range(NT):
                j = f"kd{t}"
                evac(j, kdT[:, t], bank(j).rearrange("p (h d) -> p h d", h=NH))
            for t in range(NT):
                act.dma_start(hbuf[:, t, :], h0_rows[t * P:(t + 1) * P, :]).then_inc(sem("h0_in"), 16)
            for t in range(NT + 1):
                if t < NT:
                    j = f"o{t}"
                    wait_full(act, j)
                    for h in range(NH):
                        ins = sc.activation(sq[:, h * P:(h + 1) * P], bank(j)[:, h * P:(h + 1) * P], ACT.Square,
                                            accum_out=rms[:, 4 * t + h:4 * t + h + 1])
                    ins.then_inc(sem("ms_ready"), 1)
                    act.wait_ge(sem("ms_eps"), t + 1)
                    sc.activation(rms[:, 16 + 4 * t:20 + 4 * t], rms[:, 16 + 4 * t:20 + 4 * t], ACT.Sqrt)\
                      .then_inc(sem("rms_ready"), 1)
                if t:
                    j = f"oaT{t - 1}"
                    evac(j, hT[:, 0:4, (t - 1) * P:t * P], bank(j).rearrange("p (k n) -> p k n", k=4))

            def roots_and_transposes(n):
                for t in range(NT + 1):
                    if t < NT:
                        act.wait_ge(sem("var_ready"), NT * n + t + 1)
                        sc.activation(stat[:, t:t + 1], stat[:, t:t + 1], ACT.Sqrt).then_inc(sem("std_ready"), 1)
                    if t:
                        transposed_h(n, t - 1)

            wait_full(act, f"oaT{NT - 1}")
            ld(b1raw, A["exp_b1"][0].rearrange("e (f p) -> (e f) p", p=P).rearrange("(q r) p -> r q p", q=4), "late_in")
            ld(rw, A["router_w"][0].rearrange("(k p) e -> p k e", p=P), "late_in")
            roots_and_transposes(1)
            norm_weights(2, "ln2_g", "ln2_b")
            for c in range(8):
                j = f"aq{c}"
                wait_full(act, j)
                freed(j, copy(qT[:, c, :], bank(j)))
            for t in range(NT + 1):
                if t < NT:
                    for h in range(2):
                        j = f"sc{t}.{h}"
                        act.wait_ge(sem("max_ready"), 2 * t + h + 1)
                        if t >= 2 and h == 0:
                            wait_full(act, f"PT{t - 2}.1")
                        for i in range(2):
                            hh = 2 * h + i
                            ins = sc.activation(Pb[:, t % 2, hh, :], bank(j)[:, M * i:M * i + M], ACT.Exp, scale=SCALE,
                                                bias=amax[:, 4 * t + hh:4 * t + hh + 1],
                                                accum_out=asum[:, 4 * t + hh:4 * t + hh + 1])
                        ins.then_inc(sem("exp_ready"), 1)
                if t:
                    for m in range(2):
                        j = f"PT{t - 1}.{m}"
                        wait_full(act, j)
                        freed(j, copy(PT[:, m, :, (t - 1) * P:t * P], bank(j).rearrange("p (h n) -> p h n", h=NH)))
            for c in range(8):
                j = f"ao{c}"
                wait_full(act, j)
                freed(j, copy(hT[:, c, :], bank(j)))
            ld(b2sb, A["exp_b2"][0], "b2_in")
            evac("b1T", b1T[:, :], bank("b1T"))
            roots_and_transposes(2)
            norm_weights(3, "ln3_g", "ln3_b")
            act.wait_ge(sem("top_ready"), 1)
            ins = None
            for t in range(NT):
                ins = sc.activation(gate[:, t, :], topv[:, 8 * t:8 * t + 4], ACT.Exp,
                                    bias=ntop[:, t:t + 1], accum_out=gsum[:, t:t + 1])
            ins.then_inc(sem("gate_exp"), 1)
            act.wait_ge(sem("tables_ready"), 1)
            last = act.value_load(nbt[0:1, 1:2], min_val=E - 1, max_val=NBX - 2)

            def transposed_rows():
                sc.activation(xT[:, 0:4, :], ps[:, 6, 0:4 * CAP].rearrange("p (k s) -> p k s", k=4), ACT.Copy)
                sc.activation(xT[:, 4:8, :], ps[:, 7, 0:4 * CAP].rearrange("p (k s) -> p k s", k=4), ACT.Copy)\
                  .then_inc(sem("xt_copied"), 1)

            def sigmoids():
                sc.activation(sig, glu, ACT.Sigmoid, scale=SW_ALPHA).then_inc(sem("sig_ready"), 1)

            def result_rows(b):
                for h in range(2):
                    ins = sc.activation(ysb[:, 512 * h:512 * h + 512], ps[0:CAP, 4 + h, :], ACT.Copy,
                                        scale=wtab[:, bass.ds(b, 1)])
                ins.then_inc(sem("y_copied"), 1)

            def w2_high(b):
                for q in range(4):
                    act.wait_ge(slot_full[8 + q], 16 * b + 16)
                    sc.activation(w2_hi[q][:, :], ring[:, 8 + q, :], ACT.Copy).then_inc(sem("w2_high"), 1)

            for b in range(2):
                act.wait_ge(sem("xt_full"), b + 1)
                transposed_rows()
            act.wait_ge(sem("glu_ready"), 1)
            sigmoids()
            wait_full(act, "wtab")
            w2_high(0)
            act.wait_ge(sem("xt_full"), 3)
            transposed_rows()
            act.wait_ge(sem("glu_ready"), 2)
            act.wait_ge(sem("act_ready"), 1)
            sigmoids()
            act.wait_ge(slot_free[11], 1)
            wait_read(act, "wtab")
            result_rows(0)
            with act.Fori(1, last) as b:
                w2_high(b)
                act.wait_ge(sem("xt_full"), b + 3)
                transposed_rows()
                act.wait_ge(sem("glu_ready"), b + 2)
                act.wait_ge(sem("act_ready"), b + 1)
                sigmoids()
                act.wait_ge(slot_free[11], b + 1)
                act.wait_ge(sem("y_added"), 16 * b)
                result_rows(b)
            w2_high(last)
            act.wait_ge(slot_free[11], last + 1)
            act.wait_ge(sem("y_added"), 16 * last)
            result_rows(last)
            for t in range(NT):
                act.wait_ge(sem("var_ready"), NT * 3 + t + 1)
                sc.activation(stat[:, t:t + 1], stat[:, t:t + 1], ACT.Sqrt).then_inc(sem("std_ready"), 1)

        @block.vector
        def _(v):
            ve = nc.vector
            step, steps = [0], ["dve_step"]

            def link(ins):
                step[0] += 1
                ins.then_inc(sem(steps[0]), 1)
                v.wait_ge(sem(steps[0]), step[0])

            def stats(n, t):
                link(ve.bn_stats(mvs[:, 0:6], hbuf[:, t, 0:512]))
                link(ve.bn_stats(mvs[:, 6:12], hbuf[:, t, 512:1024]))
                link(ve.bn_aggr(mv[:, 2 * t:2 * t + 2], mvs))
                ve.tensor_scalar(stat[:, t:t + 1], mv[:, 2 * t + 1:2 * t + 2], LN_EPS, None, ALU.add).then_inc(sem("var_ready"), 1)
                v.wait_ge(sem("var_ready"), NT * n + t + 1)

            def normalise(n, t):
                v.wait_ge(sem("std_ready"), NT * n + t + 1)
                link(ve.reciprocal(stat[:, 4 + t:5 + t], stat[:, t:t + 1]))
                link(ve.scalar_tensor_tensor(out=hbuf[:, t, :], in0=hbuf[:, t, :], scalar=mv[:, 2 * t:2 * t + 1],
                                             in1=lnw[:, 0, :], op0=ALU.subtract, op1=ALU.mult))
                ve.scalar_tensor_tensor(out=hbuf[:, t, :], in0=hbuf[:, t, :], scalar=stat[:, 4 + t:5 + t],
                                        in1=lnw[:, 1, :], op0=ALU.mult, op1=ALU.add).then_inc(sem("normed"), 1)
                v.wait_ge(sem("normed"), NT * n + t + 1)

            v.wait_ge(sem("consts"), 1)
            for t in range(NT):
                v.wait_ge(sem(f"x_in{t}"), 16)
                stats(0, t)
            v.wait_ge(sem("ln_in"), 32)
            for t in range(NT):
                normalise(0, t)

            wait_full(v, "par")
            freed("par", ve.tensor_copy(rowsT, bank("par")[:, 0:96]))
            wait_read(v, "par")
            wait_full(v, "cT")
            ct = bank("cT").rearrange("p (r i m) -> p r i m", r=2, i=2)
            ve.tensor_copy(cpar[:, 0].rearrange("p (i g) n -> p i (g n)", i=2), ct[:, 0])
            freed("cT", ve.tensor_scalar(cpar[:, 1].rearrange("p (i g) n -> p i (g n)", i=2), ct[:, 1], -1.0, None,
                                         ALU.mult))
            lamr, lami = rowsT[:, 16:32], rowsT[:, 32:48]
            v.wait_ge(sem("dt"), 1)
            link(ve.tensor_tensor(ab[:, 3, :], lamr, ab[:, 2, :], ALU.mult))
            link(ve.tensor_tensor(ab[:, 4, :], lami, ab[:, 2, :], ALU.mult))
            link(ve.tensor_scalar(ab[:, 7, :], ab[:, 4, :], 1.0 / TWO_PI, None, ALU.mult))
            link(ve.tensor_scalar(ab[:, 7, :], ab[:, 7, :], MAGIC, None, ALU.add))
            link(ve.tensor_scalar(ab[:, 7, :], ab[:, 7, :], MAGIC, None, ALU.subtract))
            for part in (TP1, TP2, TP3):
                link(ve.scalar_tensor_tensor(out=ab[:, 4, :], in0=ab[:, 7, :], scalar=-part, in1=ab[:, 4, :],
                                             op0=ALU.mult, op1=ALU.add))
            sine, cosine = ab[:, 5, :], ab[:, 6, :]
            link(ve.tensor_scalar(ab[:, 5, :], ab[:, 4, :], -PI_BELOW, PI_BELOW, ALU.max, ALU.min))
            ve.tensor_scalar(ab[:, 6, :], ab[:, 5, :], 0.5, None, ALU.mult).then_inc(sem("angles"), 1)
            v.wait_ge(sem("sines"), 1)
            link(ve.tensor_tensor(ab[:, 6, :], ab[:, 6, :], ab[:, 6, :], ALU.mult))
            link(ve.tensor_scalar(ab[:, 6, :], ab[:, 6, :], -2.0, 1.0, ALU.mult, ALU.add))
            link(ve.tensor_tensor(ab[:, 0, :], ab[:, 3, :], ab[:, 6, :], ALU.mult))
            ve.tensor_tensor(ab[:, 1, :], ab[:, 3, :], ab[:, 5, :], ALU.mult).then_inc(sem("s5_abar"), 1)
            v.wait_ge(sem("s5_abar"), 1)
            nr, cr, ci, den, w = (ab[:, 8 + i, :] for i in range(5))
            link(ve.tensor_scalar(nr, ab[:, 0, :], -1.0, None, ALU.add))
            link(ve.tensor_tensor(den, lamr, lamr, ALU.mult))
            link(ve.tensor_tensor(w, lami, lami, ALU.mult))
            link(ve.tensor_tensor(den, den, w, ALU.add))
            link(ve.reciprocal(den, den))
            link(ve.tensor_tensor(cr, nr, lamr, ALU.mult))
            link(ve.tensor_tensor(w, ab[:, 1, :], lami, ALU.mult))
            link(ve.tensor_tensor(cr, cr, w, ALU.add))
            link(ve.tensor_tensor(cr, cr, den, ALU.mult))
            link(ve.tensor_tensor(ci, ab[:, 1, :], lamr, ALU.mult))
            link(ve.tensor_tensor(w, nr, lami, ALU.mult))
            link(ve.tensor_tensor(ci, ci, w, ALU.subtract))
            link(ve.tensor_tensor(ci, ci, den, ALU.mult))

            def times(o0, o1, a0, a1, b0, b1, t, done=None):
                ve.tensor_tensor(t[0], b0, a0, ALU.mult)
                link(ve.tensor_tensor(t[1], b1, a1, ALU.mult))
                link(ve.tensor_tensor(o0, t[0], t[1], ALU.subtract))
                ve.tensor_tensor(t[0], b1, a0, ALU.mult)
                link(ve.tensor_tensor(t[1], b0, a1, ALU.mult))
                ins = ve.tensor_tensor(o1, t[0], t[1], ALU.add)
                if done:
                    ins.then_inc(sem(done), 1)
                    v.wait_ge(sem(done), 1)
                else:
                    link(ins)

            def wide(a):
                return a.unsqueeze(2).to_broadcast([P, GI, N])

            times(bbar[:, 0], bbar[:, 1], wide(cr), wide(ci), braw[:, 0], braw[:, 1], tq)
            ve.tensor_copy(Qb[:, 0, :, L - 1, :], bbar[:, 0])
            link(ve.tensor_copy(Qb[:, 1, :, L - 1, :], bbar[:, 1]))
            for j in range(L - 2, -1, -1):
                times(Qb[:, 0, :, j, :], Qb[:, 1, :, j, :], wide(ab[:, 0, :]), wide(ab[:, 1, :]),
                      Qb[:, 0, :, j + 1, :], Qb[:, 1, :, j + 1, :], tq, None if j else "q_ready")
            lg = rowsT[:, 0:8]
            link(ve.tensor_tensor(lbx[:, 8:12], lg[:, 0:4], lg[:, 4:8], ALU.max))
            ve.tensor_tensor(lbx[:, 0:8].rearrange("p (r h) -> p r h", r=2), lg.rearrange("p (r h) -> p r h", r=2),
                             lbx[:, 8:12].unsqueeze(1).to_broadcast([P, 2, NH]), ALU.subtract)\
              .then_inc(sem("lb_logits"), 1)
            v.wait_ge(sem("lb_exp"), 1)
            link(ve.tensor_tensor(lbx[:, 8:12], lbx[:, 0:4], lbx[:, 4:8], ALU.add))
            link(ve.reciprocal(lbx[:, 8:12], lbx[:, 8:12]))
            link(ve.tensor_tensor(lb[:, 0:4], lbx[:, 0:4], lbx[:, 8:12], ALU.mult))
            link(ve.tensor_scalar(lb[:, 4:8], lb[:, 0:4], -1.0, 1.0, ALU.mult, ALU.add))

            col = masktmp[:, 0:P]
            row = masktmp[:, P:2 * P]
            t0, t1, t2 = masktmp[:, 256:384], masktmp[:, 384:512], masktmp[:, 512:640]
            link(ve.tensor_tensor_scan(col, ones[:, :], ones[:, :], -1.0, ALU.mult, ALU.add))
            link(ve.tensor_tensor(t0, col, ident[:, :], ALU.mult))
            link(ve.tensor_reduce(row[:, 0:1], t0, AX.X, ALU.add))
            link(ve.tensor_copy(masks[:, 0, :], ident[:, :]))
            coli, rowi = masktmp[:, 640:768].bitcast(I32), masktmp[:, 768:769].bitcast(I32)
            rowb = masktmp[:, 896:1024].bitcast(I32)
            xr = masktmp[:, 1024:1152].bitcast(I32)
            link(ve.tensor_copy(coli, col))
            link(ve.tensor_copy(rowb, row[:, 0:1].to_broadcast([P, P])))
            link(ve.tensor_tensor(xr, coli, rowb, ALU.bitwise_xor))
            link(ve.tensor_copy(t0, xr))
            for n, hs in enumerate(LEVELS):
                link(ve.tensor_scalar(t1, t0, float(hs), None, ALU.is_ge))
                link(ve.tensor_scalar(t2, t0, float(2 * hs), None, ALU.is_lt))
                link(ve.tensor_tensor(t1, t1, t2, ALU.mult))
                link(ve.tensor_tensor(masks[:, n + 1, :], t1, tri[:, :], ALU.mult))

            for m, x in ((13, ab[:, 3, :]), (13, ab[:, 13, :]), (13, ab[:, 13, :])):
                link(ve.tensor_tensor(ab[:, m, :], x, x, ALU.mult))
            t2_ = [ab[:, 19, :], ab[:, 20, :]]
            times(ab[:, 14, :], ab[:, 15, :], cosine, sine, cosine, sine, t2_)
            times(ab[:, 16, :], ab[:, 17, :], ab[:, 14, :], ab[:, 15, :], ab[:, 14, :], ab[:, 15, :], t2_)
            times(turn[:, 0, :, 0], turn[:, 1, :, 0], ab[:, 16, :], ab[:, 17, :], ab[:, 16, :], ab[:, 17, :], t2_)
            wait_full(v, "W1.3")
            n = 1
            while n < NC:
                far = [turn[:, r, :, n - 1:n].to_broadcast([P, GI, n]) for r in range(2)]
                times(turn[:, 0, :, n:2 * n], turn[:, 1, :, n:2 * n], turn[:, 0, :, 0:n], turn[:, 1, :, 0:n],
                      far[0], far[1], [t[:, 0:GI * n].rearrange("p (g c) -> p g c", g=GI) for t in t3[0:2]])
                n *= 2

            for h in range(4):
                wait_read(v, f"f{h}")
                if h == 0:
                    v.wait_ge(sem("toe_shifted"), 16 * L)
                s = slice(h * T, (h + 1) * T)
                link(ve.tensor_scalar(cum[:, s], kh[:, s], lb[:, 4 + h:5 + h], lb[:, h:h + 1], ALU.mult, ALU.add))
                ve.tensor_scalar(kh[:, s], cum[:, s], -1.0, 1.0, ALU.mult, ALU.add).then_inc(sem("f_ready"), 1)
            v.wait_ge(sem("logf_ready"), 1)
            for i in range(16):
                s = slice(i * P, (i + 1) * P)
                ins = ve.tensor_tensor_scan(cum[:, s], ones[:, :], P1[:, s], 0.0, ALU.mult, ALU.add)
            ins.then_inc(sem("cum_ready"), 1)
            v.wait_ge(sem("cum_ready"), 1)

            for r in range(2):
                for h in range(2):
                    wait_read(v, f"Z{r}.{h}")
            v.wait_ge(sem("toe_ready"), 1)
            Zr, Zi = X[:, 0, :, 1:NC + 1], X[:, 1, :, 1:NC + 1]
            u0, u1, u2 = (t.rearrange("p (g c) -> p g c", g=GI) for t in t3)
            co, si = turn[:, 0], turn[:, 1]

            def turned(sign):
                ve.tensor_tensor(u0, Zr, co, ALU.mult)
                ve.tensor_tensor(u1, Zi, si, ALU.mult)
                link(ve.tensor_tensor(u2, Zr, si, ALU.mult))
                link(ve.tensor_tensor(Zr, u0, u1, ALU.subtract if sign > 0 else ALU.add))
                link(ve.tensor_tensor(u0, Zi, co, ALU.mult))
                return ve.tensor_tensor(Zi, u0, u2, ALU.add if sign > 0 else ALU.subtract)

            link(turned(-1))
            for r in range(2):
                for g in range(GI):
                    z = X[:, r, g, 1:NC + 1]
                    ins = ve.tensor_tensor_scan(z, ab[:, 13, g:g + 1].to_broadcast([P, NC]), z, 0.0, ALU.mult, ALU.add)
            link(ins)
            turned(1).then_inc(sem("x_ready"), 1)

            def gates(t):
                v.wait_ge(sem("sig_g"), t + 1)
                j = f"g{t}"
                wait_full(v, j)
                link(ve.tensor_tensor(gs[:, t, :], gs[:, t, :], bank(j), ALU.mult))
                freed(j, ve.tensor_tensor(gs[:, t, :].rearrange("p (h e) -> p h e", h=NH),
                                          gs[:, t, :].rearrange("p (h e) -> p h e", h=NH),
                                          ngb.unsqueeze(1).to_broadcast([P, NH, P]), ALU.mult))

            def halves(a, hs):
                return a.rearrange("p (b w s) -> p b w s", w=2, s=hs)

            def diff(n):
                hs = LEVELS[n]
                buf = P0 if n % 2 == 0 else P1
                if n >= 2:
                    for t in range(NT):
                        wait_full(v, f"s{n - 1}.{t}")
                c4, d4 = halves(cum, hs), halves(buf, hs)
                ref = c4[:, :, 0, hs - 1:hs].to_broadcast([P, 2048 // (2 * hs), hs])
                ve.tensor_tensor(d4[:, :, 1, :], c4[:, :, 1, :], ref, ALU.subtract)
                ve.tensor_tensor(d4[:, :, 0, :], ref, c4[:, :, 0, :], ALU.subtract).then_inc(sem("diff_ready"), 1)

            def weigh(n):
                hs = LEVELS[n]
                buf = P0 if n % 2 == 0 else P1
                v.wait_ge(sem("decay_ready"), n + 1)
                d4, q4, k4 = halves(buf, hs), halves(qh, hs), halves(kh, hs)
                ve.tensor_tensor(d4[:, :, 1, :], d4[:, :, 1, :], q4[:, :, 1, :], ALU.mult)
                ve.tensor_tensor(d4[:, :, 0, :], d4[:, :, 0, :], k4[:, :, 0, :], ALU.mult).then_inc(sem("pair_ready"), 1)

            def place(n):
                for t in range(NT):
                    j = f"s{n}.{t}"
                    wait_full(v, j)
                    if n:
                        wait_read(v, f"s{n - 1}.{t}")
                    freed(j, ve.copy_predicated(Sc[:, t], masks[:, n, :].unsqueeze(1).to_broadcast([P, NH, P]),
                                                bank(j).rearrange("p (h s) -> p h s", h=NH)))

            diff(0)
            diff(1)
            for j in ("q0", "q1", "q2", "q3"):
                wait_read(v, j)
            v.wait_ge(sem("scores_zero"), 1)
            weigh(0)
            place(0)
            for n in range(1, len(LEVELS)):
                if n + 1 < len(LEVELS):
                    diff(n + 1)
                weigh(n)
                place(n)
                if n == len(LEVELS) - 2:
                    v.wait_ge(sem("s5_in"), 16)
                    for c in range(4):
                        wait_read(v, f"z{c}")
                        ve.tensor_tensor(s5T[:, c, :].rearrange("p (c j) -> p j c", j=L),
                                         s5g[:, c, :].rearrange("p (j c) -> p j c", j=L),
                                         ycm[:, c, :].rearrange("p (j c) -> p j c", j=L), ALU.mult)\
                          .then_inc(sem("glu_done"), 1)
            v.wait_ge(sem("qe_exp"), 1)
            ve.tensor_tensor(qe, qe, qh, ALU.mult).then_inc(sem("qe_ready"), 1)
            for t in range(NT):
                wait_full(v, f"s{len(LEVELS) - 1}.{t}")
            c3 = cum.rearrange("p (b s) -> p b s", s=P)
            ve.tensor_tensor(P1.rearrange("p (b s) -> p b s", s=P), c3[:, :, P - 1:P].to_broadcast([P, 16, P]), c3,
                             ALU.subtract).then_inc(sem("diff_ready"), 1)
            v.wait_ge(sem("decay_ready"), len(LEVELS) + 1)
            ve.tensor_tensor(P1, P1, kh, ALU.mult).then_inc(sem("kdec_ready"), 1)
            place(len(LEVELS))
            for t in range(NT):
                gates(t)
            v.wait_ge(sem("el_ready"), 1)
            for t in range(NT):
                if t < NT - 1:
                    j = f"st{t}"
                    wait_full(v, j)
                    for h in range(NH):
                        if t == 0:
                            ins = ve.tensor_copy(st[:, h, :], bank(j)[:, h * P:(h + 1) * P])
                        else:
                            ins = ve.scalar_tensor_tensor(out=st[:, h, :], in0=st[:, h, :],
                                                          scalar=el[:, 4 * h + t:4 * h + t + 1],
                                                          in1=bank(j)[:, h * P:(h + 1) * P], op0=ALU.mult, op1=ALU.add)
                    freed(j, ins)
                v.wait_ge(sem("ms_ready"), t + 1)
                a, b_ = rms[:, 4 * t:4 * t + 4], rms[:, 16 + 4 * t:20 + 4 * t]
                ve.tensor_scalar(b_, a, 1.0 / P, RMS_EPS, ALU.mult, ALU.add).then_inc(sem("ms_eps"), 1)
                v.wait_ge(sem("rms_ready"), t + 1)
                link(ve.reciprocal(a, b_))
                j = f"o{t}"
                for h in range(NH):
                    s = slice(h * P, (h + 1) * P)
                    ins = ve.scalar_tensor_tensor(out=oa[:, t, s], in0=bank(j)[:, s], scalar=rms[:, 4 * t + h:4 * t + h + 1],
                                                  in1=gs[:, t, s], op0=ALU.mult, op1=ALU.mult)
                freed(j, ins)

            def residual(n, name):
                for t in range(NT):
                    for h in range(2):
                        j = f"{name}{t}.{h}"
                        wait_full(v, j)
                        s = slice(512 * h, 512 * h + 512)
                        ins = ve.scalar_tensor_tensor(out=hbuf[:, t, s], in0=hbuf[:, t, s], scalar=ALPHA, in1=bank(j),
                                                      op0=ALU.mult, op1=ALU.add)
                        freed(j, ins)
                        wait_read(v, j)
                    stats(n, t)
                    normalise(n, t)

            v.wait_ge(sem("h0_in"), 16 * NT)
            v.wait_ge(sem("ln_in"), 64)
            residual(1, "w")
            for t in range(NT):
                for h in range(2):
                    j = f"sc{t}.{h}"
                    wait_full(v, j)
                    m2 = amax[:, 4 * t + 2 * h:4 * t + 2 * h + 2]
                    link(ve.tensor_reduce(m2, bank(j).rearrange("p (i m) -> p i m", i=2), AX.X, ALU.max))
                    ve.tensor_scalar(m2, m2, -SCALE, None, ALU.mult).then_inc(sem("max_ready"), 1)
                for h in range(2):
                    j = f"sc{t}.{h}"
                    v.wait_ge(sem("exp_ready"), 2 * t + h + 1)
                    s2 = asum[:, 4 * t + 2 * h:4 * t + 2 * h + 2]
                    freed(j, ve.reciprocal(s2, s2))
                    wait_read(v, j)
                    for i in range(2):
                        hh = 2 * h + i
                        ins = ve.tensor_scalar(Pb[:, t % 2, hh, :], Pb[:, t % 2, hh, :],
                                               asum[:, 4 * t + hh:4 * t + hh + 1], None, ALU.mult)
                    ins.then_inc(sem("probs_ready"), 1)
            v.wait_ge(sem("ln_in"), 96)
            residual(2, "wo")

            lgs = rt[:, 0:128].rearrange("p (t e) -> p t e", t=NT)
            OH = rt[:, 128:640].rearrange("p (i e) -> p i e", i=16)
            tmp = rt[:, 896:1408].rearrange("p (i e) -> p i e", i=16)
            pos = rt[:, 1408:1536].rearrange("p (t e) -> p t e", t=NT)
            cnt, nov, ovi, ovs = (rt[:, 1536 + 32 * i:1568 + 32 * i] for i in range(4))
            ix = rt[:, 1664:1696].bitcast(U32).rearrange("p (t k) -> p t k", t=NT)
            ixf = rt[:, 1696:1712]
            qq = rt[:, 1712:1840].rearrange("p (t e) -> p t e", t=NT)
            bl = rt[:, 1840:1968].rearrange("p (t e) -> p t e", t=NT)
            slk, blk = rt[:, 1968:1984], rt[:, 1984:2000]
            iof = rt[:, 2000:2000 + P]
            av = rt[:, 2128:2144]
            NX = NBX - E
            cmp_ = rt[0:1, 2144:2144 + NX * E].rearrange("p (b e) -> p b e", e=E)
            tabf = rt[0:CAP, 2944:2944 + NBX]
            etf = rt[0:1, 3008:3008 + NBX]
            prow = rt[:, 3072:3073]
            topi = rt[:, 3080:3112].bitcast(U32)
            wsl = rt[:, 3120:3136]
            empty = rt[0:CAP, 3200:3200 + NBX]
            assert NX * E <= 800 and NBX <= 64
            diag = tmp[:, 0:4, :].rearrange("p i e -> p (i e)")
            link(ve.tensor_tensor_scan(iof, ones[:, :], ones[:, :], -1.0, ALU.mult, ALU.add))
            link(ve.tensor_tensor(diag, iof, ident[:, :], ALU.mult))
            link(ve.tensor_reduce(prow, diag, AX.X, ALU.add))
            for t in range(NT):
                ve.tensor_scalar(av[:, 4 * t:4 * t + 4], prow.to_broadcast([P, TOPK]), float(P * t + 1), None, ALU.add)
            wait_full(v, "lg")
            freed("lg", ve.tensor_tensor(lgs, bank("lg")[:, 0:128].rearrange("p (t e) -> p t e", t=NT),
                                         rbb.unsqueeze(1).to_broadcast([P, NT, E]), ALU.add))
            wait_read(v, "lg")
            for t in range(NT):
                link(ve.max(topv[:, 8 * t:8 * t + 8], lgs[:, t, :]))
                link(ve.max_index(topi[:, 8 * t:8 * t + 8], topv[:, 8 * t:8 * t + 8], lgs[:, t, :]))
            tv3 = topv.rearrange("p (t k) -> p t k", t=NT)
            ve.tensor_scalar(ntop, tv3[:, :, 0], -1.0, None, ALU.mult).then_inc(sem("top_ready"), 1)
            link(ve.tensor_copy(ixf.rearrange("p (t k) -> p t k", t=NT),
                                topi.rearrange("p (t k) -> p t k", t=NT)[:, :, 0:TOPK]))
            link(ve.tensor_tensor(OH, iof[:, 0:E].unsqueeze(1).to_broadcast([P, 16, E]),
                                  ixf.unsqueeze(2).to_broadcast([P, 16, E]), ALU.is_equal))

            def over_choices(o, a):
                return ve.tensor_reduce(o, a.rearrange("p (t k) e -> p t e k", t=NT), AX.X, ALU.add)

            over_choices(Msk, OH).then_inc(sem("chosen"), 1)
            v.wait_ge(sem("gate_exp"), 1)
            link(ve.reciprocal(gsum, gsum))
            link(ve.tensor_tensor(gate, gate, gsum.unsqueeze(2).to_broadcast([P, NT, TOPK]), ALU.mult))
            link(ve.tensor_tensor(tmp, OH, gate.rearrange("p t k -> p (t k)").unsqueeze(2).to_broadcast([P, 16, E]),
                                  ALU.mult))
            over_choices(Gt, tmp).then_inc(sem("gates_ready"), 1)
            wait_full(v, "pos")
            link(ve.tensor_copy(pos, bank("pos")[:, 0:128].rearrange("p (t e) -> p t e", t=NT)))
            freed("pos", ve.tensor_copy(cnt, bank("pos")[:, 128:160]))
            wait_read(v, "pos")
            wait_full(v, "GT")
            freed("GT", ve.tensor_copy(GTs, bank("GT")[0:E, :]))
            link(ve.tensor_scalar(nov, cnt, float(CAP), None, ALU.is_gt))
            for m in range(2, QMAX + 1):
                link(ve.scalar_tensor_tensor(out=nov, in0=cnt, scalar=float(m * CAP), in1=nov, op0=ALU.is_gt, op1=ALU.add))
            link(ve.tensor_tensor_scan(ovi, ones[:, 0:E], nov, 0.0, ALU.mult, ALU.add))
            link(ve.tensor_tensor(ovs, ovi, nov, ALU.subtract))
            link(ve.tensor_scalar(nbt[:, 0:1], ovi[0:1, E - 1:E], float(E), None, ALU.add))
            link(ve.tensor_scalar(nbt[:, 1:2], ovi[0:1, E - 1:E], float(E - 1), None, ALU.add))
            link(ve.tensor_scalar(qq, pos, float(CAP), None, ALU.is_ge))
            z = tmp[:, 0:4, :]
            link(ve.tensor_copy(z, qq))
            for m in range(2, QMAX + 1):
                link(ve.scalar_tensor_tensor(out=qq, in0=pos, scalar=float(m * CAP), in1=qq, op0=ALU.is_ge, op1=ALU.add))
            link(ve.scalar_tensor_tensor(out=pos, in0=qq, scalar=-float(CAP), in1=pos, op0=ALU.mult, op1=ALU.add))
            e4 = iof[:, 0:E].unsqueeze(1).to_broadcast([P, NT, E])
            link(ve.tensor_tensor(bl, qq, ovs.unsqueeze(1).to_broadcast([P, NT, E]), ALU.add))
            link(ve.tensor_tensor(bl, bl, e4, ALU.subtract))
            link(ve.scalar_tensor_tensor(out=bl, in0=bl, scalar=float(E - 1), in1=z, op0=ALU.add, op1=ALU.mult))
            link(ve.tensor_tensor(bl, bl, e4, ALU.add))

            def at_choice(o, a):
                o4 = OH.rearrange("p (t k) e -> p t k e", t=NT)
                t4 = tmp.rearrange("p (t k) e -> p t k e", t=NT)
                for t in range(NT):
                    ins = ve.tensor_tensor(t4[:, t], o4[:, t], a[:, t:t + 1, :].to_broadcast([P, TOPK, E]), ALU.mult)
                link(ins)
                link(ve.tensor_reduce(o, tmp, AX.X, ALU.add))

            at_choice(slk, pos)
            at_choice(blk, bl)
            link(ve.tensor_tensor(Aoh, iof[:, 0:CAP].unsqueeze(1).to_broadcast([P, 16, CAP]),
                                  slk.unsqueeze(2).to_broadcast([P, 16, CAP]), ALU.is_equal))
            ve.tensor_tensor(Boh, iof[:, 0:NBX].unsqueeze(1).to_broadcast([P, 16, NBX]),
                             blk.unsqueeze(2).to_broadcast([P, 16, NBX]), ALU.is_equal)
            ve.tensor_tensor(Atok, Aoh, av.unsqueeze(2).to_broadcast([P, 16, CAP]), ALU.mult).then_inc(sem("onehots"), 1)
            link(ve.tensor_tensor(cmp_, ovi[0:1, :].unsqueeze(1).to_broadcast([1, NX, E]),
                                  iof[0:1, 0:NX].unsqueeze(2).to_broadcast([1, NX, E]), ALU.is_le))
            link(ve.tensor_reduce(etf[:, E:NBX], cmp_, AX.X, ALU.add))
            link(ve.tensor_copy(etf[:, 0:E], iof[0:1, 0:E]))
            link(ve.tensor_scalar(etab[:, :], etf, float(E - 1), None, ALU.min))
            wait_full(v, "tab")
            freed("tab", ve.tensor_scalar(tabf, bank("tab")[0:CAP, 0:NBX], -1.0, None, ALU.add))
            wait_read(v, "tab")
            ve.tensor_copy(gtab[:, :], tabf).then_inc(sem("tables_ready"), 1)
            ve.tensor_tensor(Aoh, Aoh, gate.rearrange("p t k -> p (t k)").unsqueeze(2).to_broadcast([P, 16, CAP]),
                             ALU.mult).then_inc(sem("gated_onehots"), 1)
            link(ve.tensor_scalar(empty, tabf, 0.0, None, ALU.is_lt))
            link(ve.tensor_scalar(prow, prow, float(T + 1), None, ALU.add))
            link(ve.scalar_tensor_tensor(out=tabf, in0=empty, scalar=prow[0:CAP], in1=tabf, op0=ALU.mult, op1=ALU.add))
            link(ve.tensor_copy(stab[:, :], tabf))
            v.wait_ge(sem("h2_out"), 16 * NT)
            for t in range(NT):
                for h in range(2):
                    j = f"gb{t}.{h}"
                    wait_full(v, j)
                    s = slice(512 * h, 512 * h + 512)
                    ins = ve.scalar_tensor_tensor(out=hbuf[:, t, s], in0=hbuf[:, t, s], scalar=ALPHA, in1=bank(j),
                                                  op0=ALU.mult, op1=ALU.add)
                    freed(j, ins)
            wait_full(v, "wtab")
            freed("wtab", ve.tensor_copy(wtab[:, :], bank("wtab")[0:CAP, 0:NBX]))

            hh4 = ps[:, 0:4, 0:4 * CAP]
            g4 = glu.rearrange("p (b f s) -> p b f s", b=2, f=4)
            l4 = lin.rearrange("p (b f s) -> p b f s", b=2, f=4)
            wait_read(v, "b1T")
            last = v.value_load(nbt[0:1, 1:2], min_val=E - 1, max_val=NBX - 2)
            base = step[0]

            def swiglu(b, e, steps):
                n = [0]

                def link(ins):
                    n[0] += 1
                    ins.then_inc(sem("dve_step"), 1)
                    v.wait_ge(sem("dve_step"), steps + n[0])

                def bias(o):
                    return b1T[:, bass.ds(e * 16 + o, 8)].rearrange("p (b f) -> p b f", b=2).unsqueeze(3)

                v.wait_ge(slot_free[7], b + 1)
                for i in range(2):
                    ins = ve.tensor_tensor(g4[:, i], ps[:, i, 0:4 * CAP].rearrange("p (f s) -> p f s", f=4),
                                           bias(0)[:, i].to_broadcast([P, 4, CAP]), ALU.add)
                link(ins)
                ve.tensor_scalar(glu, glu, LIMIT, None, ALU.min).then_inc(sem("glu_ready"), 1)
                for i in range(2):
                    ins = ve.tensor_tensor(l4[:, i], ps[:, 2 + i, 0:4 * CAP].rearrange("p (f s) -> p f s", f=4),
                                           bias(8)[:, i].to_broadcast([P, 4, CAP]), ALU.add)
                ins.then_inc(sem("h_read"), 1)
                v.wait_ge(sem("h_read"), b + 1)
                link(ve.tensor_scalar(lin, lin, LIMIT, -LIMIT, ALU.min, ALU.max))
                link(ve.scalar_tensor_tensor(out=lin, in0=lin, scalar=1.0, in1=glu, op0=ALU.add, op1=ALU.mult))
                v.wait_ge(sem("sig_ready"), b + 1)
                if not (isinstance(b, int) and b == 0):
                    v.wait_ge(slot_free[11], b)
                link(ve.tensor_tensor(act_, lin, sig, ALU.mult))
                link(ve.tensor_copy(act_hi[:, :], act_))
                ve.tensor_tensor(act_lo[:, :], act_, act_hi[:, :].bitcast(F32), ALU.subtract)\
                  .then_inc(sem("act_ready"), 1)
                return n[0]

            def w2_rest(b):
                for q in range(4):
                    v.wait_ge(sem("w2_high"), 4 * b + (q + 1))
                    ve.tensor_tensor(w2_lo[q][:, :], ring[:, 8 + q, :], w2_hi[q][:, :].bitcast(F32), ALU.subtract)\
                      .then_inc(sem("w2_split"), 1)

            per = swiglu(0, 0, base)
            w2_rest(0)
            e = v.value_load(etab[0:1, 1:2], min_val=0, max_val=E - 1)
            swiglu(1, e, base + per)
            with v.Fori(1, last) as b:
                w2_rest(b)
                e = v.value_load(etab[0:1, bass.ds(b + 1, 1)], min_val=0, max_val=E - 1)
                swiglu(b + 1, e, (base + per) + per * b)
            w2_rest(last)
            step[0], steps[0] = 0, "last_step"
            v.wait_ge(sem("ln_in"), 128)
            for t in range(NT):
                v.wait_ge(sem(f"sum_in{t}"), 16)
                stats(3, t)
                normalise(3, t)

        @block.tensor
        def _(pe):
            te = nc.tensor

            def job(name):
                b, use = JOBS[name]
                if use > 1:
                    pe.wait_ge(bank_free[b], use - 1)
                return bank(name)

            def full(name, ins):
                ins.then_inc(bank_full[JOBS[name][0]], 1)

            def mm(o, l, r, start, stop):
                return te.matmul(o, l, r, start=start, stop=stop)

            def tr(o, i, k=P):
                return te.transpose(o, i, ident[0:k, 0:k])

            def weights(w, i):
                s, use = SLOT_OF[w, i]
                pe.wait_ge(slot_full[s], 16 * use)
                return ring[:, s, :].rearrange("p (k n) -> p k n", n=D if w[0] == "w" else HW)

            pe.wait_ge(sem("consts"), 1)
            def transpose_h(n, t):
                pe.wait_ge(sem("normed"), NT * n + t + 1)
                for h in range(2):
                    nm = f"hT{n}.{t}.{h}"
                    o = job(nm)
                    for k in range(4):
                        ins = tr(o[:, k * P:(k + 1) * P], hbuf[:, t, (4 * h + k) * P:(4 * h + k + 1) * P])
                    full(nm, ins)

            pe.wait_ge(sem("mem_in"), 16)
            for m in range(2):
                for h in range(2):
                    nm = f"mT{m}.{h}"
                    o = job(nm)
                    for k in range(4):
                        ins = tr(o[:, k * P:(k + 1) * P], memx[:, m, (4 * h + k) * P:(4 * h + k + 1) * P])
                    full(nm, ins)
            for m in range(2):
                for h in range(2):
                    wait_read(pe, f"mT{m}.{h}")

            def keys(i):
                nm = f"K{i}"
                o = job(nm)
                for c in range(2):
                    for k in range(KD):
                        w = weights("wk", k // 2)
                        ins = mm(o[:, c * M:(c + 1) * M], w[:, k % 2, (2 * i + c) * P:(2 * i + c + 1) * P], memT[:, k, :],
                                 k == 0, k == KD - 1)
                full(nm, ins)

            keys(0)
            keys(1)
            pe.wait_ge(sem("params"), 16 * PARAMS)
            o = job("par")
            tr(o[:, 0:16], rows, 16)
            for i in range(3):
                tr(o[:, 16 + 16 * i:32 + 16 * i], lam_in[:, i * P:(i + 1) * P], 16)
            full("par", tr(o[:, 64:96], dn, 32))
            o = job("cT")
            for r in range(2):
                for i in range(2):
                    ins = tr(o[:, (2 * r + i) * P:(2 * r + i + 1) * P], craw[:, r, i].rearrange("p a m -> p (a m)"))
            full("cT", ins)

            keys(2)
            keys(3)
            for t in range(NT):
                transpose_h(0, t)
                m, h = t // 2, t % 2
                nm = f"V{m}.{h}"
                o = job(nm)
                for k in range(KD):
                    w = weights("wv", k // 2)
                    ins = mm(o, memT[:, k, m * P:(m + 1) * P], w[:, k % 2, 512 * h:512 * h + 512], k == 0, k == KD - 1)
                full(nm, ins)

            def channels(w0, c):
                nm = f"{w0}{c}"
                o = job(nm)
                for k in range(KD):
                    w = weights(w0, k // 4)
                    ins = mm(o, w[:, k % 4, c * P:(c + 1) * P], hT[:, k, :], k == 0, k == KD - 1)
                full(nm, ins)

            def tokens(w0, t):
                nm = f"{w0}{t}"
                o = job(nm)
                for k in range(KD):
                    w = weights(w0, k // 4)
                    ins = mm(o, hT[:, k, t * P:(t + 1) * P], w[:, k % 4, :], k == 0, k == KD - 1)
                full(nm, ins)

            for t in range(NT):
                for h in range(2):
                    wait_read(pe, f"hT0.{t}.{h}")
            for c in range(4):
                channels("u", c)
            pe.wait_ge(sem("q_ready"), 1)
            for r in range(2):
                for q in range(4):
                    nm = f"W{r}.{q}"
                    o = job(nm)
                    for i in range(4):
                        ins = tr(o[:, i * P:(i + 1) * P], Qb[:, r, 4 * q + i].rearrange("p j n -> p (j n)"))
                    full(nm, ins)
            pe.wait_ge(sem("s5_v"), 1)
            for q in range(8):
                nm = f"KK{q}"
                o = job(nm)
                for i in range(4):
                    g = 4 * q + i
                    b0, gi = PST * (g // GI), g % GI
                    rws = slice(b0, b0 + PST)
                    for c0, c1, w in ((0, N, None), (N, P, 1)):
                        for r in range(2):
                            rhs = cpar[rws, r, gi, :] if w is None else \
                                Vc[rws, r, gi, 0:L - 1, :].rearrange("p k n -> p (k n)")
                            ins = mm(o[0:N, i * P + c0:i * P + c1], bbar[rws, r, gi, :], rhs, r == 0, r == 1)
                full(nm, ins)
            for h in range(NH):
                channels("f", h)
            pe.wait_ge(sem("u_in"), 16 * L)
            for q in range(4):
                wait_read(pe, f"W0.{q}")
                wait_read(pe, f"W1.{q}")
            for r in range(2):
                for h in range(2):
                    nm = f"Z{r}.{h}"
                    o = job(nm)
                    for i in range(8):
                        for a in range(2):
                            gi = 8 * h + i
                            ins = mm(o[PST * a:PST * (a + 1), i * NC:(i + 1) * NC], Wst[:, r, gi, PST * a:PST * (a + 1)],
                                     ug[:, GI * a + gi, :], True, True)
                    full(nm, ins)
            for h in range(NH):
                channels("q", h)
            pe.wait_ge(sem("toe_ready"), 1)
            pe.wait_ge(sem("x_ready"), 1)
            for c in range(4):
                nm = f"Y{c}"
                o = job(nm)
                for i in range(8):
                    g = 8 * c + i
                    b0, gi = PST * (g // GI), g % GI
                    oo = o[:, i * NC:(i + 1) * NC]
                    mm(oo, Toe[:, g, :], ug[:, g, :], True, False)
                    for r in range(2):
                        ins = mm(oo, Vc[b0:b0 + PST, r, gi].rearrange("p k n -> p (k n)"), X[b0:b0 + PST, r, gi, 0:NC],
                                 False, r == 1)
                full(nm, ins)

            def between(j):
                c = int(j[1])
                if j[0] != "z":
                    return tokens(j[0], c)
                pe.wait_ge(sem("s5_in"), 16)
                o = job(j)
                w = weights("glu", 0)
                for k in range(4):
                    ins = mm(o, w[:, k, c * P:(c + 1) * P], ycm[:, k, :], k == 0, k == 3)
                full(j, ins)

            for n in range(len(LEVELS) + 1):
                if n == 0:
                    pe.wait_ge(sem("f_ready"), 4)
                    for h in range(4):
                        wait_read(pe, f"q{h}")
                    lt, rh = kh, qh
                else:
                    pe.wait_ge(sem("pair_ready"), n)
                    lt = rh = P0 if (n - 1) % 2 == 0 else P1
                for t in range(NT):
                    nm = f"s{n}.{t}"
                    o = job(nm)
                    for h in range(NH):
                        s = slice(h * T + t * P, h * T + (t + 1) * P)
                        ins = mm(o[:, h * P:(h + 1) * P], lt[:, s], rh[:, s], True, True)
                    full(nm, ins)
                for j in BETWEEN[n]:
                    between(j)
            pe.wait_ge(sem("kdec_ready"), 1)
            for t in range(NT):
                nm = f"kd{t}"
                o = job(nm)
                for h in range(NH):
                    s = slice(h * T + t * P, h * T + (t + 1) * P)
                    ins = tr(o[:, h * P:(h + 1) * P], P1[:, s])
                full(nm, ins)
            pe.wait_ge(sem("qe_ready"), 1)

            def transpose_oa(t):
                nm = f"oaT{t}"
                wait_read(pe, f"o{t}")
                o = job(nm)
                for c in range(4):
                    ins = tr(o[:, c * P:(c + 1) * P], oa[:, t, c * P:(c + 1) * P])
                full(nm, ins)

            for t in range(NT):
                wait_read(pe, f"s{len(LEVELS)}.{t}")
                wait_read(pe, f"kd{t}")
                if t:
                    wait_read(pe, f"st{t - 1}")
                nm = f"o{t}"
                o = job(nm)
                for h in range(NH):
                    oo = o[:, h * P:(h + 1) * P]
                    ins = mm(oo, Sc[:, t, h, :], vh[:, t, h * P:(h + 1) * P], True, t == 0)
                    if t:
                        ins = mm(oo, qe[:, h * T + t * P:h * T + (t + 1) * P], st[:, h, :], False, True)
                full(nm, ins)
                if t < NT - 1:
                    nm = f"st{t}"
                    o = job(nm)
                    for h in range(NH):
                        ins = mm(o[:, h * P:(h + 1) * P], kdT[:, t, h, :], vh[:, t, h * P:(h + 1) * P], True, True)
                    full(nm, ins)
                if t:
                    transpose_oa(t - 1)
            transpose_oa(NT - 1)

            def project(nm0, w0, n, left):
                for t in range(NT):
                    for h in range(2):
                        nm = f"{nm0}{t}.{h}"
                        o = job(nm)
                        for k in range(KD):
                            w = weights(w0, k // 2)
                            ins = mm(o, left(k, t), w[:, k % 2, 512 * h:512 * h + 512], k == 0, k == KD - 1)
                        full(nm, ins)
                    if t:
                        transpose_h(n, t - 1)
                transpose_h(n, NT - 1)

            for t in range(NT):
                wait_read(pe, f"oaT{t}")
            pe.wait_ge(sem("glu_done"), 4)
            project("w", "wout", 1, lambda k, t: hT[:, k, t * P:(t + 1) * P] if k < 4 else
                    s5T[:, k - 4, t * P:(t + 1) * P])
            for t in range(NT):
                for h in range(2):
                    wait_read(pe, f"hT1.{t}.{h}")
            for c in range(8):
                nm = f"aq{c}"
                o = job(nm)
                for k in range(KD):
                    w = weights("wq", k // 2)
                    ins = mm(o, w[:, k % 2, c * P:(c + 1) * P], hT[:, k, :], k == 0, k == KD - 1)
                full(nm, ins)
            for c in range(8):
                wait_read(pe, f"aq{c}")

            for t in range(NT + 1):
                if t < NT:
                    for h in range(2):
                        nm = f"sc{t}.{h}"
                        o = job(nm)
                        for i in range(2):
                            for kk in range(2):
                                c = 2 * (2 * h + i) + kk
                                ins = mm(o[:, i * M:(i + 1) * M], qT[:, c, t * P:(t + 1) * P], kT[:, c, :],
                                         kk == 0, kk == 1)
                        full(nm, ins)
                if t:
                    pe.wait_ge(sem("probs_ready"), 2 * t)
                    for m in range(2):
                        nm = f"PT{t - 1}.{m}"
                        o = job(nm)
                        for hh in range(NH):
                            ins = tr(o[:, hh * P:(hh + 1) * P], Pb[:, (t - 1) % 2, hh, m * P:(m + 1) * P])
                        full(nm, ins)
            for t in range(NT):
                for m in range(2):
                    wait_read(pe, f"PT{t}.{m}")
            for c in range(8):
                nm = f"ao{c}"
                o = job(nm)
                for m in range(2):
                    ins = mm(o, vm[:, m, c * P:(c + 1) * P], PT[:, m, c // 2, :], m == 0, m == 1)
                full(nm, ins)
            pe.wait_ge(sem("late_in"), 32)
            o = job("b1T")
            for q in range(4):
                ins = tr(o[:, q * P:(q + 1) * P], b1raw[:, q, :])
            full("b1T", ins)
            for c in range(8):
                wait_read(pe, f"ao{c}")
            project("wo", "wo", 2, lambda k, t: hT[:, k, t * P:(t + 1) * P])
            for t in range(NT):
                for h in range(2):
                    wait_read(pe, f"hT2.{t}.{h}")
            o = job("lg")
            for t in range(NT):
                for k in range(KD):
                    ins = mm(o[:, t * E:(t + 1) * E], hT[:, k, t * P:(t + 1) * P], rw[:, k, :], k == 0, k == KD - 1)
            full("lg", ins)
            pe.wait_ge(sem("chosen"), 1)
            o = job("pos")
            for t in range(NT):
                for i in range(t + 1):
                    mm(o[:, t * E:(t + 1) * E], (tri if i == t else ones)[:, :], Msk[:, i, :], i == 0, i == t)
            for i in range(NT):
                ins = mm(o[:, NT * E:NT * E + E], ones[:, :], Msk[:, i, :], i == 0, i == NT - 1)
            full("pos", ins)
            pe.wait_ge(sem("gates_ready"), 1)
            o = job("GT")
            for t in range(NT):
                ins = mm(o[0:E, t * P:(t + 1) * P], Gt[:, t, :], ident[:, :], True, True)
            full("GT", ins)
            wait_read(pe, "GT")
            pe.wait_ge(sem("b2_in"), 16)

            def bias_sums(t):
                for h in range(2):
                    nm = f"gb{t}.{h}"
                    o = job(nm)
                    full(nm, mm(o, GTs[:, t * P:(t + 1) * P], b2sb[:, 512 * h:512 * h + 512], True, True))

            def slot_table(nm, left):
                o = job(nm)
                for i in range(16):
                    ins = mm(o[0:CAP, 0:NBX], left[:, i, :], Boh[:, i, :], i == 0, i == 15)
                full(nm, ins)

            bias_sums(0)
            bias_sums(1)
            pe.wait_ge(sem("onehots"), 1)
            slot_table("tab", Atok)
            bias_sums(2)
            bias_sums(3)
            pe.wait_ge(sem("gated_onehots"), 1)
            slot_table("wtab", Aoh)
            pe.wait_ge(sem("tables_ready"), 1)
            last = pe.value_load(nbt[0:1, 1:2], min_val=E - 1, max_val=NBX - 2)
            for b_ in range(8):
                pe.wait_ge(bank_free[b_], sum(bb == b_ for bb, _ in JOBS.values()))

            def rows_in(b):
                pe.wait_ge(sem("x_gathered"), 16 * b + 16)
                for k in range(KD):
                    ins = tr(ps[:, 6 + k // 4, (k % 4) * CAP:(k % 4 + 1) * CAP], Xg[:, k * P:(k + 1) * P], CAP)
                ins.then_inc(sem("xt_full"), 1)

            def first(b):
                pe.wait_ge(sem("xt_copied"), b + 1)
                if not (isinstance(b, int) and b == 0):
                    pe.wait_ge(sem("h_read"), b)
                for k in range(KD):
                    pe.wait_ge(slot_full[k], 16 * b + 16 * (USES[k] + 1))
                    for f in range(16):
                        ins = te.matmul(ps[:, f // 4, (f % 4) * CAP:(f % 4 + 1) * CAP],
                                        ring[:, k, f * P:(f + 1) * P], xT[:, k, :],
                                        start=(k == 0 and f % 4 == 0), stop=(k == KD - 1), skip_group_check=True)
                    ins.then_inc(slot_free[k], 1)

            def second(b):
                pe.wait_ge(sem("act_ready"), b + 1)
                if not (isinstance(b, int) and b == 0):
                    pe.wait_ge(sem("y_copied"), b)
                for k in range(KD):
                    q = k // 2
                    if k % 2 == 0:
                        pe.wait_ge(sem("w2_split"), 4 * b + (q + 1))
                    for h in range(2):
                        c = slice((k % 2) * D + 512 * h, (k % 2) * D + 512 * h + 512)
                        a = slice(k * CAP, (k + 1) * CAP)
                        y = ps[0:CAP, 4 + h, :]
                        te.matmul(y, act_hi[:, a], w2_hi[q][:, c], start=(k == 0), stop=False)
                        te.matmul(y, act_hi[:, a], w2_lo[q][:, c], start=False, stop=False)
                        ins = te.matmul(y, act_lo[:, a], w2_hi[q][:, c], start=False, stop=(k == KD - 1))
                    if k % 2 == 1:
                        ins.then_inc(slot_free[8 + q], 1)

            rows_in(0)
            first(0)
            rows_in(1)
            first(1)
            rows_in(2)
            second(0)
            with pe.Fori(1, last) as b:
                first(b + 1)
                rows_in(b + 2)
                second(b)
            second(last)


def kernel(**inputs):
    import concourse.bacc as _bacc
    from concourse.bass_utils import run_bass_kernel_spmd as _run

    nc = _bacc.Bacc("TRN2", target_bir_lowering=False, num_devices=1)
    arrays, aps = {}, {}
    for name, value in inputs.items():
        a = np.ascontiguousarray(value)
        arrays[f"in_{name}"] = a
        aps[name] = nc.dram_tensor(f"in_{name}", a.shape, mybir.dt.from_np(a.dtype), kind="ExternalInput").ap()
    out = nc.dram_tensor("out_rows", (1, T, D), F32, kind="ExternalOutput").ap()
    trunk_layer(nc, aps, out)
    r = _run(nc, [arrays], core_ids=[0])
    return r.results[0]["out_rows"]
```

```python
import numpy as np
import concourse.bass as bass
from concourse import mybir
from concourse.alu_op_type import AluOpType as ALU

ACT = mybir.ActivationFunctionType
AX = mybir.AxisListType
F32, I32, U32, U8 = mybir.dt.float32, mybir.dt.int32, mybir.dt.uint32, mybir.dt.uint8
F32R = mybir.dt.float32r

P = 128
D = 1024
T = 512
NT = T // P
KD = D // P
HW = 512
NH = 4
G, PST, N = 32, 64, 16
GI = G // 2
L = 8
NC = T // L
M = 256
XD = 256
SCALE = XD ** -0.5
E, TOPK = 32, 4
CAP = 96
QMAX = (T - 1) // CAP
NBX = E + (T * TOPK) // (CAP + 1) + 1 + 2
LIMIT, SW_ALPHA = 7.0, 1.702
ALPHA = 2.0 ** 0.25
LN_EPS, RMS_EPS = 1e-5, 1e-6
MAGIC = 12582912.0
TWO_PI = 6.283185307179586
TP1 = 6.28125
TP2 = float(np.float32(0.0019353071))
TP3 = float(TWO_PI - TP1 - TP2)
PI_BELOW = 3.1415925
LN2, LN2_HIGH, LN2_REST = 0.6931471805599453, 0.693359375, -2.121944400546905e-4

RING, SLOT = 12, 2048
PRE = 5
COLS = {"q": 0, "f": HW, "i": 2 * HW, "g": 3 * HW, "u": 4 * HW}
STREAM = ([("wk", i) for i in range(4)] + [("wv", 0)]
          + [(w, i) for w in ("u", "f", "q", "i") for i in range(2)] + [("glu", 0)]
          + [("g", i) for i in range(2)] + [("wout", i) for i in range(4)]
          + [("wq_high", 3)] + [("wo", i) for i in range(4)])
SLOT_OF = {w: (n % PRE, n // PRE + 1) for n, w in enumerate(STREAM)}
LOADS = [sum(n % PRE == s and STREAM[n][0] != "wq_high" for n in range(len(STREAM))) for s in range(8)]
LAST_JOB = {"u": "u3", "wk": "K3", "wv": "V1.1", "glu": "z3", "f": "f3", "q": "q3", "i": "i3", "g": "g3",
            "wout": "w3.1", "wq_high": "aq1.3", "wo": "wo3.1"}

PARAMS = 17
LEVELS = [64, 32, 16, 8, 4, 2, 1]
BETWEEN = [["i0"], ["i1"], ["i2"], ["z0", "z1"], ["z2", "z3"], ["i3"], ["g0"], ["g1", "g2", "g3"]]
GATED_BIASES = [f"gb{t}.{h}" for t in range(NT) for h in range(2)]


def job_order():
    j = [f"mT{m}.{h}" for m in range(2) for h in range(2)] + ["K0", "K1", "par", "cT", "K2", "K3"]
    for t in range(NT):
        j += [f"hT0.{t}.{h}" for h in range(2)] + [f"V{t // 2}.{t % 2}"]
    j += [f"u{c}" for c in range(4)]
    j += [f"W{r}.{q}" for r in range(2) for q in range(4)]
    j += [f"KK{q}" for q in range(8)]
    j += [f"f{h}" for h in range(4)] + [f"Z{r}.{h}" for r in range(2) for h in range(2)] + [f"q{h}" for h in range(4)]
    j += [f"Y{c}" for c in range(4)]
    for n in range(len(LEVELS) + 1):
        j += [f"s{n}.{t}" for t in range(NT)] + BETWEEN[n]
    j += [f"kd{t}" for t in range(NT)]
    for t in range(NT):
        j += [f"o{t}"] + ([f"st{t}"] if t < NT - 1 else [])
        if t:
            j += [f"oaT{t - 1}"]
    j += [f"oaT{NT - 1}"]
    for t in range(NT):
        j += [f"w{t}.{h}" for h in range(2)]
        if t:
            j += [f"hT1.{t - 1}.{h}" for h in range(2)]
    j += [f"aq0.{c}" for c in range(4)] + [f"hT1.{NT - 1}.{h}" for h in range(2)] + [f"aq1.{c}" for c in range(4)]
    for t in range(NT):
        j += [f"sc{t}.{h}" for h in range(2)]
        if t:
            j += [f"PT{t - 1}.{h}" for h in range(2)]
    j += [f"PT{NT - 1}.{h}" for h in range(2)]
    j += [f"ao{c}" for c in range(8)] + ["b1T"]
    for t in range(NT):
        j += [f"wo{t}.{h}" for h in range(2)]
        if t:
            j += [f"hT2.{t - 1}.{h}" for h in range(2)]
        if t > 1:
            j += [f"lg{t - 2}"]
    j += [f"hT2.{NT - 1}.{h}" for h in range(2)] + [f"lg{NT - 2}", f"lg{NT - 1}", "pos", "GT"]
    return j + ["tab"] + GATED_BIASES

JOBS = {name: (n % 8, n // 8 + 1) for n, name in enumerate(job_order())}


def trunk_layer(nc, A, out):
    x, mem = A["x"][0], A["mem"][0]
    w_in, w_out, w_glu = A["w_in"][0], A["w_out"][0], A["s5_w_glu"][0]
    w1, w2 = A["exp_w1"][0], A["exp_w2"][0]

    def rows_in_dram(name, n, width):
        return nc.dram_tensor(name, [n, width], F32, kind="Internal").ap()

    h0_rows = rows_in_dram("h0_rows", T, D)
    h2_rows = rows_in_dram("h2_rows", T, D)
    sum_rows = rows_in_dram("sum_rows", T + CAP, D)
    u_rows = rows_in_dram("u_rows", HW, T)
    s5_rows = rows_in_dram("s5_rows", HW, T)

    place = {}

    def sb(name, shape, dt=F32):
        place[name] = (nc.sbuf_base + 31) // 32 * 32
        return nc.alloc_sbuf_tensor(name, shape, dt)

    def float32r_view(name, of, at, n):
        return nc.alloc_sbuf_tensor_at(name, [P, n], F32R, offset=place[of] + 4 * at)

    ring = sb("ring", [P, RING, SLOT])
    hbuf = sb("hbuf", [P, NT, D])
    hT = sb("hT", [P, KD, T])
    lnw = sb("lnw", [P, 2, D])
    kv = sb("kv", [P, 4096])
    ident = sb("ident", [P, P])
    tri = sb("tri", [P, P])
    ones = sb("ones", [P, P])
    masks = sb("masks", [P, len(LEVELS) + 1, P], U8)
    b1T = sb("b1T", [P, E * 16])
    C = sb("arena_c", [P, 11392])
    small = sb("small", [P, 1280])

    def flat(t, a, n):
        return t[:, a:a + n]

    B_ = hbuf[:, :, :].rearrange("p t d -> p (t d)")

    W_ = [ring[:, PRE + i, :] for i in range(RING - PRE)]
    W34, W56 = (ring[:, PRE + i:PRE + i + 2, :].rearrange("p s n -> p (s n)") for i in (3, 5))
    W12 = ring[:, PRE + 1:PRE + 3, :].rearrange("p s n -> p (s n)")
    memx = W_[3].rearrange("p (m d) -> p m d", m=2)
    memT = W_[4].rearrange("p (k m) -> p k m", k=KD)
    wv_rest = {1: PRE + 1, 2: PRE + 2, 3: PRE + 6}
    Wst = W34.rearrange("p (r g m) -> p r g m", r=2, g=GI)
    ucm = W_[5].rearrange("p (c t) -> p c t", c=4)
    Toe = W56.rearrange("p (g m) -> p g m", g=G)
    Vc = flat(C, 0, 4096).rearrange("p (r g k n) -> p r g k n", r=2, g=GI, k=L)
    Qb = flat(C, 4096, 4096).rearrange("p (r g k n) -> p r g k n", r=2, g=GI, k=L)
    X = flat(C, 6144, 2 * GI * (NC + 1)).rearrange("p (r g c) -> p r g c", r=2, g=GI)
    turn = W_[0].rearrange("p (r g c) -> p r g c", r=2, g=GI)
    t3 = [flat(C, 4096 + 1024 * i, 1024) for i in range(2)] + [flat(C, 10368, 1024)]
    KKs = W12[0:N, :].rearrange("p (g m) -> p g m", g=G)
    ug = B_[:, 0:2048].rearrange("p (g c) -> p g c", g=G)
    Ys = flat(C, 4096, 2048).rearrange("p (g c) -> p g c", g=G)
    ycm = W_[5].rearrange("p (c t) -> p c t", c=4)
    s5g = flat(C, 4096, 2048).rearrange("p (c t) -> p c t", c=4)
    s5T = W_[6].rearrange("p (c t) -> p c t", c=4)
    kT = flat(kv, 0, 2048).rearrange("p (c m) -> p c m", c=KD)
    vm = flat(kv, 2048, 2048).rearrange("p (m d) -> p m d", m=2)
    cum, qh, P0, P1 = W_[1], W_[2], W_[3], B_[:, 2048:4096]
    kh = flat(C, 8256, 2048)
    Sc = W_[4].rearrange("p (t h s) -> p t h s", t=NT, h=NH)
    vh = flat(C, 0, 2048).rearrange("p (t e) -> p t e", t=NT)
    gs = flat(C, 2048, 2048).rearrange("p (t e) -> p t e", t=NT)
    qe = flat(C, 6144, 2048)
    oa = flat(C, 4096, 2048).rearrange("p (t e) -> p t e", t=NT)
    st = flat(C, 10368, 512).rearrange("p (h e) -> p h e", h=NH)
    sq = flat(C, 10880, 512)
    kdT = cum.rearrange("p (t h d) -> p t h d", t=NT, h=NH)
    qT = flat(C, 0, 4096).rearrange("p (c t) -> p c t", c=KD)
    Pb = flat(C, 4096, 2048).rearrange("p (b h m) -> p b h m", b=2, h=NH)
    PT = flat(C, 6144, 4096).rearrange("p (m h t) -> p m h t", m=2, h=NH)
    WQ = [PRE, PRE + 1, PRE + 2, PRE + 5]
    wq_lo = [float32r_view(f"wq_rest{i}", "ring", SLOT * WQ[i], SLOT) for i in range(4)]
    wq_hi = [float32r_view(f"wq_high{i}", "arena_c", 4096 + SLOT * i, SLOT) for i in range(3)] + \
            [float32r_view("wq_high3", "ring", SLOT * SLOT_OF["wq_high", 3][0], SLOT)]
    wo_lo = [float32r_view(f"wo_rest{i}", "ring", SLOT * SLOT_OF["wo", i][0], SLOT) for i in range(4)]
    wo_hi = wq_lo
    hT_hi = float32r_view("hT_high", "hT", 0, KD * T)
    hT_lo = float32r_view("hT_rest", "ring", SLOT * (PRE + 3), KD * T)
    Aoh = flat(kv, 2304, 16 * CAP).rearrange("p (i s) -> p i s", i=16)
    Boh = flat(C, 5888, 16 * NBX).rearrange("p (i s) -> p i s", i=16)
    Btg = flat(C, 1792, 32 * NBX).rearrange("p (i s) -> p i s", i=16)
    gsc = hT[:, :, :].rearrange("p k t -> p (k t)").rearrange("p (t d) -> p t d", t=NT)
    Xg = C[0:CAP, 0:D]
    xT = flat(C, 1024, KD * CAP).rearrange("p (k s) -> p k s", k=KD)
    glu = flat(C, 1792, KD * CAP)
    lin = flat(C, 2560, KD * CAP)
    sig = flat(C, 3328, KD * CAP)
    act_ = flat(C, 4096, KD * CAP)
    act_hi = float32r_view("act_high", "arena_c", 5888, KD * CAP)
    act_lo = float32r_view("act_rest", "arena_c", 6720, KD * CAP)
    w2_hi = [float32r_view(f"w2_high{i}", "hT" if i < 2 else "kv", SLOT * (i % 2), SLOT) for i in range(4)]
    w2_lo = [float32r_view(f"w2_rest{i}", "ring", SLOT * (8 + i), SLOT) for i in range(4)]
    ysb = C[0:CAP, 4864:4864 + D]
    rt = C[:, 6912:11392]
    b1raw = flat(C, 10368, 512).rearrange("p (q f) -> p q f", q=4)
    b2sb = kv[0:E, 512:512 + D]
    GTs = kv[0:E, 1792:2304]
    sofar = rt[:, 3296:3456].rearrange("p (t e) -> p t e", t=NT + 1)
    Msk = rt[:, 640:768].rearrange("p (t e) -> p t e", t=NT)
    Gt = rt[:, 768:896].rearrange("p (t e) -> p t e", t=NT)
    rw = flat(C, 10880, KD * E).rearrange("p (k e) -> p k e", k=KD)

    at = [0]

    def sm(n, parts=P):
        a = at[0]
        at[0] += n
        assert at[0] <= 1280
        return small[0:parts, a:a + n]

    rows = b1T[0:16, 0:128]
    lam_in = b1T[0:GI, 128:512]
    dn = sm(128, G)
    rowsT = sm(96)
    ab = sm(16 * 24).rearrange("p (n g) -> p n g", g=GI)
    lb = sm(8)
    lbx = sm(12)
    rms = sm(32)
    amax, asum = sm(16), sm(16)
    mvs = sm(12)
    topv = sm(32)
    ntop, gsum = sm(4), sm(4)
    ngb = sm(128)
    stat = sm(16)
    mv = sm(8)
    el = sm(16)
    gate = sm(16).rearrange("p (t k) -> p t k", t=NT)
    rbb = sm(32)
    idle = sm(1)
    gix, six = nc.alloc_sbuf_tensor("gix", [CAP, 1], I32), nc.alloc_sbuf_tensor("six", [CAP, 1], I32)
    gtab = nc.alloc_sbuf_tensor("gtab", [CAP, NBX], I32)
    stab = nc.alloc_sbuf_tensor("stab", [CAP, NBX], I32)
    wtab = nc.alloc_sbuf_tensor("wtab", [CAP, NBX], F32)
    etab = nc.alloc_sbuf_tensor("etab", [1, NBX], I32)
    nbt = nc.alloc_sbuf_tensor("nbt", [1, 2], I32)
    s5p = flat(C, 8256, 2048)
    braw = s5p[:, 0:512].rearrange("p (r g n) -> p r g n", r=2, g=GI)
    bbar = flat(C, 10368, 512).rearrange("p (r g n) -> p r g n", r=2, g=GI)
    craw = s5p[:, 512:1024].rearrange("p (r i a m) -> p r i a m", r=2, i=2, a=2)
    cpar = flat(C, 10880, 512).rearrange("p (r g n) -> p r g n", r=2, g=GI)
    tq = [s5p[:, 1024 + 256 * i:1280 + 256 * i].rearrange("p (g n) -> p g n", g=GI) for i in range(2)]
    masktmp = W_[0]
    tv = [s5p[:, 1536 + 256 * i:1792 + 256 * i].rearrange("p (g n) -> p g n", g=GI) for i in range(2)]

    skip = b1T[0:N, :].rearrange("p (g n) -> p g n", g=G)

    def columns(t, h, tile):
        return t[:, 4 * h * T:(4 * h + 4) * T].rearrange("p (k t) -> p k t", k=4)[:, :, tile * P:(tile + 1) * P]

    ps = nc.alloc_psum_tensor("ps", [P, 8, 512], F32)
    S = {}

    def sem(name):
        if name not in S:
            S[name] = nc.alloc_semaphore(name)
        return S[name]

    bank_full = [sem(f"bank_full{b}") for b in range(8)]
    bank_free = [sem(f"bank_free{b}") for b in range(8)]
    slot_full = [sem(f"slot_full{s}") for s in range(RING)]
    slot_free = [sem(f"slot_free{s}") for s in range(RING)]

    def bank(job):
        return ps[:, JOBS[job][0], :]

    def wait_full(eng, job):
        b, use = JOBS[job]
        eng.wait_ge(bank_full[b], use)

    def wait_read(eng, job):
        b, use = JOBS[job]
        eng.wait_ge(bank_free[b], use)

    def freed(job, ins):
        ins.then_inc(bank_free[JOBS[job][0]], 1)

    block = nc.Block()
    with block:
        @block.sync
        def _(sp):
            def two_chunks(w, i):
                return w[i * 256:(i + 1) * 256, :].rearrange("(k p) n -> p k n", p=P)

            def load(n):
                w, i = STREAM[n]
                s, use = SLOT_OF[w, i]
                if w == "wq_high":
                    wait_full(sp, "o3")
                    sp.wait_ge(sem("glu_done"), 4)
                    sp.wait_ge(sem("qe_ready"), 1)
                    for k in range(4):
                        sp.dma_start(ring[:, WQ[k], :].rearrange("p (k n) -> p k n", n=D),
                                     two_chunks(A["xa_w_q"][0], k)).then_inc(sem(f"wq_in{k}"), 16)
                    return
                if use > 1:
                    wait_full(sp, LAST_JOB[STREAM[n - PRE][0]])
                if w in COLS:
                    src = w_in[i * 512:(i + 1) * 512, COLS[w]:COLS[w] + HW].rearrange("(k p) n -> p k n", p=P)
                elif w == "glu":
                    src = w_glu.rearrange("(k p) n -> p k n", p=P)
                else:
                    src = two_chunks({"wk": A["xa_w_k"][0], "wv": A["xa_w_v"][0], "wout": w_out,
                                      "wo": A["xa_w_o"][0]}[w], i)
                dst = ring[:, s, :].rearrange("p (k n) -> p k n", n=D if w[0] == "w" else HW)
                sp.dma_start(dst, src).then_inc(slot_full[s], 16)

            for t in range(NT):
                load(t)
                sp.dma_start(hbuf[:, t, :], x[t * P:(t + 1) * P, :]).then_inc(sem(f"x_in{t}"), 16)
            sp.dma_start(lnw[:, 0, :], A["ln_in_g"].partition_broadcast(P)).then_inc(sem("ln_in"), 16)
            sp.dma_start(lnw[:, 1, :], A["ln_in_b"].partition_broadcast(P)).then_inc(sem("ln_in"), 16)
            for i, nm in enumerate(("s5_lam_re", "s5_lam_im", "s5_log_dt")):
                sp.dma_start(lam_in[:, i * P:(i + 1) * P].rearrange("g (a p) -> g a p", a=2),
                             A[nm][0].rearrange("(a g) p -> g a p", a=2)).then_inc(sem("params"), 16)
            for r, nm in enumerate(("s5_b_re", "s5_b_im")):
                for a in range(2):
                    sp.dma_start(braw[a * PST:(a + 1) * PST, r],
                                 A[nm][0, a * GI:(a + 1) * GI].rearrange("g p n -> p g n")).then_inc(sem("params"), 16)
            load(NT)
            for i, s in wv_rest.items():
                sp.dma_start(ring[:, s, :].rearrange("p (k n) -> p k n", n=D), two_chunks(A["xa_w_v"][0], i))\
                  .then_inc(sem(f"wv_in{i}"), 16)
            for n in range(NT + 1, len(STREAM)):
                load(n)

            def load_w1(k, e_rows):
                sp.dma_start(ring[:, k, :], e_rows).then_inc(slot_full[k], 16)

            def load_w1_dyn(b, e):
                for k in range(8):
                    sp.wait_ge(slot_free[k], b)
                    load_w1(k, w1[bass.ds(e, 1), k * P:(k + 1) * P, :].rearrange("a p n -> p (a n)"))

            def load_w2_dyn(b, e):
                for q in range(4):
                    sp.wait_ge(slot_free[8 + q], b)
                    sp.dma_start(ring[:, 8 + q, :].rearrange("p (k n) -> p k n", k=2),
                                 w2[bass.ds(e, 1), q * 256:(q + 1) * 256, :]
                                 .rearrange("a (k p) n -> p (a k) n", p=P)).then_inc(slot_full[8 + q], 16)

            sp.wait_ge(sem("normed"), 2 * NT)
            sp.dma_start(ring[:, 11, :].rearrange("p (k n) -> p k n", k=2), two_chunks(w2[0], 3)).then_inc(slot_full[11], 16)
            wait_full(sp, "aq1.3")
            early = SLOT_OF["wq_high", 3][0]
            load_w1(early, w1[0, early * P:(early + 1) * P, :])
            wait_full(sp, LAST_JOB["wo"])
            for k in range(8):
                if k != early:
                    load_w1(k, w1[0, k * P:(k + 1) * P, :])
            for q in range(3):
                sp.dma_start(ring[:, 8 + q, :].rearrange("p (k n) -> p k n", k=2),
                             two_chunks(w2[0], q)).then_inc(slot_full[8 + q], 16)
            for t in range(NT):
                sp.wait_ge(sem("normed"), 2 * NT + t + 1)
                sp.dma_start(h2_rows[t * P:(t + 1) * P, :], hbuf[:, t, :]).then_inc(sem("h2_out"), 16)
            for t in range(NT):
                sp.wait_ge(sem("h_scaled"), t + 1)
                sp.dma_start(sum_rows[t * P:(t + 1) * P, :], hbuf[:, t, :]).then_inc(sem("sum_out"), 16)
            sp.dma_start(sum_rows[T:T + CAP, :], hbuf[0:CAP, 0, :]).then_inc(sem("sum_out"), 16)
            sp.wait_ge(sem("tables_ready"), 1)
            nb = sp.value_load(nbt[0:1, 0:1], min_val=E, max_val=NBX - 1)
            last = sp.value_load(nbt[0:1, 1:2], min_val=E - 1, max_val=NBX - 2)
            for k in range(8):
                sp.wait_ge(slot_free[k], 1)
                load_w1(k, w1[1, k * P:(k + 1) * P, :])
            with sp.Fori(1, last) as b:
                e = sp.value_load(etab[0:1, bass.ds(b + 1, 1)], min_val=0, max_val=E - 1)
                before = sp.value_load(etab[0:1, bass.ds(b, 1)], min_val=0, max_val=E - 1)
                load_w1_dyn(b + 1, e)
                load_w2_dyn(b, before)
            load_w2_dyn(last, sp.value_load(etab[0:1, bass.ds(last, 1)], min_val=0, max_val=E - 1))
            sp.wait_ge(sem("y_added"), nb * 16)
            for t in range(NT):
                sp.dma_start(hbuf[:, t, :], sum_rows[t * P:(t + 1) * P, :]).then_inc(sem(f"sum_in{t}"), 16)
            for t in range(NT):
                sp.wait_ge(sem("normed"), 3 * NT + t + 1)
                sp.dma_start(out[0, t * P:(t + 1) * P, :], hbuf[:, t, :]).then_inc(sem("out_done"), 16)
            sp.wait_ge(sem("out_done"), 16 * NT)

        @block.gpsimd
        def _(pool):
            gp = nc.gpsimd
            step = [0]

            def link(ins):
                step[0] += 1
                ins.then_inc(sem("pool_step"), 1)
                pool.wait_ge(sem("pool_step"), step[0])

            gp.memset(ones[:, :], 1.0)
            gp.memset(tri[:, :], 1.0)
            link(gp.memset(ident[:, :], 1.0))
            gp.affine_select(out=tri[:, :], in_=tri[:, :], compare_op=ALU.is_gt, fill=0.0, base=0,
                             pattern=[[1, P]], channel_multiplier=-1)
            gp.affine_select(out=ident[:, :], in_=ident[:, :], compare_op=ALU.is_equal, fill=0.0, base=0,
                             pattern=[[-1, P]], channel_multiplier=1).then_inc(sem("consts"), 1)
            wait_read(pool, "cT")
            pool.wait_ge(sem("s5_abar"), 1)
            ar = ab[:, 0, :].unsqueeze(2).to_broadcast([P, GI, N])
            ai = ab[:, 1, :].unsqueeze(2).to_broadcast([P, GI, N])

            def times_conj(o0, o1, v0, v1):
                gp.tensor_tensor(tv[0], v0, ar, ALU.mult)
                link(gp.tensor_tensor(tv[1], v1, ai, ALU.mult))
                link(gp.tensor_tensor(o0, tv[0], tv[1], ALU.add))
                gp.tensor_tensor(tv[0], v1, ar, ALU.mult)
                link(gp.tensor_tensor(tv[1], v0, ai, ALU.mult))
                link(gp.tensor_tensor(o1, tv[0], tv[1], ALU.subtract))

            times_conj(Vc[:, 0, :, 0, :], Vc[:, 1, :, 0, :], cpar[:, 0], cpar[:, 1])
            for k in range(1, L):
                times_conj(Vc[:, 0, :, k, :], Vc[:, 1, :, k, :], Vc[:, 0, :, k - 1, :], Vc[:, 1, :, k - 1, :])
            gp.memset(idle, 0.0).then_inc(sem("s5_v"), 1)
            pool.wait_ge(sem("u_out"), 16)
            link(gp.memset(Toe, 0.0))
            for q in range(8):
                wait_read(pool, f"KK{q}")
            link(gp.tensor_tensor(skip, ident[0:N, 0:N].unsqueeze(1).to_broadcast([N, G, N]),
                                  rowsT[0:N, 64:96].unsqueeze(2).to_broadcast([N, G, N]), ALU.mult))
            link(gp.tensor_tensor(KKs[:, :, 0:N], KKs[:, :, 0:N], skip, ALU.add))
            for i in range(L):
                gp.dma_start(Toe[i * N:(i + 1) * N, :, i * N:P], KKs[:, :, 0:P - i * N])\
                  .then_inc(sem("toe_shifted"), 16)
            pool.wait_ge(sem("toe_shifted"), 16 * L)
            gp.memset(X[:, :, :, 0], 0.0).then_inc(sem("toe_ready"), 1)
            wait_full(pool, "Z1.1")
            gp.memset(Sc, 0.0).then_inc(sem("scores_zero"), 1)
            for i in range(4):
                s = SLOT_OF["wo", i][0]
                pool.wait_ge(sem("wo_high"), i + 1)
                gp.tensor_tensor(wo_lo[i][:, :], ring[:, s, :], wo_hi[i][:, :].bitcast(F32), ALU.subtract)\
                  .then_inc(sem("wo_split"), 1)
            wait_full(pool, "lg0")
            link(gp.memset(Xg, 0.0))
            pool.wait_ge(sem("gates_ready"), 1)
            pool.wait_ge(sem("block_onehots"), 1)
            gp.tensor_tensor(Btg[:, :, NBX:], Boh, gate.rearrange("p t k -> p (t k)").unsqueeze(2)
                             .to_broadcast([P, 16, NBX]), ALU.mult).then_inc(sem("gate_onehots"), 1)
            pool.wait_ge(sem("tables_ready"), 1)
            pool.wait_ge(sem("h2_out"), 16 * NT)
            last = pool.value_load(nbt[0:1, 1:2], min_val=E - 1, max_val=NBX - 2)

            last_token = pool.to_reg(T - 1)

            def gather():
                gp.indirect_dma_start(Xg, None, h2_rows, bass.IndirectOffsetOnAxis(ap=gix[:, 0:1].bitcast(U32), axis=0),
                                      bounds_check=last_token, oob_is_err=False).then_inc(sem("x_gathered"), 16)

            def indices(dst, table, b, n):
                gp.tensor_copy(dst[:, :], table[:, bass.ds(b, 1)]).then_inc(sem("pool_step"), 1)
                pool.wait_ge(sem("pool_step"), n)
                gp.tensor_tensor(idle, ones[:, 0:1], ones[:, 0:1], ALU.add)

            def scatter():
                gp.indirect_dma_start(sum_rows, bass.IndirectOffsetOnAxis(ap=six[:, 0:1].bitcast(U32), axis=0), ysb, None,
                                      compute_op=ALU.add).then_inc(sem("y_added"), 16)

            link(gp.tensor_copy(gix[:, :], gtab[:, 0:1]))
            gather()
            pool.wait_ge(sem("x_gathered"), 16)
            pool.wait_ge(sem("xt_full"), 1)
            link(gp.tensor_copy(gix[:, :], gtab[:, 1:2]))
            gather()
            pool.wait_ge(sem("x_gathered"), 32)
            pool.wait_ge(sem("xt_full"), 2)
            link(gp.tensor_copy(gix[:, :], gtab[:, 2:3]))
            gather()
            pool.wait_ge(sem("sum_out"), 16 * (NT + 1))
            pool.wait_ge(sem("y_copied"), 1)
            link(gp.tensor_copy(six[:, :], stab[:, 0:1]))
            scatter()
            base = step[0]
            with pool.Fori(1, last) as b:
                pool.wait_ge(sem("x_gathered"), 16 * b + 32)
                pool.wait_ge(sem("xt_full"), b + 2)
                indices(gix, gtab, b + 2, 2 * b + (base - 1))
                gather()
                pool.wait_ge(sem("y_copied"), b + 1)
                pool.wait_ge(sem("y_added"), 16 * b)
                indices(six, stab, b, 2 * b + base)
                scatter()
            pool.wait_ge(sem("y_copied"), last + 1)
            pool.wait_ge(sem("y_added"), 16 * last)
            indices(six, stab, last, 2 * last + (base - 1))
            scatter()

        @block.scalar
        def _(act):
            sc = nc.scalar
            step = [0]

            def link(ins):
                step[0] += 1
                ins.then_inc(sem("act_step"), 1)
                act.wait_ge(sem("act_step"), step[0])

            def ld(o, i, name="params"):
                act.dma_start(o, i).then_inc(sem(name), 16)

            ld(memx, mem.rearrange("(m p) d -> p m d", p=P), "mem_in")
            ld(rows[0:8, :], A["hgrn_lb_logits"].rearrange("r (h d) -> (r h) d", d=P))
            ld(rows[8:12, :], A["s5_b_glu"].rearrange("a (c d) -> (a c) d", d=P))
            ld(rows[12:16, :], A["s5_b_glu"].rearrange("a (c d) -> (a c) d", d=P))
            ld(dn.rearrange("g (i n) -> g i n", n=N),
               A["s5_d"][0].rearrange("(g n) -> g n", n=N).unsqueeze(1).to_broadcast([G, L, N]))
            for r, nm in enumerate(("s5_c_re", "s5_c_im")):
                for i in range(2):
                    ld(craw[:, r, i], A[nm][0].rearrange("(a i g) n p -> i (g n) a p", a=2, i=2)[i])
            ld(ngb, A["hgrn_norm_g"][0].partition_broadcast(P))
            ld(rbb, A["router_b"][0].partition_broadcast(P))

            def copy(dst, src):
                return sc.activation(dst, src, ACT.Copy)

            def evac(j, dst, src):
                wait_full(act, j)
                freed(j, copy(dst, src))

            def transposed_h(n, t):
                for h in range(2):
                    j = f"hT{n}.{t}.{h}"
                    if n == 1:
                        wait_full(act, j)
                        sc.activation(columns(hT_hi, h, t), bank(j).rearrange("p (k n) -> p k n", k=4), ACT.Copy)\
                          .then_inc(sem("h_high"), 1)
                        continue
                    evac(j, hT[:, 4 * h:4 * h + 4, t * P:(t + 1) * P], bank(j).rearrange("p (k n) -> p k n", k=4))

            def norm_weights(n, g, b):
                act.wait_ge(sem("normed"), NT * n)
                ld(lnw[:, 0, :], A[g][0].partition_broadcast(P), "ln_in")
                ld(lnw[:, 1, :], A[b][0].partition_broadcast(P), "ln_in")

            for m in range(2):
                for h in range(2):
                    j = f"mT{m}.{h}"
                    evac(j, memT[:, 4 * h:4 * h + 4, m * P:(m + 1) * P], bank(j).rearrange("p (k n) -> p k n", k=4))
            act.wait_ge(sem("var_ready"), NT)
            sc.activation(stat[:, 0:NT], stat[:, 0:NT], ACT.Sqrt).then_inc(sem("std_ready"), NT)
            for i in range(4):
                j = f"K{i}"
                evac(j, kT[:, 2 * i:2 * i + 2, :], bank(j).rearrange("p (k n) -> p k n", k=2))
            for t in range(NT):
                if t == 1:
                    act.wait_ge(sem("angles"), 1)
                    sc.activation(ab[:, 5, :], ab[:, 5, :], ACT.Sin)
                    sc.activation(ab[:, 6, :], ab[:, 6, :], ACT.Sin).then_inc(sem("sines"), 1)
                transposed_h(0, t)
                evac(f"V{t // 2}.{t % 2}", vm[:, t // 2, 512 * (t % 2):512 * (t % 2) + 512], bank(f"V{t // 2}.{t % 2}"))
            for t in range(NT):
                act.wait_ge(sem("normed"), t + 1)
                act.dma_start(h0_rows[t * P:(t + 1) * P, :], hbuf[:, t, :]).then_inc(sem("h0_out"), 16)
            norm_weights(1, "ln1_g", "ln1_b")
            for c in range(4):
                j = f"u{c}"
                evac(j, ucm[:, c, :].rearrange("p (j c) -> p c j", j=L), bank(j).rearrange("p (c j) -> p c j", j=L))
            wait_read(act, "u3")
            act.dma_start(u_rows.rearrange("(c p) t -> p c t", p=P), ucm).then_inc(sem("u_out"), 16)
            for r in range(2):
                for q in range(4):
                    j = f"W{r}.{q}"
                    evac(j, Wst[:, r, 4 * q:4 * q + 4, :], bank(j).rearrange("p (g m) -> p g m", g=4))
            act.wait_ge(sem("u_out"), 16)
            act.wait_ge(sem("h0_out"), 16 * NT)
            for j in range(L):
                act.dma_start(ug[j * N:(j + 1) * N], u_rows.rearrange("(g n) (j c) -> j n g c", n=N, j=L)[j])\
                   .then_inc(sem("u_in"), 16)
            for q in range(8):
                j = f"KK{q}"
                evac(j, KKs[:, 4 * q:4 * q + 4, :], bank(j)[0:N, :].rearrange("p (g m) -> p g m", g=4))
            act.wait_ge(sem("lb_logits"), 1)
            sc.activation(lbx[:, 0:8], lbx[:, 0:8], ACT.Exp).then_inc(sem("lb_exp"), 1)
            act.wait_ge(sem("s5_v"), 1)
            for h in range(4):
                j = f"f{h}"
                wait_full(act, j)
                freed(j, sc.activation(kh[:, h * T:(h + 1) * T], bank(j), ACT.Sigmoid))
            act.wait_ge(sem("f_ready"), 4)
            sc.activation(P1, cum, ACT.Ln).then_inc(sem("logf_ready"), 1)
            for r in range(2):
                for h in range(2):
                    j = f"Z{r}.{h}"
                    evac(j, X[:, r, 8 * h:8 * h + 8, 1:NC + 1], bank(j).rearrange("p (g c) -> p g c", g=8))
            for h in range(4):
                j = f"q{h}"
                evac(j, qh[:, h * T:(h + 1) * T], bank(j))
            for c in range(4):
                j = f"Y{c}"
                wait_full(act, j)
                freed(j, sc.activation(Ys[:, 8 * c:8 * c + 8, :], bank(j).rearrange("p (g c) -> p g c", g=8),
                                       ACT.Gelu_apprx_tanh))
            wait_read(act, "Y3")
            for j in range(L):
                act.dma_start(s5_rows.rearrange("(g n) (j c) -> j n g c", n=N, j=L)[j], Ys[j * N:(j + 1) * N])\
                   .then_inc(sem("s5_out"), 16)

            def decay(n):
                act.wait_ge(sem("diff_ready"), n + 1)
                buf = P0 if n % 2 == 0 else P1
                sc.activation(buf, buf, ACT.Exp).then_inc(sem("decay_ready"), 1)

            def between(j):
                c = int(j[1])
                if j[0] == "i":
                    evac(j, vh[:, c, :], bank(j))
                elif j[0] == "g":
                    wait_full(act, j)
                    sc.activation(gs[:, c, :], bank(j), ACT.Sigmoid).then_inc(sem("sig_g"), 1)
                else:
                    wait_full(act, j)
                    freed(j, sc.activation(s5g[:, c, :], bank(j), ACT.Sigmoid, bias=rowsT[:, 8 + c:9 + c]))

            decay(0)
            decay(1)
            act.wait_ge(sem("s5_out"), 16 * L)
            act.dma_start(ycm, s5_rows.rearrange("(c p) t -> p c t", p=P)).then_inc(sem("s5_in"), 16)
            for n in range(len(LEVELS)):
                for j in BETWEEN[n]:
                    between(j)
                if n + 2 < len(LEVELS):
                    decay(n + 2)
            sc.activation(qe, cum, ACT.Exp).then_inc(sem("qe_exp"), 1)
            sc.activation(el, cum.rearrange("p (b s) -> p b s", s=P)[:, :, P - 1], ACT.Exp).then_inc(sem("el_ready"), 1)
            act.wait_ge(sem("diff_ready"), len(LEVELS) + 1)
            sc.activation(P1, P1, ACT.Exp).then_inc(sem("decay_ready"), 1)
            for j in BETWEEN[-1]:
                between(j)
            for t in range(NT):
                j = f"kd{t}"
                evac(j, kdT[:, t], bank(j).rearrange("p (h d) -> p h d", h=NH))
            for t in range(NT):
                act.dma_start(hbuf[:, t, :], h0_rows[t * P:(t + 1) * P, :]).then_inc(sem("h0_in"), 16)
            for t in range(NT + 1):
                if t < NT:
                    j = f"o{t}"
                    wait_full(act, j)
                    for h in range(NH):
                        ins = sc.activation(sq[:, h * P:(h + 1) * P], bank(j)[:, h * P:(h + 1) * P], ACT.Square,
                                            accum_out=rms[:, 4 * t + h:4 * t + h + 1])
                    ins.then_inc(sem("ms_ready"), 1)
                    act.wait_ge(sem("ms_eps"), t + 1)
                    sc.activation(rms[:, 16 + 4 * t:20 + 4 * t], rms[:, 16 + 4 * t:20 + 4 * t], ACT.Sqrt)\
                      .then_inc(sem("rms_ready"), 1)
                if t:
                    j = f"oaT{t - 1}"
                    evac(j, hT[:, 0:4, (t - 1) * P:t * P], bank(j).rearrange("p (k n) -> p k n", k=4))

            def roots_and_transposes(n, tiles=NT):
                for t in range(NT + 1):
                    if t < NT:
                        act.wait_ge(sem("var_ready"), NT * n + t + 1)
                        sc.activation(stat[:, t:t + 1], stat[:, t:t + 1], ACT.Sqrt).then_inc(sem("std_ready"), 1)
                    if 0 < t <= tiles:
                        transposed_h(n, t - 1)

            wait_full(act, f"oaT{NT - 1}")
            ld(b1raw, A["exp_b1"][0].rearrange("e (f p) -> (e f) p", p=P).rearrange("(q r) p -> r q p", q=4), "late_in")
            ld(rw, A["router_w"][0].rearrange("(k p) e -> p k e", p=P), "late_in")
            for i in range(4):
                act.wait_ge(sem(f"wq_in{i}"), 16)
                sc.activation(wq_hi[i][:, :], ring[:, WQ[i], :], ACT.Copy).then_inc(sem("wq_high"), 1)
            roots_and_transposes(1, NT - 1)
            norm_weights(2, "ln2_g", "ln2_b")
            for half in range(2):
                if half:
                    transposed_h(1, NT - 1)
                for c in range(4):
                    j = f"aq{half}.{c}"
                    evac(j, qT[:, 2 * c:2 * c + 2, half * M:(half + 1) * M], bank(j).rearrange("p (c t) -> p c t", c=2))
            for t in range(NT + 1):
                if t < NT:
                    for h in range(2):
                        j = f"sc{t}.{h}"
                        act.wait_ge(sem("max_ready"), 2 * t + h + 1)
                        if t >= 2 and h == 0:
                            wait_full(act, f"PT{t - 2}.1")
                        for i in range(2):
                            hh = 2 * h + i
                            ins = sc.activation(Pb[:, t % 2, hh, :], bank(j)[:, M * i:M * i + M], ACT.Exp, scale=SCALE,
                                                bias=amax[:, 4 * t + hh:4 * t + hh + 1],
                                                accum_out=asum[:, 4 * t + hh:4 * t + hh + 1])
                        ins.then_inc(sem("exp_ready"), 1)
                if t:
                    for m in range(2):
                        j = f"PT{t - 1}.{m}"
                        wait_full(act, j)
                        freed(j, copy(PT[:, m, :, (t - 1) * P:t * P], bank(j).rearrange("p (h n) -> p h n", h=NH)))
            for c in range(8):
                j = f"ao{c}"
                wait_full(act, j)
                sc.activation(hT_hi[:, c * T:(c + 1) * T], bank(j), ACT.Copy).then_inc(sem("ao_high"), 1)
            ld(b2sb, A["exp_b2"][0], "b2_in")
            evac("b1T", b1T[:, :], bank("b1T"))
            roots_and_transposes(2)
            norm_weights(3, "ln3_g", "ln3_b")
            act.wait_ge(sem("top_ready"), NT)
            for t in range(NT):
                ins = sc.activation(gate[:, t, :], topv[:, 8 * t:8 * t + 4], ACT.Exp,
                                    bias=ntop[:, t:t + 1], accum_out=gsum[:, t:t + 1])
            ins.then_inc(sem("gate_exp"), 1)
            evac("GT", GTs, bank("GT")[0:E, :])
            for t in range(NT):
                for h in range(2):
                    evac(f"gb{t}.{h}", gsc[:, t, 512 * h:512 * h + 512], bank(f"gb{t}.{h}"))
            act.wait_ge(sem("tables_ready"), 1)
            last = act.value_load(nbt[0:1, 1:2], min_val=E - 1, max_val=NBX - 2)

            def transposed_rows():
                sc.activation(xT[:, 0:4, :], ps[:, 6, 0:4 * CAP].rearrange("p (k s) -> p k s", k=4), ACT.Copy)
                sc.activation(xT[:, 4:8, :], ps[:, 7, 0:4 * CAP].rearrange("p (k s) -> p k s", k=4), ACT.Copy)\
                  .then_inc(sem("xt_copied"), 1)

            def sigmoids():
                sc.activation(sig, glu, ACT.Sigmoid, scale=SW_ALPHA).then_inc(sem("sig_ready"), 1)

            def result_rows(b):
                for h in range(2):
                    ins = sc.activation(ysb[:, 512 * h:512 * h + 512], ps[0:CAP, 4 + h, :], ACT.Copy,
                                        scale=wtab[:, bass.ds(b, 1)])
                ins.then_inc(sem("y_copied"), 1)

            def w2_high(b):
                for q in range(4):
                    act.wait_ge(slot_full[8 + q], 16 * b + 16)
                    sc.activation(w2_hi[q][:, :], ring[:, 8 + q, :], ACT.Copy).then_inc(sem("w2_high"), 1)

            for b in range(2):
                act.wait_ge(sem("xt_full"), b + 1)
                transposed_rows()
            act.wait_ge(sem("glu_ready"), 1)
            sigmoids()
            act.wait_ge(sem("h_scaled"), NT)
            w2_high(0)
            act.wait_ge(sem("xt_full"), 3)
            transposed_rows()
            act.wait_ge(sem("glu_ready"), 2)
            act.wait_ge(sem("act_ready"), 1)
            sigmoids()
            act.wait_ge(slot_free[11], 1)
            act.wait_ge(sem("wtab_ready"), 1)
            result_rows(0)
            with act.Fori(1, last) as b:
                w2_high(b)
                act.wait_ge(sem("xt_full"), b + 3)
                transposed_rows()
                act.wait_ge(sem("glu_ready"), b + 2)
                act.wait_ge(sem("act_ready"), b + 1)
                sigmoids()
                act.wait_ge(slot_free[11], b + 1)
                act.wait_ge(sem("y_added"), 16 * b)
                result_rows(b)
            w2_high(last)
            act.wait_ge(slot_free[11], last + 1)
            act.wait_ge(sem("y_added"), 16 * last)
            result_rows(last)
            for t in range(NT):
                act.wait_ge(sem("var_ready"), NT * 3 + t + 1)
                sc.activation(stat[:, t:t + 1], stat[:, t:t + 1], ACT.Sqrt).then_inc(sem("std_ready"), 1)

        @block.vector
        def _(v):
            ve = nc.vector
            step, steps = [0], ["dve_step"]

            def link(ins):
                step[0] += 1
                ins.then_inc(sem(steps[0]), 1)
                v.wait_ge(sem(steps[0]), step[0])

            def stats(n, t):
                link(ve.bn_stats(mvs[:, 0:6], hbuf[:, t, 0:512]))
                link(ve.bn_stats(mvs[:, 6:12], hbuf[:, t, 512:1024]))
                link(ve.bn_aggr(mv[:, 2 * t:2 * t + 2], mvs))
                ve.tensor_scalar(stat[:, t:t + 1], mv[:, 2 * t + 1:2 * t + 2], LN_EPS, None, ALU.add).then_inc(sem("var_ready"), 1)
                v.wait_ge(sem("var_ready"), NT * n + t + 1)

            def normalise(n, t):
                v.wait_ge(sem("std_ready"), NT * n + t + 1)
                link(ve.reciprocal(stat[:, 4 + t:5 + t], stat[:, t:t + 1]))
                link(ve.scalar_tensor_tensor(out=hbuf[:, t, :], in0=hbuf[:, t, :], scalar=mv[:, 2 * t:2 * t + 1],
                                             in1=lnw[:, 0, :], op0=ALU.subtract, op1=ALU.mult))
                ve.scalar_tensor_tensor(out=hbuf[:, t, :], in0=hbuf[:, t, :], scalar=stat[:, 4 + t:5 + t],
                                        in1=lnw[:, 1, :], op0=ALU.mult, op1=ALU.add).then_inc(sem("normed"), 1)
                v.wait_ge(sem("normed"), NT * n + t + 1)

            v.wait_ge(sem("consts"), 1)
            for t in range(NT):
                v.wait_ge(sem(f"x_in{t}"), 16)
                stats(0, t)
            v.wait_ge(sem("ln_in"), 32)
            for t in range(NT):
                normalise(0, t)

            wait_full(v, "par")
            freed("par", ve.tensor_copy(rowsT, bank("par")[:, 0:96]))
            wait_read(v, "par")
            wait_full(v, "cT")
            ct = bank("cT").rearrange("p (r i m) -> p r i m", r=2, i=2)
            ve.tensor_copy(cpar[:, 0].rearrange("p (i g) n -> p i (g n)", i=2), ct[:, 0])
            freed("cT", ve.tensor_scalar(cpar[:, 1].rearrange("p (i g) n -> p i (g n)", i=2), ct[:, 1], -1.0, None,
                                         ALU.mult))
            lamr, lami = rowsT[:, 16:32], rowsT[:, 32:48]

            def exponential(dst, src):
                n, r, p, bits = ab[:, 21, :], ab[:, 22, :], ab[:, 23, :], ab[:, 20, :].bitcast(I32)
                link(ve.tensor_scalar(n, src, 1.0 / LN2, None, ALU.mult))
                link(ve.tensor_scalar(n, n, MAGIC, None, ALU.add))
                link(ve.tensor_scalar(n, n, MAGIC, None, ALU.subtract))
                link(ve.scalar_tensor_tensor(out=r, in0=n, scalar=-LN2_HIGH, in1=src, op0=ALU.mult, op1=ALU.add))
                link(ve.scalar_tensor_tensor(out=r, in0=n, scalar=-LN2_REST, in1=r, op0=ALU.mult, op1=ALU.add))
                link(ve.tensor_scalar(p, r, 1.0 / 5040, None, ALU.mult))
                for c in (720, 120, 24, 6, 2, 1):
                    link(ve.scalar_tensor_tensor(out=p, in0=p, scalar=1.0 / c, in1=r, op0=ALU.add, op1=ALU.mult))
                link(ve.tensor_scalar(n, n, 127.0, 0.0, ALU.add, ALU.max))
                link(ve.tensor_scalar(bits, n, 255.0, None, ALU.min))
                link(ve.tensor_scalar(bits, bits, 23, None, ALU.logical_shift_left))
                link(ve.scalar_tensor_tensor(out=dst, in0=p, scalar=1.0, in1=bits.bitcast(F32), op0=ALU.add, op1=ALU.mult))

            exponential(ab[:, 2, :], rowsT[:, 48:64])
            link(ve.tensor_tensor(ab[:, 3, :], lamr, ab[:, 2, :], ALU.mult))
            link(ve.tensor_tensor(ab[:, 4, :], lami, ab[:, 2, :], ALU.mult))
            link(ve.tensor_scalar(ab[:, 7, :], ab[:, 4, :], 1.0 / TWO_PI, None, ALU.mult))
            link(ve.tensor_scalar(ab[:, 7, :], ab[:, 7, :], MAGIC, None, ALU.add))
            link(ve.tensor_scalar(ab[:, 7, :], ab[:, 7, :], MAGIC, None, ALU.subtract))
            for part in (TP1, TP2, TP3):
                link(ve.scalar_tensor_tensor(out=ab[:, 4, :], in0=ab[:, 7, :], scalar=-part, in1=ab[:, 4, :],
                                             op0=ALU.mult, op1=ALU.add))
            sine, cosine = ab[:, 5, :], ab[:, 6, :]
            link(ve.tensor_scalar(ab[:, 5, :], ab[:, 4, :], -PI_BELOW, PI_BELOW, ALU.max, ALU.min))
            ve.tensor_scalar(ab[:, 6, :], ab[:, 5, :], 0.5, None, ALU.mult).then_inc(sem("angles"), 1)
            exponential(ab[:, 3, :], ab[:, 3, :])
            v.wait_ge(sem("sines"), 1)
            link(ve.tensor_tensor(ab[:, 6, :], ab[:, 6, :], ab[:, 6, :], ALU.mult))
            link(ve.tensor_scalar(ab[:, 6, :], ab[:, 6, :], -2.0, 1.0, ALU.mult, ALU.add))
            link(ve.tensor_tensor(ab[:, 0, :], ab[:, 3, :], ab[:, 6, :], ALU.mult))
            ve.tensor_tensor(ab[:, 1, :], ab[:, 3, :], ab[:, 5, :], ALU.mult).then_inc(sem("s5_abar"), 1)
            v.wait_ge(sem("s5_abar"), 1)
            nr, cr, ci, den, w = (ab[:, 8 + i, :] for i in range(5))
            link(ve.tensor_scalar(nr, ab[:, 0, :], -1.0, None, ALU.add))
            link(ve.tensor_tensor(den, lamr, lamr, ALU.mult))
            link(ve.tensor_tensor(w, lami, lami, ALU.mult))
            link(ve.tensor_tensor(den, den, w, ALU.add))
            link(ve.reciprocal(den, den))
            link(ve.tensor_tensor(cr, nr, lamr, ALU.mult))
            link(ve.tensor_tensor(w, ab[:, 1, :], lami, ALU.mult))
            link(ve.tensor_tensor(cr, cr, w, ALU.add))
            link(ve.tensor_tensor(cr, cr, den, ALU.mult))
            link(ve.tensor_tensor(ci, ab[:, 1, :], lamr, ALU.mult))
            link(ve.tensor_tensor(w, nr, lami, ALU.mult))
            link(ve.tensor_tensor(ci, ci, w, ALU.subtract))
            link(ve.tensor_tensor(ci, ci, den, ALU.mult))

            def times(o0, o1, a0, a1, b0, b1, t, done=None):
                ve.tensor_tensor(t[0], b0, a0, ALU.mult)
                link(ve.tensor_tensor(t[1], b1, a1, ALU.mult))
                link(ve.tensor_tensor(o0, t[0], t[1], ALU.subtract))
                ve.tensor_tensor(t[0], b1, a0, ALU.mult)
                link(ve.tensor_tensor(t[1], b0, a1, ALU.mult))
                ins = ve.tensor_tensor(o1, t[0], t[1], ALU.add)
                if done:
                    ins.then_inc(sem(done), 1)
                    v.wait_ge(sem(done), 1)
                else:
                    link(ins)

            def wide(a):
                return a.unsqueeze(2).to_broadcast([P, GI, N])

            times(bbar[:, 0], bbar[:, 1], wide(cr), wide(ci), braw[:, 0], braw[:, 1], tq)
            ve.tensor_copy(Qb[:, 0, :, L - 1, :], bbar[:, 0])
            link(ve.tensor_copy(Qb[:, 1, :, L - 1, :], bbar[:, 1]))
            for j in range(L - 2, -1, -1):
                times(Qb[:, 0, :, j, :], Qb[:, 1, :, j, :], wide(ab[:, 0, :]), wide(ab[:, 1, :]),
                      Qb[:, 0, :, j + 1, :], Qb[:, 1, :, j + 1, :], tq, None if j else "q_ready")
            lg = rowsT[:, 0:8]
            link(ve.tensor_tensor(lbx[:, 8:12], lg[:, 0:4], lg[:, 4:8], ALU.max))
            ve.tensor_tensor(lbx[:, 0:8].rearrange("p (r h) -> p r h", r=2), lg.rearrange("p (r h) -> p r h", r=2),
                             lbx[:, 8:12].unsqueeze(1).to_broadcast([P, 2, NH]), ALU.subtract)\
              .then_inc(sem("lb_logits"), 1)
            v.wait_ge(sem("lb_exp"), 1)
            link(ve.tensor_tensor(lbx[:, 8:12], lbx[:, 0:4], lbx[:, 4:8], ALU.add))
            link(ve.reciprocal(lbx[:, 8:12], lbx[:, 8:12]))
            link(ve.tensor_tensor(lb[:, 0:4], lbx[:, 0:4], lbx[:, 8:12], ALU.mult))
            link(ve.tensor_scalar(lb[:, 4:8], lb[:, 0:4], -1.0, 1.0, ALU.mult, ALU.add))

            col = masktmp[:, 0:P]
            row = masktmp[:, P:2 * P]
            t0, t1, t2 = masktmp[:, 256:384], masktmp[:, 384:512], masktmp[:, 512:640]
            link(ve.tensor_tensor_scan(col, ones[:, :], ones[:, :], -1.0, ALU.mult, ALU.add))
            link(ve.tensor_tensor(t0, col, ident[:, :], ALU.mult))
            link(ve.tensor_reduce(row[:, 0:1], t0, AX.X, ALU.add))
            link(ve.tensor_copy(masks[:, 0, :], ident[:, :]))
            coli = masktmp[:, 640:768].bitcast(I32)
            rowb = masktmp[:, 896:1024].bitcast(I32)
            xr = masktmp[:, 1024:1152].bitcast(I32)
            link(ve.tensor_copy(coli, col))
            link(ve.tensor_copy(rowb, row[:, 0:1].to_broadcast([P, P])))
            link(ve.tensor_tensor(xr, coli, rowb, ALU.bitwise_xor))
            link(ve.tensor_copy(t0, xr))
            for n, hs in enumerate(LEVELS):
                link(ve.tensor_scalar(t1, t0, float(hs), None, ALU.is_ge))
                link(ve.tensor_scalar(t2, t0, float(2 * hs), None, ALU.is_lt))
                link(ve.tensor_tensor(t1, t1, t2, ALU.mult))
                link(ve.tensor_tensor(masks[:, n + 1, :], t1, tri[:, :], ALU.mult))

            for m, x in ((13, ab[:, 3, :]), (13, ab[:, 13, :]), (13, ab[:, 13, :])):
                link(ve.tensor_tensor(ab[:, m, :], x, x, ALU.mult))
            t2_ = [ab[:, 19, :], ab[:, 20, :]]
            times(ab[:, 14, :], ab[:, 15, :], cosine, sine, cosine, sine, t2_)
            times(ab[:, 16, :], ab[:, 17, :], ab[:, 14, :], ab[:, 15, :], ab[:, 14, :], ab[:, 15, :], t2_)
            times(turn[:, 0, :, 0], turn[:, 1, :, 0], ab[:, 16, :], ab[:, 17, :], ab[:, 16, :], ab[:, 17, :], t2_)
            wait_full(v, "W1.3")
            n = 1
            while n < NC:
                far = [turn[:, r, :, n - 1:n].to_broadcast([P, GI, n]) for r in range(2)]
                times(turn[:, 0, :, n:2 * n], turn[:, 1, :, n:2 * n], turn[:, 0, :, 0:n], turn[:, 1, :, 0:n],
                      far[0], far[1], [t[:, 0:GI * n].rearrange("p (g c) -> p g c", g=GI) for t in t3[0:2]])
                n *= 2

            for h in range(4):
                wait_read(v, f"f{h}")
                if h == 0:
                    v.wait_ge(sem("toe_shifted"), 16 * L)
                s = slice(h * T, (h + 1) * T)
                link(ve.tensor_scalar(cum[:, s], kh[:, s], lb[:, 4 + h:5 + h], lb[:, h:h + 1], ALU.mult, ALU.add))
                ve.tensor_scalar(kh[:, s], cum[:, s], -1.0, 1.0, ALU.mult, ALU.add).then_inc(sem("f_ready"), 1)
            v.wait_ge(sem("logf_ready"), 1)
            for i in range(16):
                s = slice(i * P, (i + 1) * P)
                ins = ve.tensor_tensor_scan(cum[:, s], ones[:, :], P1[:, s], 0.0, ALU.mult, ALU.add)
            ins.then_inc(sem("cum_ready"), 1)
            v.wait_ge(sem("cum_ready"), 1)

            for r in range(2):
                for h in range(2):
                    wait_read(v, f"Z{r}.{h}")
            v.wait_ge(sem("toe_ready"), 1)
            Zr, Zi = X[:, 0, :, 1:NC + 1], X[:, 1, :, 1:NC + 1]
            u0, u1, u2 = (t.rearrange("p (g c) -> p g c", g=GI) for t in t3)
            co, si = turn[:, 0], turn[:, 1]

            def turned(sign):
                ve.tensor_tensor(u0, Zr, co, ALU.mult)
                ve.tensor_tensor(u1, Zi, si, ALU.mult)
                link(ve.tensor_tensor(u2, Zr, si, ALU.mult))
                link(ve.tensor_tensor(Zr, u0, u1, ALU.subtract if sign > 0 else ALU.add))
                link(ve.tensor_tensor(u0, Zi, co, ALU.mult))
                return ve.tensor_tensor(Zi, u0, u2, ALU.add if sign > 0 else ALU.subtract)

            link(turned(-1))
            for r in range(2):
                for g in range(GI):
                    z = X[:, r, g, 1:NC + 1]
                    ins = ve.tensor_tensor_scan(z, ab[:, 13, g:g + 1].to_broadcast([P, NC]), z, 0.0, ALU.mult, ALU.add)
            link(ins)
            turned(1).then_inc(sem("x_ready"), 1)

            def gates(t):
                v.wait_ge(sem("sig_g"), t + 1)
                j = f"g{t}"
                wait_full(v, j)
                link(ve.tensor_tensor(gs[:, t, :], gs[:, t, :], bank(j), ALU.mult))
                freed(j, ve.tensor_tensor(gs[:, t, :].rearrange("p (h e) -> p h e", h=NH),
                                          gs[:, t, :].rearrange("p (h e) -> p h e", h=NH),
                                          ngb.unsqueeze(1).to_broadcast([P, NH, P]), ALU.mult))

            def halves(a, hs):
                return a.rearrange("p (b w s) -> p b w s", w=2, s=hs)

            def diff(n):
                hs = LEVELS[n]
                buf = P0 if n % 2 == 0 else P1
                if n >= 2:
                    for t in range(NT):
                        wait_full(v, f"s{n - 1}.{t}")
                c4, d4 = halves(cum, hs), halves(buf, hs)
                ref = c4[:, :, 0, hs - 1:hs].to_broadcast([P, 2048 // (2 * hs), hs])
                ve.tensor_tensor(d4[:, :, 1, :], c4[:, :, 1, :], ref, ALU.subtract)
                ve.tensor_tensor(d4[:, :, 0, :], ref, c4[:, :, 0, :], ALU.subtract).then_inc(sem("diff_ready"), 1)

            def weigh(n):
                hs = LEVELS[n]
                buf = P0 if n % 2 == 0 else P1
                v.wait_ge(sem("decay_ready"), n + 1)
                d4, q4, k4 = halves(buf, hs), halves(qh, hs), halves(kh, hs)
                ve.tensor_tensor(d4[:, :, 1, :], d4[:, :, 1, :], q4[:, :, 1, :], ALU.mult)
                ve.tensor_tensor(d4[:, :, 0, :], d4[:, :, 0, :], k4[:, :, 0, :], ALU.mult).then_inc(sem("pair_ready"), 1)

            def place(n):
                for t in range(NT):
                    j = f"s{n}.{t}"
                    wait_full(v, j)
                    if n:
                        wait_read(v, f"s{n - 1}.{t}")
                    freed(j, ve.copy_predicated(Sc[:, t], masks[:, n, :].unsqueeze(1).to_broadcast([P, NH, P]),
                                                bank(j).rearrange("p (h s) -> p h s", h=NH)))

            diff(0)
            diff(1)
            for j in ("q0", "q1", "q2", "q3"):
                wait_read(v, j)
            v.wait_ge(sem("scores_zero"), 1)
            weigh(0)
            place(0)
            for n in range(1, len(LEVELS)):
                if n + 1 < len(LEVELS):
                    diff(n + 1)
                weigh(n)
                place(n)
                if n == len(LEVELS) - 2:
                    v.wait_ge(sem("s5_in"), 16)
                    for c in range(4):
                        wait_read(v, f"z{c}")
                        ve.tensor_tensor(s5T[:, c, :].rearrange("p (c j) -> p j c", j=L),
                                         s5g[:, c, :].rearrange("p (j c) -> p j c", j=L),
                                         ycm[:, c, :].rearrange("p (j c) -> p j c", j=L), ALU.mult)\
                          .then_inc(sem("glu_done"), 1)
            v.wait_ge(sem("qe_exp"), 1)
            ve.tensor_tensor(qe, qe, qh, ALU.mult).then_inc(sem("qe_ready"), 1)
            for t in range(NT):
                wait_full(v, f"s{len(LEVELS) - 1}.{t}")
            c3 = cum.rearrange("p (b s) -> p b s", s=P)
            ve.tensor_tensor(P1.rearrange("p (b s) -> p b s", s=P), c3[:, :, P - 1:P].to_broadcast([P, 16, P]), c3,
                             ALU.subtract).then_inc(sem("diff_ready"), 1)
            v.wait_ge(sem("decay_ready"), len(LEVELS) + 1)
            ve.tensor_tensor(P1, P1, kh, ALU.mult).then_inc(sem("kdec_ready"), 1)
            place(len(LEVELS))
            for t in range(NT):
                gates(t)
            v.wait_ge(sem("el_ready"), 1)
            for t in range(NT):
                if t < NT - 1:
                    j = f"st{t}"
                    wait_full(v, j)
                    for h in range(NH):
                        if t == 0:
                            ins = ve.tensor_copy(st[:, h, :], bank(j)[:, h * P:(h + 1) * P])
                        else:
                            ins = ve.scalar_tensor_tensor(out=st[:, h, :], in0=st[:, h, :],
                                                          scalar=el[:, 4 * h + t:4 * h + t + 1],
                                                          in1=bank(j)[:, h * P:(h + 1) * P], op0=ALU.mult, op1=ALU.add)
                    freed(j, ins)
                v.wait_ge(sem("ms_ready"), t + 1)
                a, b_ = rms[:, 4 * t:4 * t + 4], rms[:, 16 + 4 * t:20 + 4 * t]
                ve.tensor_scalar(b_, a, 1.0 / P, RMS_EPS, ALU.mult, ALU.add).then_inc(sem("ms_eps"), 1)
                v.wait_ge(sem("rms_ready"), t + 1)
                link(ve.reciprocal(a, b_))
                j = f"o{t}"
                for h in range(NH):
                    s = slice(h * P, (h + 1) * P)
                    ins = ve.scalar_tensor_tensor(out=oa[:, t, s], in0=bank(j)[:, s], scalar=rms[:, 4 * t + h:4 * t + h + 1],
                                                  in1=gs[:, t, s], op0=ALU.mult, op1=ALU.mult)
                freed(j, ins)

            def residual(n, name, then=None):
                for t in range(NT):
                    for h in range(2):
                        j = f"{name}{t}.{h}"
                        wait_full(v, j)
                        s = slice(512 * h, 512 * h + 512)
                        ins = ve.scalar_tensor_tensor(out=hbuf[:, t, s], in0=hbuf[:, t, s], scalar=ALPHA, in1=bank(j),
                                                      op0=ALU.mult, op1=ALU.add)
                        freed(j, ins)
                        wait_read(v, j)
                    stats(n, t)
                    normalise(n, t)
                    if then:
                        then(t)

            v.wait_ge(sem("h0_in"), 16 * NT)
            v.wait_ge(sem("ln_in"), 64)
            for i in range(4):
                v.wait_ge(sem("wq_high"), i + 1)
                ve.tensor_tensor(wq_lo[i][:, :], ring[:, WQ[i], :], wq_hi[i][:, :].bitcast(F32), ALU.subtract)\
                  .then_inc(sem("wq_split"), 1)

            def h_rest(t):
                for h in range(2):
                    j = f"hT1.{t}.{h}"
                    v.wait_ge(sem("h_high"), 2 * t + h + 1)
                    freed(j, ve.tensor_tensor(columns(hT_lo, h, t), bank(j).rearrange("p (k n) -> p k n", k=4),
                                              columns(hT_hi, h, t).bitcast(F32), ALU.subtract))

            residual(1, "w", lambda t: h_rest(t - 1) if t else None)
            h_rest(NT - 1)
            wait_full(v, "aq1.3")
            for t in range(NT):
                s, use = SLOT_OF["wo", t]
                v.wait_ge(slot_full[s], 16 * use)
                ve.tensor_copy(wo_hi[t][:, :], ring[:, s, :]).then_inc(sem("wo_high"), 1)
                for h in range(2):
                    j = f"sc{t}.{h}"
                    wait_full(v, j)
                    m2 = amax[:, 4 * t + 2 * h:4 * t + 2 * h + 2]
                    link(ve.tensor_reduce(m2, bank(j).rearrange("p (i m) -> p i m", i=2), AX.X, ALU.max))
                    ve.tensor_scalar(m2, m2, -SCALE, None, ALU.mult).then_inc(sem("max_ready"), 1)
                for h in range(2):
                    j = f"sc{t}.{h}"
                    v.wait_ge(sem("exp_ready"), 2 * t + h + 1)
                    s2 = asum[:, 4 * t + 2 * h:4 * t + 2 * h + 2]
                    freed(j, ve.reciprocal(s2, s2))
                    wait_read(v, j)
                    for i in range(2):
                        hh = 2 * h + i
                        ins = ve.tensor_scalar(Pb[:, t % 2, hh, :], Pb[:, t % 2, hh, :],
                                               asum[:, 4 * t + hh:4 * t + hh + 1], None, ALU.mult)
                    ins.then_inc(sem("probs_ready"), 1)
            for c in range(8):
                v.wait_ge(sem("ao_high"), c + 1)
                s = slice(c * T, (c + 1) * T)
                freed(f"ao{c}", ve.tensor_tensor(hT_lo[:, s], bank(f"ao{c}"), hT_hi[:, s].bitcast(F32), ALU.subtract))
            v.wait_ge(sem("ln_in"), 96)
            lgs = rt[:, 0:128].rearrange("p (t e) -> p t e", t=NT)
            OH = rt[:, 128:640].rearrange("p (i e) -> p i e", i=16)
            tmp = rt[:, 896:1408].rearrange("p (i e) -> p i e", i=16)
            pos = rt[:, 1408:1536].rearrange("p (t e) -> p t e", t=NT)
            cnt, nov, ovi, ovs = (rt[:, 1536 + 32 * i:1568 + 32 * i] for i in range(4))
            ixf = rt[:, 1696:1712]
            qq = rt[:, 1712:1840].rearrange("p (t e) -> p t e", t=NT)
            bl = rt[:, 1840:1968].rearrange("p (t e) -> p t e", t=NT)
            slk, blk = rt[:, 1968:1984], rt[:, 1984:2000]
            iof = rt[:, 2000:2000 + P]
            av = rt[:, 2128:2144]
            NX = NBX - E
            cmp_ = C[0:1, 4864:4864 + NX * E].rearrange("p (b e) -> p b e", e=E)
            tabf = rt[0:CAP, 2144:2144 + NBX]
            empty = rt[0:CAP, 2240:2240 + NBX]
            etf = rt[0:1, 2336:2336 + NBX]
            prow = rt[:, 2432:2433]
            topi = rt[:, 2440:2472].bitcast(U32)
            z = rt[:, 3136:3264].rearrange("p (t e) -> p t e", t=NT)
            assert NX * E <= D and NBX <= 96
            diag = tmp[:, 0:4, :].rearrange("p i e -> p (i e)")

            def numbers():
                link(ve.tensor_tensor_scan(iof, ones[:, :], ones[:, :], -1.0, ALU.mult, ALU.add))
                link(ve.tensor_tensor(diag, iof, ident[:, :], ALU.mult))
                link(ve.tensor_reduce(prow, diag, AX.X, ALU.add))
                for t in range(NT):
                    ve.tensor_scalar(av[:, 4 * t:4 * t + 4], prow.to_broadcast([P, TOPK]), float(P * t + 1), None, ALU.add)
                link(ve.memset(sofar[:, 0, :], 0.0))

            def choose(t):
                j = f"lg{t}"
                wait_full(v, j)
                freed(j, ve.tensor_tensor(lgs[:, t, :], bank(j)[:, 0:E], rbb, ALU.add))
                wait_read(v, j)
                top, ids = topv[:, 8 * t:8 * t + 8], topi[:, 8 * t:8 * t + 8]
                link(ve.max(top, lgs[:, t, :]))
                link(ve.max_index(ids, top, lgs[:, t, :]))
                ve.tensor_scalar(ntop[:, t:t + 1], top[:, 0:1], -1.0, None, ALU.mult).then_inc(sem("top_ready"), 1)
                c = slice(4 * t, 4 * t + 4)
                link(ve.tensor_copy(ixf[:, c], ids[:, 0:TOPK]))
                link(ve.tensor_tensor(OH[:, c], iof[:, 0:E].unsqueeze(1).to_broadcast([P, TOPK, E]),
                                      ixf[:, c].unsqueeze(2).to_broadcast([P, TOPK, E]), ALU.is_equal))
                link(ve.tensor_reduce(Msk[:, t, :], OH[:, c].rearrange("p k e -> p e k"), AX.X, ALU.add))
                ve.tensor_tensor(sofar[:, t + 1, :], sofar[:, t, :], Msk[:, t, :], ALU.add).then_inc(sem("chosen"), 1)
                v.wait_ge(sem("chosen"), t + 1)

            residual(2, "wo", lambda t: numbers() if t == 0 else choose(t - 2) if t > 1 else None)
            choose(NT - 2)
            choose(NT - 1)
            v.wait_ge(sem("gate_exp"), 1)
            link(ve.reciprocal(gsum, gsum))
            link(ve.tensor_tensor(gate, gate, gsum.unsqueeze(2).to_broadcast([P, NT, TOPK]), ALU.mult))
            link(ve.tensor_tensor(tmp, OH, gate.rearrange("p t k -> p (t k)").unsqueeze(2).to_broadcast([P, 16, E]),
                                  ALU.mult))
            ve.tensor_reduce(Gt, tmp.rearrange("p (t k) e -> p t e k", t=NT), AX.X, ALU.add).then_inc(sem("gates_ready"), 1)
            wait_full(v, "pos")
            link(ve.tensor_copy(pos, bank("pos")[:, 0:128].rearrange("p (t e) -> p t e", t=NT)))
            freed("pos", ve.tensor_copy(cnt, bank("pos")[:, 128:160]))
            wait_read(v, "pos")
            ve.tensor_scalar(qq, pos, float(CAP), None, ALU.is_ge)
            ve.tensor_scalar(z, pos, float(CAP), None, ALU.is_ge)
            link(ve.tensor_scalar(nov, cnt, float(CAP), None, ALU.is_gt))
            for m in range(2, QMAX + 1):
                ve.scalar_tensor_tensor(out=qq, in0=pos, scalar=float(m * CAP), in1=qq, op0=ALU.is_ge, op1=ALU.add)
                link(ve.scalar_tensor_tensor(out=nov, in0=cnt, scalar=float(m * CAP), in1=nov, op0=ALU.is_gt, op1=ALU.add))
            ve.scalar_tensor_tensor(out=pos, in0=qq, scalar=-float(CAP), in1=pos, op0=ALU.mult, op1=ALU.add)
            link(ve.tensor_tensor_scan(ovi, ones[:, 0:E], nov, 0.0, ALU.mult, ALU.add))
            link(ve.tensor_tensor(ovs, ovi, nov, ALU.subtract))
            e4 = iof[:, 0:E].unsqueeze(1).to_broadcast([P, NT, E])
            link(ve.tensor_tensor(bl, qq, ovs.unsqueeze(1).to_broadcast([P, NT, E]), ALU.add))
            link(ve.tensor_tensor(bl, bl, e4, ALU.subtract))
            link(ve.scalar_tensor_tensor(out=bl, in0=bl, scalar=float(E - 1), in1=z, op0=ALU.add, op1=ALU.mult))
            link(ve.tensor_tensor(bl, bl, e4, ALU.add))

            def at_choice(o, a):
                o4 = OH.rearrange("p (t k) e -> p t k e", t=NT)
                t4 = tmp.rearrange("p (t k) e -> p t k e", t=NT)
                for t in range(NT):
                    ins = ve.tensor_tensor(t4[:, t], o4[:, t], a[:, t:t + 1, :].to_broadcast([P, TOPK, E]), ALU.mult)
                link(ins)
                link(ve.tensor_reduce(o, tmp, AX.X, ALU.add))

            at_choice(blk, bl)
            ve.tensor_tensor(Boh, iof[:, 0:NBX].unsqueeze(1).to_broadcast([P, 16, NBX]),
                             blk.unsqueeze(2).to_broadcast([P, 16, NBX]), ALU.is_equal).then_inc(sem("block_onehots"), 1)
            at_choice(slk, pos)
            v.wait_ge(sem("block_onehots"), 1)
            ve.tensor_tensor(Btg[:, :, 0:NBX], Boh, av.unsqueeze(2).to_broadcast([P, 16, NBX]), ALU.mult)
            ve.tensor_tensor(Aoh, iof[:, 0:CAP].unsqueeze(1).to_broadcast([P, 16, CAP]),
                             slk.unsqueeze(2).to_broadcast([P, 16, CAP]), ALU.is_equal).then_inc(sem("onehots"), 1)
            ve.tensor_scalar(nbt[:, 0:1], ovi[0:1, E - 1:E], float(E), None, ALU.add)
            ve.tensor_scalar(nbt[:, 1:2], ovi[0:1, E - 1:E], float(E - 1), None, ALU.add)
            link(ve.tensor_tensor(cmp_, ovi[0:1, :].unsqueeze(1).to_broadcast([1, NX, E]),
                                  iof[0:1, 0:NX].unsqueeze(2).to_broadcast([1, NX, E]), ALU.is_le))
            link(ve.tensor_reduce(etf[:, E:NBX], cmp_, AX.X, ALU.add))
            link(ve.tensor_copy(etf[:, 0:E], iof[0:1, 0:E]))
            link(ve.tensor_scalar(etab[:, :], etf, float(E - 1), None, ALU.min))
            link(ve.tensor_scalar(prow, prow, float(T + 1), None, ALU.add))
            wait_full(v, "tab")
            ve.tensor_scalar(gtab[:, :], bank("tab")[0:CAP, 0:NBX], -1.0, None, ALU.add).then_inc(sem("tables_ready"), 1)
            ve.tensor_scalar(tabf, bank("tab")[0:CAP, 0:NBX], -1.0, None, ALU.add)
            freed("tab", ve.tensor_copy(wtab[:, :], bank("tab")[0:CAP, NBX:2 * NBX]))
            wait_read(v, "tab")
            link(ve.tensor_scalar(empty, tabf, 0.0, None, ALU.is_lt))
            link(ve.scalar_tensor_tensor(out=tabf, in0=empty, scalar=prow[0:CAP], in1=tabf, op0=ALU.mult, op1=ALU.add))
            ve.tensor_copy(stab[:, :], tabf).then_inc(sem("wtab_ready"), 1)
            v.wait_ge(sem("h2_out"), 16 * NT)
            for t in range(NT):
                wait_read(v, f"gb{t}.0")
                wait_read(v, f"gb{t}.1")
                ve.scalar_tensor_tensor(out=hbuf[:, t, :], in0=hbuf[:, t, :], scalar=ALPHA, in1=gsc[:, t, :],
                                        op0=ALU.mult, op1=ALU.add).then_inc(sem("h_scaled"), 1)

            g4 = glu.rearrange("p (b f s) -> p b f s", b=2, f=4)
            l4 = lin.rearrange("p (b f s) -> p b f s", b=2, f=4)
            wait_read(v, "b1T")
            last = v.value_load(nbt[0:1, 1:2], min_val=E - 1, max_val=NBX - 2)
            base = step[0]

            def swiglu(b, e, steps):
                n = [0]

                def link(ins):
                    n[0] += 1
                    ins.then_inc(sem("dve_step"), 1)
                    v.wait_ge(sem("dve_step"), steps + n[0])

                def bias(o):
                    return b1T[:, bass.ds(e * 16 + o, 8)].rearrange("p (b f) -> p b f", b=2).unsqueeze(3)

                v.wait_ge(slot_free[7], b + 1)
                for i in range(2):
                    ins = ve.tensor_tensor(g4[:, i], ps[:, i, 0:4 * CAP].rearrange("p (f s) -> p f s", f=4),
                                           bias(0)[:, i].to_broadcast([P, 4, CAP]), ALU.add)
                link(ins)
                ve.tensor_scalar(glu, glu, LIMIT, None, ALU.min).then_inc(sem("glu_ready"), 1)
                for i in range(2):
                    ins = ve.tensor_tensor(l4[:, i], ps[:, 2 + i, 0:4 * CAP].rearrange("p (f s) -> p f s", f=4),
                                           bias(8)[:, i].to_broadcast([P, 4, CAP]), ALU.add)
                ins.then_inc(sem("h_read"), 1)
                v.wait_ge(sem("h_read"), b + 1)
                link(ve.tensor_scalar(lin, lin, LIMIT, -LIMIT, ALU.min, ALU.max))
                link(ve.scalar_tensor_tensor(out=lin, in0=lin, scalar=1.0, in1=glu, op0=ALU.add, op1=ALU.mult))
                v.wait_ge(sem("sig_ready"), b + 1)
                if not (isinstance(b, int) and b == 0):
                    v.wait_ge(slot_free[11], b)
                link(ve.tensor_tensor(act_, lin, sig, ALU.mult))
                link(ve.tensor_copy(act_hi[:, :], act_))
                ve.tensor_tensor(act_lo[:, :], act_, act_hi[:, :].bitcast(F32), ALU.subtract)\
                  .then_inc(sem("act_ready"), 1)
                return n[0]

            def w2_rest(b):
                for q in range(4):
                    v.wait_ge(sem("w2_high"), 4 * b + (q + 1))
                    ve.tensor_tensor(w2_lo[q][:, :], ring[:, 8 + q, :], w2_hi[q][:, :].bitcast(F32), ALU.subtract)\
                      .then_inc(sem("w2_split"), 1)

            per = swiglu(0, 0, base)
            w2_rest(0)
            e = v.value_load(etab[0:1, 1:2], min_val=0, max_val=E - 1)
            swiglu(1, e, base + per)
            with v.Fori(1, last) as b:
                w2_rest(b)
                e = v.value_load(etab[0:1, bass.ds(b + 1, 1)], min_val=0, max_val=E - 1)
                swiglu(b + 1, e, (base + per) + per * b)
            w2_rest(last)
            step[0], steps[0] = 0, "last_step"
            v.wait_ge(sem("ln_in"), 128)
            for t in range(NT + 1):
                if t < NT:
                    v.wait_ge(sem(f"sum_in{t}"), 16)
                    stats(3, t)
                if t:
                    normalise(3, t - 1)

        @block.tensor
        def _(pe):
            te = nc.tensor

            def job(name):
                b, use = JOBS[name]
                if use > 1:
                    pe.wait_ge(bank_free[b], use - 1)
                return bank(name)

            def full(name, ins):
                ins.then_inc(bank_full[JOBS[name][0]], 1)

            def mm(o, l, r, start, stop):
                return te.matmul(o, l, r, start=start, stop=stop)

            def tr(o, i, k=P):
                return te.transpose(o, i, ident[0:k, 0:k])

            def weights(w, i):
                if w == "wv" and i:
                    pe.wait_ge(sem(f"wv_in{i}"), 16)
                    return ring[:, wv_rest[i], :].rearrange("p (k n) -> p k n", n=D)
                s, use = SLOT_OF[w, i]
                pe.wait_ge(slot_full[s], 16 * use)
                return ring[:, s, :].rearrange("p (k n) -> p k n", n=D if w[0] == "w" else HW)

            pe.wait_ge(sem("consts"), 1)
            def transpose_h(n, t):
                pe.wait_ge(sem("normed"), NT * n + t + 1)
                for h in range(2):
                    nm = f"hT{n}.{t}.{h}"
                    o = job(nm)
                    for k in range(4):
                        ins = tr(o[:, k * P:(k + 1) * P], hbuf[:, t, (4 * h + k) * P:(4 * h + k + 1) * P])
                    full(nm, ins)

            pe.wait_ge(sem("mem_in"), 16)
            for m in range(2):
                for h in range(2):
                    nm = f"mT{m}.{h}"
                    o = job(nm)
                    for k in range(4):
                        ins = tr(o[:, k * P:(k + 1) * P], memx[:, m, (4 * h + k) * P:(4 * h + k + 1) * P])
                    full(nm, ins)
            for m in range(2):
                for h in range(2):
                    wait_read(pe, f"mT{m}.{h}")

            def keys(i):
                nm = f"K{i}"
                o = job(nm)
                for c in range(2):
                    for k in range(KD):
                        w = weights("wk", k // 2)
                        ins = mm(o[:, c * M:(c + 1) * M], w[:, k % 2, (2 * i + c) * P:(2 * i + c + 1) * P], memT[:, k, :],
                                 k == 0, k == KD - 1)
                full(nm, ins)

            keys(0)
            keys(1)
            pe.wait_ge(sem("params"), 16 * PARAMS)
            o = job("par")
            tr(o[:, 0:16], rows, 16)
            for i in range(3):
                tr(o[:, 16 + 16 * i:32 + 16 * i], lam_in[:, i * P:(i + 1) * P], 16)
            full("par", tr(o[:, 64:96], dn, 32))
            o = job("cT")
            for r in range(2):
                for i in range(2):
                    ins = tr(o[:, (2 * r + i) * P:(2 * r + i + 1) * P], craw[:, r, i].rearrange("p a m -> p (a m)"))
            full("cT", ins)

            keys(2)
            keys(3)
            for t in range(NT):
                transpose_h(0, t)
                m, h = t // 2, t % 2
                nm = f"V{m}.{h}"
                o = job(nm)
                for k in range(KD):
                    w = weights("wv", k // 2)
                    ins = mm(o, memT[:, k, m * P:(m + 1) * P], w[:, k % 2, 512 * h:512 * h + 512], k == 0, k == KD - 1)
                full(nm, ins)

            def channels(w0, c):
                nm = f"{w0}{c}"
                o = job(nm)
                for k in range(KD):
                    w = weights(w0, k // 4)
                    ins = mm(o, w[:, k % 4, c * P:(c + 1) * P], hT[:, k, :], k == 0, k == KD - 1)
                full(nm, ins)

            def tokens(w0, t):
                nm = f"{w0}{t}"
                o = job(nm)
                for k in range(KD):
                    w = weights(w0, k // 4)
                    ins = mm(o, hT[:, k, t * P:(t + 1) * P], w[:, k % 4, :], k == 0, k == KD - 1)
                full(nm, ins)

            for t in range(NT):
                for h in range(2):
                    wait_read(pe, f"hT0.{t}.{h}")
            for c in range(4):
                channels("u", c)
            pe.wait_ge(sem("q_ready"), 1)
            for r in range(2):
                for q in range(4):
                    nm = f"W{r}.{q}"
                    o = job(nm)
                    for i in range(4):
                        ins = tr(o[:, i * P:(i + 1) * P], Qb[:, r, 4 * q + i].rearrange("p j n -> p (j n)"))
                    full(nm, ins)
            pe.wait_ge(sem("s5_v"), 1)
            for q in range(8):
                nm = f"KK{q}"
                o = job(nm)
                for i in range(4):
                    g = 4 * q + i
                    b0, gi = PST * (g // GI), g % GI
                    rws = slice(b0, b0 + PST)
                    for c0, c1, w in ((0, N, None), (N, P, 1)):
                        for r in range(2):
                            rhs = cpar[rws, r, gi, :] if w is None else \
                                Vc[rws, r, gi, 0:L - 1, :].rearrange("p k n -> p (k n)")
                            ins = mm(o[0:N, i * P + c0:i * P + c1], bbar[rws, r, gi, :], rhs, r == 0, r == 1)
                full(nm, ins)
            for h in range(NH):
                channels("f", h)
            pe.wait_ge(sem("u_in"), 16 * L)
            for q in range(4):
                wait_read(pe, f"W0.{q}")
                wait_read(pe, f"W1.{q}")
            for r in range(2):
                for h in range(2):
                    nm = f"Z{r}.{h}"
                    o = job(nm)
                    for i in range(8):
                        for a in range(2):
                            gi = 8 * h + i
                            ins = mm(o[PST * a:PST * (a + 1), i * NC:(i + 1) * NC], Wst[:, r, gi, PST * a:PST * (a + 1)],
                                     ug[:, GI * a + gi, :], True, True)
                    full(nm, ins)
            for h in range(NH):
                channels("q", h)
            pe.wait_ge(sem("toe_ready"), 1)
            pe.wait_ge(sem("x_ready"), 1)
            for c in range(4):
                nm = f"Y{c}"
                o = job(nm)
                for i in range(8):
                    g = 8 * c + i
                    b0, gi = PST * (g // GI), g % GI
                    oo = o[:, i * NC:(i + 1) * NC]
                    mm(oo, Toe[:, g, :], ug[:, g, :], True, False)
                    for r in range(2):
                        ins = mm(oo, Vc[b0:b0 + PST, r, gi].rearrange("p k n -> p (k n)"), X[b0:b0 + PST, r, gi, 0:NC],
                                 False, r == 1)
                full(nm, ins)

            def between(j):
                c = int(j[1])
                if j[0] != "z":
                    return tokens(j[0], c)
                pe.wait_ge(sem("s5_in"), 16)
                o = job(j)
                w = weights("glu", 0)
                for k in range(4):
                    ins = mm(o, w[:, k, c * P:(c + 1) * P], ycm[:, k, :], k == 0, k == 3)
                full(j, ins)

            for n in range(len(LEVELS) + 1):
                if n == 0:
                    pe.wait_ge(sem("f_ready"), 4)
                    for h in range(4):
                        wait_read(pe, f"q{h}")
                    lt, rh = kh, qh
                else:
                    pe.wait_ge(sem("pair_ready"), n)
                    lt = rh = P0 if (n - 1) % 2 == 0 else P1
                for t in range(NT):
                    nm = f"s{n}.{t}"
                    o = job(nm)
                    for h in range(NH):
                        s = slice(h * T + t * P, h * T + (t + 1) * P)
                        ins = mm(o[:, h * P:(h + 1) * P], lt[:, s], rh[:, s], True, True)
                    full(nm, ins)
                for j in BETWEEN[n]:
                    between(j)
            pe.wait_ge(sem("kdec_ready"), 1)
            for t in range(NT):
                nm = f"kd{t}"
                o = job(nm)
                for h in range(NH):
                    s = slice(h * T + t * P, h * T + (t + 1) * P)
                    ins = tr(o[:, h * P:(h + 1) * P], P1[:, s])
                full(nm, ins)
            pe.wait_ge(sem("qe_ready"), 1)

            def transpose_oa(t):
                nm = f"oaT{t}"
                wait_read(pe, f"o{t}")
                o = job(nm)
                for c in range(4):
                    ins = tr(o[:, c * P:(c + 1) * P], oa[:, t, c * P:(c + 1) * P])
                full(nm, ins)

            for t in range(NT):
                wait_read(pe, f"s{len(LEVELS)}.{t}")
                wait_read(pe, f"kd{t}")
                if t:
                    wait_read(pe, f"st{t - 1}")
                nm = f"o{t}"
                o = job(nm)
                for h in range(NH):
                    oo = o[:, h * P:(h + 1) * P]
                    ins = mm(oo, Sc[:, t, h, :], vh[:, t, h * P:(h + 1) * P], True, t == 0)
                    if t:
                        ins = mm(oo, qe[:, h * T + t * P:h * T + (t + 1) * P], st[:, h, :], False, True)
                full(nm, ins)
                if t < NT - 1:
                    nm = f"st{t}"
                    o = job(nm)
                    for h in range(NH):
                        ins = mm(o[:, h * P:(h + 1) * P], kdT[:, t, h, :], vh[:, t, h * P:(h + 1) * P], True, True)
                    full(nm, ins)
                if t:
                    transpose_oa(t - 1)
            transpose_oa(NT - 1)

            def logits(t):
                nm = f"lg{t}"
                wait_read(pe, f"hT2.{t}.0")
                wait_read(pe, f"hT2.{t}.1")
                o = job(nm)
                for k in range(KD):
                    ins = mm(o[:, 0:E], hT[:, k, t * P:(t + 1) * P], rw[:, k, :], k == 0, k == KD - 1)
                full(nm, ins)

            def three_passes(o, l_hi, l_lo, r_hi, r_lo, start, stop):
                mm(o, l_hi, r_hi, start, False)
                mm(o, l_hi, r_lo, False, False)
                return mm(o, l_lo, r_hi, False, stop)

            def project(nm0, n, product, then=None):
                for t in range(NT):
                    for h in range(2):
                        nm = f"{nm0}{t}.{h}"
                        o = job(nm)
                        for k in range(KD):
                            ins = product(o, k, t, h)
                        full(nm, ins)
                    if t:
                        transpose_h(n, t - 1)
                    if then and t > 1:
                        then(t - 2)

            for t in range(NT):
                wait_read(pe, f"oaT{t}")
            pe.wait_ge(sem("glu_done"), 4)

            def mixed(o, k, t, h):
                w = weights("wout", k // 2)
                left = hT[:, k, :] if k < 4 else s5T[:, k - 4, :]
                return mm(o, left[:, t * P:(t + 1) * P], w[:, k % 2, 512 * h:512 * h + 512], k == 0, k == KD - 1)

            project("w", 1, mixed)
            for half in range(2):
                if half:
                    transpose_h(1, NT - 1)
                for t in range(2 * half, 2 * half + 2):
                    for h in range(2):
                        wait_read(pe, f"hT1.{t}.{h}")
                for c2 in range(4):
                    nm = f"aq{half}.{c2}"
                    o = job(nm)
                    for i in range(2):
                        c = 2 * c2 + i
                        for k in range(KD):
                            pe.wait_ge(sem("wq_split"), k // 2 + 1)
                            a = slice((k % 2) * D + c * P, (k % 2) * D + (c + 1) * P)
                            b = slice(k * T + half * M, k * T + (half + 1) * M)
                            ins = three_passes(o[:, i * M:(i + 1) * M], wq_hi[k // 2][:, a], wq_lo[k // 2][:, a],
                                               hT_hi[:, b], hT_lo[:, b], k == 0, k == KD - 1)
                    full(nm, ins)
            for half in range(2):
                for c in range(4):
                    wait_read(pe, f"aq{half}.{c}")

            for t in range(NT + 1):
                if t < NT:
                    for h in range(2):
                        nm = f"sc{t}.{h}"
                        o = job(nm)
                        for i in range(2):
                            for kk in range(2):
                                c = 2 * (2 * h + i) + kk
                                ins = mm(o[:, i * M:(i + 1) * M], qT[:, c, t * P:(t + 1) * P], kT[:, c, :],
                                         kk == 0, kk == 1)
                        full(nm, ins)
                if t:
                    pe.wait_ge(sem("probs_ready"), 2 * t)
                    for m in range(2):
                        nm = f"PT{t - 1}.{m}"
                        o = job(nm)
                        for hh in range(NH):
                            ins = tr(o[:, hh * P:(hh + 1) * P], Pb[:, (t - 1) % 2, hh, m * P:(m + 1) * P])
                        full(nm, ins)
            for t in range(NT):
                for m in range(2):
                    wait_read(pe, f"PT{t}.{m}")
            for c in range(8):
                nm = f"ao{c}"
                o = job(nm)
                for m in range(2):
                    ins = mm(o, vm[:, m, c * P:(c + 1) * P], PT[:, m, c // 2, :], m == 0, m == 1)
                full(nm, ins)
            pe.wait_ge(sem("late_in"), 32)
            o = job("b1T")
            for q in range(4):
                ins = tr(o[:, q * P:(q + 1) * P], b1raw[:, q, :])
            full("b1T", ins)
            for c in range(8):
                wait_read(pe, f"ao{c}")

            def attended(o, k, t, h):
                pe.wait_ge(sem("wo_split"), k // 2 + 1)
                a = slice(k * T + t * P, k * T + (t + 1) * P)
                b = slice((k % 2) * D + 512 * h, (k % 2) * D + 512 * h + 512)
                return three_passes(o, hT_hi[:, a], hT_lo[:, a], wo_hi[k // 2][:, b], wo_lo[k // 2][:, b],
                                    k == 0, k == KD - 1)

            project("wo", 2, attended, logits)
            transpose_h(2, NT - 1)
            logits(NT - 2)
            logits(NT - 1)
            o = job("pos")
            for t in range(NT):
                pe.wait_ge(sem("chosen"), t + 1)
                if t:
                    mm(o[:, t * E:(t + 1) * E], ones[:, :], sofar[:, t, :], True, False)
                mm(o[:, t * E:(t + 1) * E], tri[:, :], Msk[:, t, :], t == 0, True)
            full("pos", mm(o[:, NT * E:NT * E + E], ones[:, :], sofar[:, NT, :], True, True))
            pe.wait_ge(sem("gates_ready"), 1)
            o = job("GT")
            for t in range(NT):
                ins = mm(o[0:E, t * P:(t + 1) * P], Gt[:, t, :], ident[:, :], True, True)
            full("GT", ins)
            pe.wait_ge(sem("onehots"), 1)
            pe.wait_ge(sem("gate_onehots"), 1)
            o = job("tab")
            for i in range(16):
                ins = mm(o[0:CAP, 0:2 * NBX], Aoh[:, i, :], Btg[:, i, :], i == 0, i == 15)
            full("tab", ins)
            wait_read(pe, "GT")
            pe.wait_ge(sem("b2_in"), 16)
            for nm in GATED_BIASES:
                t, h = int(nm[2]), int(nm[4])
                full(nm, mm(job(nm), GTs[:, t * P:(t + 1) * P], b2sb[:, 512 * h:512 * h + 512], True, True))
            pe.wait_ge(sem("tables_ready"), 1)
            last = pe.value_load(nbt[0:1, 1:2], min_val=E - 1, max_val=NBX - 2)
            for b_ in range(8):
                pe.wait_ge(bank_free[b_], sum(bb == b_ for bb, _ in JOBS.values()))

            def rows_in(b):
                pe.wait_ge(sem("x_gathered"), 16 * b + 16)
                for k in range(KD):
                    ins = tr(ps[:, 6 + k // 4, (k % 4) * CAP:(k % 4 + 1) * CAP], Xg[:, k * P:(k + 1) * P], CAP)
                ins.then_inc(sem("xt_full"), 1)

            def first(b):
                pe.wait_ge(sem("xt_copied"), b + 1)
                if not (isinstance(b, int) and b == 0):
                    pe.wait_ge(sem("h_read"), b)
                for k in range(KD):
                    pe.wait_ge(slot_full[k], 16 * b + 16 * (LOADS[k] + 1))
                    for f in range(16):
                        ins = te.matmul(ps[:, f // 4, (f % 4) * CAP:(f % 4 + 1) * CAP],
                                        ring[:, k, f * P:(f + 1) * P], xT[:, k, :],
                                        start=(k == 0 and f % 4 == 0), stop=(k == KD - 1), skip_group_check=True)
                    ins.then_inc(slot_free[k], 1)

            def second(b):
                pe.wait_ge(sem("act_ready"), b + 1)
                if not (isinstance(b, int) and b == 0):
                    pe.wait_ge(sem("y_copied"), b)
                for k in range(KD):
                    q = k // 2
                    if k % 2 == 0:
                        pe.wait_ge(sem("w2_split"), 4 * b + (q + 1))
                    for h in range(2):
                        c = slice((k % 2) * D + 512 * h, (k % 2) * D + 512 * h + 512)
                        a = slice(k * CAP, (k + 1) * CAP)
                        y = ps[0:CAP, 4 + h, :]
                        te.matmul(y, act_hi[:, a], w2_hi[q][:, c], start=(k == 0), stop=False)
                        te.matmul(y, act_hi[:, a], w2_lo[q][:, c], start=False, stop=False)
                        ins = te.matmul(y, act_lo[:, a], w2_hi[q][:, c], start=False, stop=(k == KD - 1))
                    if k % 2 == 1:
                        ins.then_inc(slot_free[8 + q], 1)

            rows_in(0)
            first(0)
            rows_in(1)
            first(1)
            rows_in(2)
            second(0)
            with pe.Fori(1, last) as b:
                first(b + 1)
                rows_in(b + 2)
                second(b)
            second(last)


def kernel(**inputs):
    import concourse.bacc as _bacc
    from concourse.bass_utils import run_bass_kernel_spmd as _run

    nc = _bacc.Bacc("TRN2", target_bir_lowering=False, num_devices=1)
    arrays, aps = {}, {}
    for name, value in inputs.items():
        a = np.ascontiguousarray(value)
        arrays[f"in_{name}"] = a
        aps[name] = nc.dram_tensor(f"in_{name}", a.shape, mybir.dt.from_np(a.dtype), kind="ExternalInput").ap()
    out = nc.dram_tensor("out_rows", (1, T, D), F32, kind="ExternalOutput").ap()
    trunk_layer(nc, aps, out)
    r = _run(nc, [arrays], core_ids=[0])
    return r.results[0]["out_rows"]
```
